# Optimizing a Trainium2 kernel written in Bass

```python
import jax, jax.numpy as jnp
from jax import lax
import numpy as np

D_MODEL = 1024
BATCH = 1
SEQ = 1024
DEPTH = 2

N_A = DEPTH // 2
N_B = DEPTH - N_A
D_RNN = D_MODEL
LRU_BLOCK_W = 256
LRU_BLOCKS = D_RNN // LRU_BLOCK_W
CONV_W = 4
LRU_C = 8.0
N_HEADS = 16
HEAD_DIM = D_MODEL // N_HEADS
Q_BLOCK = 128
D_FF = ((8 * D_MODEL + 3 * 256 - 1) // (3 * 256)) * 256
EPS = 1e-6

kernel_name = "hawk_fox_yoco_hybrid"

def rmsnorm(x, g):
    xf = x.astype(jnp.float32)
    y = xf * lax.rsqrt(jnp.mean(xf * xf, axis=-1, keepdims=True) + EPS)
    return (y * g.astype(jnp.float32)).astype(x.dtype)

def swiglu(x, w_in, w_out):
    gate, up = jnp.split(x @ w_in, 2, axis=-1)
    return (jax.nn.silu(gate) * up) @ w_out

def causal_depthwise_conv(x, w, b):
    S = x.shape[1]
    xp = jnp.pad(x, ((0, 0), (CONV_W - 1, 0), (0, 0)))
    out = b
    for tap in range(CONV_W):
        out = out + xp[:, tap:tap + S] * w[tap]
    return out

def _lin_rec_combine(left, right):
    a1, b1 = left
    a2, b2 = right
    return a1 * a2, a2 * b1 + b2

def rg_lru(x, w_gates, b_gates, lru_param):
    B, S, _ = x.shape
    xb = x.reshape(B, S, LRU_BLOCKS, LRU_BLOCK_W)
    g = (jnp.einsum('bsnw,nwv->bsnv', xb, w_gates) + b_gates).astype(jnp.float32)
    gate_i = jax.nn.sigmoid(g[..., :LRU_BLOCK_W])
    gate_r = jax.nn.sigmoid(g[..., LRU_BLOCK_W:])
    log_a = -LRU_C * gate_r * jax.nn.softplus(-lru_param.astype(jnp.float32).reshape(LRU_BLOCKS, LRU_BLOCK_W))
    a = jnp.exp(log_a)
    mult = jnp.sqrt(-jnp.expm1(2.0 * log_a))
    u = xb.astype(jnp.float32) * gate_i * mult
    a = a.reshape(B, S, D_RNN)
    u = u.reshape(B, S, D_RNN)
    _, h = lax.associative_scan(_lin_rec_combine, (a, u), axis=1)
    return h.astype(x.dtype)

def recurrent_mixer(xn, w_in, conv_w, conv_b, w_gates, b_gates, lru_param, w_out):
    proj = xn @ w_in
    gate_branch, rec = proj[..., :D_RNN], proj[..., D_RNN:]
    rec = causal_depthwise_conv(rec, conv_w, conv_b)
    h = rg_lru(rec, w_gates, b_gates, lru_param)
    return (jax.nn.gelu(gate_branch) * h) @ w_out

def shared_kv_forget(xs, norm_kv, w_kvf, b_forget):
    B, S, _ = xs.shape
    p = rmsnorm(xs, norm_kv) @ w_kvf
    k = p[..., :D_MODEL].reshape(B, S, N_HEADS, HEAD_DIM).transpose(0, 2, 1, 3)
    v = p[..., D_MODEL:2 * D_MODEL].reshape(B, S, N_HEADS, HEAD_DIM).transpose(0, 2, 1, 3)
    f_logit = (p[..., 2 * D_MODEL:] + b_forget).astype(jnp.float32)
    c = jnp.cumsum(jax.nn.log_sigmoid(f_logit), axis=1).transpose(0, 2, 1)
    return k, v, c

def forgetting_attention(xn, w_q, w_o, k, v, c):
    B, S, _ = xn.shape
    q = (xn @ w_q).reshape(B, S, N_HEADS, HEAD_DIM).transpose(0, 2, 1, 3)
    scale = HEAD_DIM ** -0.5
    outs = []
    for blk in range(S // Q_BLOCK):
        q0 = blk * Q_BLOCK
        q1 = q0 + Q_BLOCK
        s = jnp.einsum('bhqd,bhkd->bhqk', q[:, :, q0:q1], k[:, :, :q1],
                       preferred_element_type=jnp.float32) * scale
        s = s + c[:, :, q0:q1, None] - c[:, :, None, :q1]
        mask = (q0 + jnp.arange(Q_BLOCK))[:, None] >= jnp.arange(q1)[None, :]
        s = jnp.where(mask, s, -jnp.inf)
        p = jax.nn.softmax(s, axis=-1)
        outs.append(jnp.einsum('bhqk,bhkd->bhqd', p.astype(v.dtype), v[:, :, :q1]))
    o = jnp.concatenate(outs, axis=2).transpose(0, 2, 1, 3).reshape(B, S, D_MODEL)
    return o @ w_o

def setup_inputs(seed: int = 0) -> dict:
    key = jax.random.key(seed)
    ks = jax.random.split(key, 20)
    f32 = jnp.float32
    nrm = lambda k, shape, fan_in: jax.random.normal(k, shape, f32) * (fan_in ** -0.5)
    gain = lambda k, shape: 1.0 + 0.01 * jax.random.normal(k, shape, f32)

    x = jax.random.normal(ks[0], (BATCH, SEQ, D_MODEL), f32)
    norm_mix = gain(ks[1], (DEPTH, D_MODEL))
    norm_ffn = gain(ks[2], (DEPTH, D_MODEL))
    w_ffn_in = nrm(ks[3], (DEPTH, D_MODEL, 2 * D_FF), D_MODEL)
    w_ffn_out = nrm(ks[4], (DEPTH, D_FF, D_MODEL), D_FF)

    w_rec_in = nrm(ks[5], (N_A, D_MODEL, 2 * D_RNN), D_MODEL)
    conv_w = nrm(ks[6], (N_A, CONV_W, D_RNN), CONV_W)
    conv_b = 0.01 * jax.random.normal(ks[7], (N_A, D_RNN), f32)
    w_lru_gates = nrm(ks[8], (N_A, LRU_BLOCKS, LRU_BLOCK_W, 2 * LRU_BLOCK_W), LRU_BLOCK_W)
    b_lru_gates = 0.01 * jax.random.normal(ks[9], (N_A, LRU_BLOCKS, 2 * LRU_BLOCK_W), f32)
    u = jax.random.uniform(ks[10], (N_A, D_RNN), f32, 0.9, 0.999)
    s = u ** (1.0 / LRU_C)
    lru_param = jnp.log(s) - jnp.log1p(-s)
    w_rec_out = nrm(ks[11], (N_A, D_RNN, D_MODEL), D_RNN)

    norm_kv = gain(ks[12], (D_MODEL,))
    w_kvf = nrm(ks[13], (D_MODEL, 2 * D_MODEL + N_HEADS), D_MODEL)
    b_forget = jnp.linspace(1.0, 5.0, N_HEADS, dtype=f32) + 0.1 * jax.random.normal(ks[14], (N_HEADS,), f32)
    w_q = nrm(ks[15], (N_B, D_MODEL, D_MODEL), D_MODEL)
    w_o = nrm(ks[16], (N_B, D_MODEL, D_MODEL), D_MODEL)
    norm_final = gain(ks[17], (D_MODEL,))
    return {"x": x, "norm_mix": norm_mix, "norm_ffn": norm_ffn, "w_ffn_in": w_ffn_in,
            "w_ffn_out": w_ffn_out, "w_rec_in": w_rec_in, "conv_w": conv_w, "conv_b": conv_b,
            "w_lru_gates": w_lru_gates, "b_lru_gates": b_lru_gates, "lru_param": lru_param,
            "w_rec_out": w_rec_out, "norm_kv": norm_kv, "w_kvf": w_kvf, "b_forget": b_forget,
            "w_q": w_q, "w_o": w_o, "norm_final": norm_final}

def reference(x, norm_mix, norm_ffn, w_ffn_in, w_ffn_out, w_rec_in, conv_w, conv_b,
              w_lru_gates, b_lru_gates, lru_param, w_rec_out, norm_kv, w_kvf, b_forget,
              w_q, w_o, norm_final):
    h = x
    k = v = c = None
    for layer in range(DEPTH):
        xn = rmsnorm(h, norm_mix[layer])
        if layer < N_A:
            i = layer
            mix = recurrent_mixer(xn, w_rec_in[i], conv_w[i], conv_b[i], w_lru_gates[i],
                                  b_lru_gates[i], lru_param[i], w_rec_out[i])
        else:
            if layer == N_A:
                k, v, c = shared_kv_forget(h, norm_kv, w_kvf, b_forget)
            j = layer - N_A
            mix = forgetting_attention(xn, w_q[j], w_o[j], k, v, c)
        h = h + mix
        h = h + swiglu(rmsnorm(h, norm_ffn[layer]), w_ffn_in[layer], w_ffn_out[layer])
    return rmsnorm(h, norm_final)


_drawn_inputs = setup_inputs


def setup_inputs(seed=0):
    import zlib

    import numpy as np

    out = dict(_drawn_inputs(seed))
    spreads = {}
    factors = {'norm_mix': 8.0,
     'norm_ffn': 17.058,
     'b_lru_gates': 8.0,
     'norm_kv': 101.22,
     'norm_final': 189.783,
     'conv_b': 3.266}
    for name, (base, spread) in spreads.items():
        noise = np.random.default_rng([zlib.crc32(name.encode()), seed]).standard_normal(out[name].shape)
        drawn = base * np.exp(spread * noise) if base else spread * noise
        out[name] = __import__('jax').numpy.asarray(drawn.astype(out[name].dtype))
    for name, factor in factors.items():
        out[name] = (out[name] * factor).astype(out[name].dtype)
    return out
```

```python
import concourse.bass as bass
from concourse import mybir
from contextlib import ExitStack

F32 = mybir.dt.float32
F32R = mybir.dt.float32r
BF16 = mybir.dt.bfloat16
ALU = mybir.AluOpType
ACT = mybir.ActivationFunctionType
AX = mybir.AxisListType

P = 128
BANK = 512
EPS = 1e-6
LRU_C = 8.0
NEG = -1e30
TINY = 1e-34


class Turns:

    def __init__(self, slots):
        self.total = [0] * slots
        self.segments = {}

    def plan(self, name, order, iters=1, first=0):
        self.segments[name] = (list(self.total), order, first)
        for s in order:
            self.total[s] += iters
        return self

    def use(self, name, j, i=0):
        base, order, first = self.segments[name]
        s = order[j]
        per = order.count(s)
        return s, i * per + (base[s] - first * per + order[:j].count(s) + 1)


def hawk_fox_yoco(nc, x, norm_mix, norm_ffn, w_ffn_in, w_ffn_out, w_rec_in, conv_w, conv_b,
                  w_lru_gates, b_lru_gates, lru_param, w_rec_out, norm_kv, w_kvf, b_forget,
                  w_q, w_o, norm_final, out):
    S, D = x.shape[1], x.shape[2]
    KT = D // P
    FF = w_ffn_out.shape[1]
    GROUPS = FF // (2 * P)
    BLOCKS, LW = w_lru_gates.shape[1], w_lru_gates.shape[2]
    TAPS = conv_w.shape[1]
    HEADS = w_kvf.shape[1] - 2 * D
    HD = D // HEADS
    PAIRS = HEADS * HD // P
    QB = S // P
    RANGES = QB // 2
    UNITS = 2 * RANGES
    assert KT == 8 and S == 2 * BANK and LW == 2 * P and HD == 64 and FF % (2 * P) == 0

    V_MIX, V_FFN, V_KV, V_FINAL = 0, 2 * KT, 4 * KT, 5 * KT
    V_CONVB, V_LRU, V_CONVW, V_GATEB = 6 * KT, 7 * KT, 8 * KT, (8 + TAPS) * KT
    V_ALL = V_GATEB + BLOCKS * 2 * LW // P

    GATE_SLOT = 3
    pieces = Turns(4)
    pieces.plan("recA", [0, 1, 2, 0]).plan("recL", [1, 2, 0, 1, 2, 0], BLOCKS - 1, 1).plan("recE", [1, 2])
    pieces.plan("gates", [3], BLOCKS)
    for f in range(2):
        pieces.plan(f"ffn{f}A", [0, 1, 2, 0]).plan(f"ffn{f}L", [1, 2, 0, 1, 2, 0], GROUPS - 1, 1)
        pieces.plan(f"ffn{f}E", [1, 2])
        if f == 0:
            pieces.plan("forget", [3])
            pieces.plan("attA", [0, 1, 0]).plan("attL", [1, 0, 1, 0], PAIRS - 1, 1).plan("attE", [1])
    tiles = Turns(4)
    OUT_STAT = [0, 1, 2, 0, 1, 2, 0, 1, 3]
    tiles.plan("vec", [3]).plan("start", OUT_STAT)
    tiles.plan("recA", [0, 1, 2, 3] * 2).plan("recL", [0, 1, 2, 3] * 4, BLOCKS - 1, 1).plan("recE", OUT_STAT)
    for f in range(2):
        tiles.plan(f"ffn{f}A", [0, 1, 2, 3]).plan(f"ffn{f}L", [0, 1, 2, 3] * 3, GROUPS - 1, 1)
        tiles.plan(f"ffn{f}E", OUT_STAT)
        if f == 0:
            tiles.plan("forget", [3])
            tiles.plan("attA", [0, 1, 2, 3] + [0, 1] * QB)
            tiles.plan("attL", [0, 1, 2, 3] * 3 + [0, 1] * QB, PAIRS - 1, 1).plan("attE", OUT_STAT)
    tiles.plan("final", [0, 1, 2, 3] * 2)

    IN_REC, IN_FFN, IN_ATT = 0, [4 * BLOCKS, 4 * BLOCKS + 4 * GROUPS + 3 * PAIRS], 4 * BLOCKS + 4 * GROUPS
    OUT_REC, OUT_FFN, OUT_ATT = 0, [8 * BLOCKS, 8 * (BLOCKS + GROUPS + PAIRS)], 8 * (BLOCKS + GROUPS)
    STAT = {"start": 0, "recE": 1, "ffn0E": 2, "attE": 3, "ffn1E": 4}
    LRU_STEPS, FORGET_STEPS = 15, 16
    T_PAIR = RANGES * (RANGES + 1)

    with ExitStack() as life:
        def sb(name, shape, dt, at=life):
            return at.enter_context(nc.sbuf_tensor(name, shape, dt))

        def sem(name):
            return life.enter_context(nc.semaphore(name))

        resid = sb("resid", [P, KT, S], F32)
        xh = sb("xh", [P, KT, S], F32R)
        xl = sb("xl", [P, KT, S], F32R)
        rstd = sb("rstd", [P, S], F32)
        raw = [sb(f"raw{s}", [P, 1024], F32) for s in range(2)]
        wh = [sb(f"wh{s}", [P, 1024], F32R) for s in range(2)]
        wl = [sb(f"wl{s}", [P, 1024], F32R) for s in range(2)]
        ident = sb("ident", [P, P], F32)
        ones = sb("ones", [P, P], F32)
        identb = sb("identb", [P, P], BF16)
        maskb = sb("maskb", [P, P], BF16)
        vec = sb("vec", [P, V_ALL], F32)
        lru = sb("lru", [P, 6, KT], F32)
        bforget = sb("bforget", [HEADS, 1], F32)
        negsel = sb("negsel", [P, HEADS], F32)

        with ExitStack() as att:
            kh = sb("kh", [P, 2, S], F32R, att)
            kl = sb("kl", [P, 2, S], F32R, att)
            qs = sb("qs", [P, 2, S], F32R, att)
            vs = sb("vs", [P, 2, QB, 2, HD], F32R, att)
            probs = [sb(f"probs{b}", [P, 2, S], F32, att) for b in range(2)]
            pth = [sb(f"pth{b}", [P, BANK], F32R, att) for b in range(2)]
            ptl = [sb(f"ptl{b}", [P, BANK], F32R, att) for b in range(2)]
            oh = sb("oh", [P, S], F32R, att)
            ol = sb("ol", [P, S], F32R, att)
            kv_tmp = sb("kv_tmp", [P, S], F32, att)
            qo_tmp = sb("qo_tmp", [P, S], F32, att)
            c2 = sb("c2", [P, S], F32R, att)
            sel = sb("sel", [P, 2, P], F32R, att)
            o_low = [sb(f"o_low{b}", [HD, 2 * P], F32, att) for b in range(2)]
            nmax = sb("nmax", [P, 2 * QB], F32, att)
            rsum = sb("rsum", [P, 2 * QB], F32, att)
            rinv = sb("rinv", [P, 2 * QB], F32, att)

        raw += [sb(f"raw{s}", [P, 1024], F32) for s in (2, 3)]
        wh += [sb(f"wh{s}", [P, 1024], F32R) for s in (2, 3)]
        wl += [sb(f"wl{s}", [P, 1024], F32R) for s in (2, 3)]
        tmp = [sb(f"tmp{b}", [P, S], F32) for b in range(4)]
        with ExitStack() as load:
            vrow = sb("vrow", [V_ALL, P], F32, load)
            xin = sb("xin", [P, QB, D], F32, load)
        with ExitStack() as rec:
            gelu = sb("gelu", [P, 2, S], F32, rec)
            ch = sb("ch", [P, 2, S], F32R, rec)
            cl = sb("cl", [P, 2, S], F32R, rec)
            yh = sb("yh", [P, 2, S], F32R, rec)
            yl = sb("yl", [P, 2, S], F32R, rec)
        hh = sb("hh", [P, 2, S], F32R)
        hl = sb("hl", [P, 2, S], F32R)

        ps = [life.enter_context(nc.psum_tensor(f"ps{s}", [P, S], F32)) for s in range(4)]
        t_ps = [ps[2][:, b * BANK:(b + 1) * BANK] for b in range(2)]
        o_ps = [ps[3][:, b * BANK:b * BANK + 2 * P] for b in range(2)]

        vec_loaded = sem("vec_loaded")
        bforget_loaded = sem("bforget_loaded")
        x_loaded = sem("x_loaded")
        loaded = [sem(f"loaded{s}") for s in range(4)]
        hi_ready = [sem(f"hi_ready{s}") for s in range(4)]
        lo_ready = [sem(f"lo_ready{s}") for s in range(4)]
        drained = [sem(f"drained{s}") for s in range(4)]
        const_ready = sem("const_ready")
        const_zero = sem("const_zero")
        vec_filled = sem("vec_filled")
        vec_ready = sem("vec_ready")
        lru_step = sem("lru_step")
        xt_filled = sem("xt_filled")
        in_filled = sem("in_filled")
        gates_filled = sem("gates_filled")
        out_filled = sem("out_filled")
        stat_filled = sem("stat_filled")
        xh_ready = sem("xh_ready")
        sq_ready = sem("sq_ready")
        sq_used = sem("sq_used")
        xl_ready = sem("xl_ready")
        root_ready = sem("root_ready")
        rstd_ready = sem("rstd_ready")
        conv_step = sem("conv_step")
        conv_ready = sem("conv_ready")
        ch_ready = sem("ch_ready")
        cl_ready = sem("cl_ready")
        gelu_ready = sem("gelu_ready")
        sig_ready = sem("sig_ready")
        lru_act = sem("lru_act")
        lru_dve = sem("lru_dve")
        y_ready = sem("y_ready")
        yh_ready = sem("yh_ready")
        yl_ready = sem("yl_ready")
        silu_ready = sem("silu_ready")
        h_ready = sem("h_ready")
        hh_ready = sem("hh_ready")
        hl_ready = sem("hl_ready")
        forget_filled = sem("forget_filled")
        forget_dve = sem("forget_dve")
        forget_act = sem("forget_act")
        c_ready = sem("c_ready")
        vt_filled = sem("vt_filled")
        s_filled = sem("s_filled")
        t_filled = sem("t_filled")
        o_filled = sem("o_filled")
        kh_ready = sem("kh_ready")
        kl_ready = sem("kl_ready")
        kdup_ready = sem("kdup_ready")
        qh_ready = sem("qh_ready")
        ql_ready = sem("ql_ready")
        vh_ready = sem("vh_ready")
        sel_ready = sem("sel_ready")
        nmax_ready = sem("nmax_ready")
        rinv_ready = sem("rinv_ready")
        p_ready = sem("p_ready")
        pth_ready = sem("pth_ready")
        ptl_ready = sem("ptl_ready")
        pt_used = sem("pt_used")
        o_low_ready = sem("o_low_ready")
        o_added = sem("o_added")
        oh_ready = sem("oh_ready")
        ol_ready = sem("ol_ready")
        y_final = sem("y_final")
        rows_filled = sem("rows_filled")
        rows_ready = sem("rows_ready")
        rows_stored = [sem(f"rows_stored{b}") for b in range(4)]

        def cols(w, c0):
            return w[:, bass.ds(c0, P)].rearrange("(k p) n -> p k n", p=P)

        def rows(w, r0, c0, n):
            return w[bass.ds(r0, 2 * P), c0:c0 + n].rearrange("(k p) n -> p k n", p=P)

        def rec_piece(j, first):
            if j < 2:
                return cols(w_rec_in[0], first + (D + j * P))
            if j < 4:
                return cols(w_rec_in[0], first + (j - 2) * P)
            return rows(w_rec_out[0], first, (j - 4) * BANK, BANK)

        def ffn_piece(f, kind, g):
            what, j = kind[0], int(kind[1])
            if what == "O":
                return rows(w_ffn_out[f], g * (2 * P), j * BANK, BANK)
            return cols(w_ffn_in[f], g * (2 * P) + (j * P + (FF if what == "U" else 0)))

        def att_piece(kind, i):
            if kind == "O":
                return w_o[0][bass.ds(i * P, P), :]
            return cols(w_q[0] if kind == "Q" else w_kvf, i * P + (D if kind == "V" else 0))

        def sq(seg, k):
            if seg == "attE":
                return (kv_tmp, qo_tmp)[k % 2][:, :]
            return tmp[k % 2][:, :]

        GAIN = {"rec": V_MIX, "ffn0": V_FFN, "ffn1": V_FFN + KT, "K": V_KV, "V": V_KV, "Q": V_MIX + KT}

        def rec_free(j, b):
            return [(in_filled, b * 4), (gates_filled, b * 4 - 3), (gates_filled, b * 4 - 3),
                    (in_filled, b * 4 + 1), (in_filled, b * 4 + 2), (in_filled, b * 4 + 3)][j]

        def ffn_free(f, j, g):
            i0, o0 = IN_FFN[f], OUT_FFN[f]
            return [(in_filled, g * 4 + (i0 - 2)), (in_filled, g * 4 + (i0 - 1)), (in_filled, g * 4 + i0),
                    (in_filled, g * 4 + (i0 + 1)), (out_filled, g * 8 + (o0 - 4)), (out_filled, g * 8 + o0)][j]

        def att_free(j, i):
            return [(in_filled, i * 3 + IN_ATT), (s_filled, i * 2 * QB - (2 * QB - 1)),
                    (in_filled, i * 3 + (IN_ATT + 1)), (in_filled, i * 3 + (IN_ATT + 2))][j]

        FFN_START = [
            [(out_filled, 8 * (BLOCKS - 1)), (out_filled, 8 * BLOCKS - 4), (out_filled, 8 * BLOCKS),
             (in_filled, IN_FFN[0] + 1)],
            [(out_filled, OUT_FFN[1] - 8), (out_filled, OUT_FFN[1]), (out_filled, OUT_FFN[1]),
             (in_filled, IN_FFN[1] + 1)]]
        FFN_END = [[(in_filled, IN_FFN[f] + 4 * GROUPS - 2), (in_filled, IN_FFN[f] + 4 * GROUPS - 1)] for f in range(2)]
        REC_END = [(in_filled, 4 * BLOCKS), (out_filled, 8 * (BLOCKS - 2) + 4)]
        ATT_START = [(in_filled, IN_ATT), (out_filled, OUT_ATT - 4), (in_filled, IN_ATT + 1)]
        ATT_END = [(in_filled, IN_ATT + 3 * PAIRS)]

        def tiles_before(u):
            return sum(v % RANGES + 1 for v in range(u))

        def pt_used_at(i, t):
            u = max(v for v in range(UNITS) if tiles_before(v) <= t)
            if t - tiles_before(u) == u % RANGES:
                return o_filled, i * UNITS + (u + 1)
            return pt_used, i * (T_PAIR - UNITS) + (t + 1 - u)

        block = life.enter_context(nc.Block())

        @block.sync
        def _(sp):
            def load(use, src, k=KT, wait=True):
                slot, n = use
                if wait:
                    sp.wait_ge(lo_ready[slot], n - 1)
                dst = raw[slot][:, :] if k == 1 else raw[slot][:, :].rearrange("p (k n) -> p k n", k=k)
                sp.dma_start(dst, src).then_inc(loaded[slot], 16)

            for first, v in ((V_MIX, norm_mix.rearrange("l (k p) -> (l k) p", p=P)),
                             (V_FFN, norm_ffn.rearrange("l (k p) -> (l k) p", p=P)),
                             (V_KV, norm_kv.rearrange("(k p) -> k p", p=P)),
                             (V_FINAL, norm_final.rearrange("(k p) -> k p", p=P)),
                             (V_CONVB, conv_b[0].rearrange("(k p) -> k p", p=P)),
                             (V_LRU, lru_param[0].rearrange("(k p) -> k p", p=P)),
                             (V_CONVW, conv_w[0].rearrange("t (k p) -> (t k) p", p=P)),
                             (V_GATEB, b_lru_gates[0].rearrange("b (m p) -> (b m) p", p=P))):
                sp.dma_start(vrow[first:first + v.shape[0], :], v).then_inc(vec_loaded, 16)
            for b in range(QB):
                sp.dma_start(xin[:, b, :], x[0, b * P:(b + 1) * P, :]).then_inc(x_loaded, 16)
            sp.dma_start(bforget[:, :], b_forget.rearrange("(h a) -> h a", a=1)).then_inc(bforget_loaded, 16)

            for j in range(4):
                load(pieces.use("recA", j), rec_piece(j, 0))
            load(pieces.use("gates", 0, 0), w_lru_gates[0, 0].rearrange("(k p) n -> p k n", p=P), 2)
            with sp.Fori(1, BLOCKS) as b:
                first = b * LW
                slot, n = pieces.use("recL", 2, b)
                for j in range(4):
                    if j == 1:
                        sp.wait_ge(lo_ready[slot], n - 1)
                    load(pieces.use("recL", j, b), rec_piece(j, first), wait=(j != 2))
                for j in range(4, 6):
                    load(pieces.use("recL", j, b), rec_piece(j, first - LW), 2)
                load(pieces.use("gates", 0, b), w_lru_gates[0, bass.ds(b, 1)].rearrange("b (k p) n -> p (b k) n", p=P), 2)
            for j in range(2):
                load(pieces.use("recE", j), rec_piece(j + 4, (BLOCKS - 1) * LW), 2)

            def load_ffn(f):
                for j, kind in enumerate(("G0", "U0", "G1", "U1")):
                    if f == 1 and j == 2:
                        sp.wait_ge(out_filled, OUT_FFN[1])
                    load(pieces.use(f"ffn{f}A", j), ffn_piece(f, kind, 0))
                with sp.Fori(1, GROUPS) as g:
                    for j, kind in enumerate(("G0", "O0", "O1", "U0", "G1", "U1")):
                        is_out = kind[0] == "O"
                        load(pieces.use(f"ffn{f}L", j, g), ffn_piece(f, kind, g - 1 if is_out else g),
                             2 if is_out else KT)
                for j, kind in enumerate(("O0", "O1")):
                    load(pieces.use(f"ffn{f}E", j), ffn_piece(f, kind, GROUPS - 1), 2)

            load_ffn(0)

            slot, n = pieces.use("forget", 0)
            sp.wait_ge(forget_dve, 1)
            sp.dma_start(raw[slot][:, :].rearrange("p (k n) -> p k n", k=KT)[:, :, 0:HEADS],
                         w_kvf[:, 2 * D:].rearrange("(k p) n -> p k n", p=P)).then_inc(loaded[slot], 16)
            for j, kind in enumerate("KVQ"):
                load(pieces.use("attA", j), att_piece(kind, 0))
            with sp.Fori(1, PAIRS) as i:
                for j, kind in enumerate("KVQ"):
                    load(pieces.use("attL", j, i), att_piece(kind, i))
                load(pieces.use("attL", 3, i), att_piece("O", i - 1), 1)
            load(pieces.use("attE", 0), att_piece("O", PAIRS - 1), 1)

            load_ffn(1)

            for b in range(QB):
                sp.wait_ge(rows_ready, b + 1)
                sp.dma_start(out[0, b * P:(b + 1) * P, :], tmp[b % 4][:, :]).then_inc(rows_stored[b % 4], 16)
            for b in range(4):
                sp.wait_ge(rows_stored[b], 16 * (QB // 4))

        @block.gpsimd
        def _(pool):
            pool.memset(ident[:, :], 0.0)
            pool.memset(ones[:, :], 1.0)
            pool.memset(identb[:, :], 0.0)
            pool.memset(maskb[:, :], 0.0)
            pool.memset(negsel[:, :], 0.0).then_inc(const_zero, 1)
            pool.wait_ge(const_zero, 1)
            for m in (ident, identb):
                pool.affine_select(out=m[:, :], in_=m[:, :], compare_op=ALU.not_equal, fill=1.0, base=0,
                                   pattern=[[-1, P]], channel_multiplier=1)
            pool.affine_select(out=maskb[:, :], in_=maskb[:, :], compare_op=ALU.is_ge, fill=NEG, base=0,
                               pattern=[[-1, P]], channel_multiplier=1)
            pool.affine_select(out=negsel[:, :], in_=negsel[:, :], compare_op=ALU.not_equal, fill=-1.0, base=0,
                               pattern=[[-1, HEADS]], channel_multiplier=1).then_inc(const_zero, 1)
            pool.wait_ge(const_zero, 2)
            pool.affine_select(out=negsel[:, :], in_=negsel[:, :], compare_op=ALU.not_equal, fill=-1.0, base=-32,
                               pattern=[[-1, HEADS]], channel_multiplier=1).then_inc(const_ready, 1)

        @block.tensor
        def _(pe):
            halves = [slice(0, BANK), slice(BANK, S)]

            def claim(use):
                slot, n = use
                pe.wait_ge(drained[slot], n - 1)
                return ps[slot]

            def split_product(acc, terms):
                last = None
                for k, (w_hi, w_lo, x_hi, x_lo) in enumerate(terms):
                    for p, (w, v) in enumerate(((w_hi, x_hi), (w_hi, x_lo), (w_lo, x_hi))):
                        for h in halves:
                            last = pe.matmul(acc[:, h], w, v[:, h], start=(k == 0 and p == 0),
                                             stop=(k == len(terms) - 1 and p == 2))
                return last

            def stationary(slot, k, n, width):
                at = k * width + n * P
                return wh[slot][:, at:at + P], wl[slot][:, at:at + P]

            def in_tile(piece, tile):
                slot, n = piece
                acc = claim(tile)
                pe.wait_ge(lo_ready[slot], n)
                split_product(acc, [(*stationary(slot, k, 0, P), xh[:, k, :], xl[:, k, :])
                                    for k in range(KT)]).then_inc(in_filled, 1)

            def out_tiles(piece, tile_uses, hi, lo):
                slot, n = piece
                for m, tile in enumerate(tile_uses):
                    acc = claim(tile)
                    if m == 0:
                        pe.wait_ge(lo_ready[slot], n)
                    split_product(acc, [(*stationary(slot, k, m, BANK), hi[:, k, :], lo[:, k, :])
                                        for k in range(2)]).then_inc(out_filled, 1)

            def stat(seg, k):
                if k == 0:
                    claim(tiles.use(seg, 8))
                pe.wait_ge(sq_ready, STAT[seg] * KT + k + 1)
                for h in halves:
                    last = pe.matmul(ps[3][:, h], ones[:, :], sq(seg, k)[:, h], start=(k == 0), stop=(k == KT - 1))
                last.then_inc(stat_filled if k == KT - 1 else sq_used, 1)

            def out_and_stat(seg, tile_of):
                for m in range(KT):
                    tile_of(m)
                    if m >= 2:
                        stat(seg, m - 2)
                stat(seg, KT - 2)
                stat(seg, KT - 1)
                if seg != "ffn1E":
                    pe.wait_ge(xl_ready, (STAT[seg] + 1) * KT)

            def out_epilogue(seg, piece_seg, hi, lo):
                def tile_of(m):
                    slot, n = pieces.use(piece_seg, m // 4)
                    acc = claim(tiles.use(seg, m))
                    pe.wait_ge(lo_ready[slot], n)
                    split_product(acc, [(*stationary(slot, k, m % 4, BANK), hi[:, k, :], lo[:, k, :])
                                        for k in range(2)]).then_inc(out_filled, 1)
                out_and_stat(seg, tile_of)

            pe.wait_ge(const_ready, 1)
            pe.wait_ge(vec_loaded, 16 * 8)
            claim(tiles.use("vec", 0))
            pe.transpose(ps[3][:, 0:V_ALL], vrow[:, :], ident[0:V_ALL, 0:V_ALL]).then_inc(vec_filled, 1)
            pe.wait_ge(x_loaded, 16 * QB)

            def x_tile(m):
                acc = claim(tiles.use("start", m))
                for b in range(QB):
                    last = pe.transpose(acc[:, b * P:(b + 1) * P], xin[:, b, m * P:(m + 1) * P], ident[:, :])
                last.then_inc(xt_filled, 1)
            out_and_stat("start", x_tile)

            def rec_in(seg, b):
                for j in range(4):
                    in_tile(pieces.use(seg, j, b), tiles.use(seg, j, b))

            def rec_gates(seg, b, first):
                slot, n = pieces.use("gates", 0, b)
                pe.wait_ge(lo_ready[slot], n)
                pe.wait_ge(cl_ready, 2 * b + 2)
                for j, m in enumerate((2, 0, 3, 1)):
                    acc = claim(tiles.use(seg, first + j, b))
                    split_product(acc, [(*stationary(slot, k, m, BANK), ch[:, k, :], cl[:, k, :])
                                        for k in range(2)]).then_inc(gates_filled, 1)

            rec_in("recA", 0)
            rec_gates("recA", 0, 4)
            with pe.Fori(1, BLOCKS) as b:
                rec_in("recL", b)
                pe.wait_ge(yl_ready, 2 * b)
                for j in range(2):
                    out_tiles(pieces.use("recL", 4 + j, b),
                              [tiles.use("recL", 4 + 4 * j + m, b) for m in range(4)], yh, yl)
                rec_gates("recL", b, 12)
            pe.wait_ge(yl_ready, 2 * BLOCKS)
            out_epilogue("recE", "recE", yh, yl)

            def ffn(f):
                def step(seg, j, t, g):
                    in_tile(pieces.use(seg, j, g), tiles.use(seg, t, g))
                for j in range(4):
                    step(f"ffn{f}A", j, j, 0)
                with pe.Fori(1, GROUPS) as g:
                    seg = f"ffn{f}L"
                    step(seg, 0, 0, g)
                    pe.wait_ge(hl_ready, g * 2 + 2 * f * GROUPS)
                    for j in range(2):
                        out_tiles(pieces.use(seg, 1 + j, g),
                                  [tiles.use(seg, 1 + 4 * j + m, g) for m in range(4)], hh, hl)
                    for j in range(3):
                        step(seg, 3 + j, 9 + j, g)
                pe.wait_ge(hl_ready, (f + 1) * 2 * GROUPS)
                out_epilogue(f"ffn{f}E", f"ffn{f}E", hh, hl)

            ffn(0)

            slot, n = pieces.use("forget", 0)
            acc = claim(tiles.use("forget", 0))
            pe.wait_ge(lo_ready[slot], n)
            split_product(acc, [(*stationary(slot, k, 0, P), xh[:, k, :], xl[:, k, :])
                                for k in range(KT)]).then_inc(forget_filled, 1)

            def project(seg, i):
                for j in range(3):
                    if j == 2:
                        pe.wait_ge(ptl_ready, i * T_PAIR)
                    in_tile(pieces.use(seg, j, i), tiles.use(seg, j, i))
                acc = claim(tiles.use(seg, 3, i))
                pe.wait_ge(o_added, i * UNITS)
                v_slot, v_n = tiles.use(seg, 1, i)
                pe.wait_ge(drained[v_slot], v_n)
                for b in range(QB):
                    last = pe.transpose(acc[:, b * P:(b + 1) * P], kv_tmp[:, b * P:(b + 1) * P], ident[:, :])
                last.then_inc(vt_filled, 1)

            def scores(seg, first, i, u):
                j, r = u // RANGES, u % RANGES
                for half in range(2):
                    n = 2 * r + half
                    acc = claim(tiles.use(seg, first + 2 * u + half, i))
                    w = (n + 1) * P
                    for c0 in range(0, w, BANK):
                        c1 = min(w, c0 + BANK)
                        pe.matmul(acc[:, c0:c1], sel[:, j, :], c2[:, c0:c1], start=True, stop=False)
                        if c1 == w:
                            pe.matmul(acc[:, w - P:w], identb[:, :], maskb[:, :], start=False, stop=False)
                        q = qs[:, j, n * P:(n + 1) * P]
                        pe.matmul(acc[:, c0:c1], q, kh[:, j, c0:c1], start=False, stop=False)
                        last = pe.matmul(acc[:, c0:c1], q, kl[:, j, c0:c1], start=False, stop=True)
                    last.then_inc(s_filled, 1)

            def blocks_of(r, m):
                if m < r:
                    return [(2 * m, 0, 0), (2 * m + 1, 0, 2 * P)]
                return [(2 * m, 0, 0), (2 * m + 1, 1, 2 * P)]

            def attend(seg, first, i):
                t = [0]

                def transposes(u, m):
                    r = u % RANGES
                    t_now = t[0]
                    if t_now < 2:
                        pe.wait_ge(ptl_ready, i * T_PAIR)
                    else:
                        pe.wait_ge(ptl_ready, i * T_PAIR + (t_now - 1))
                    for kb, q0, col in blocks_of(r, m):
                        for q in range(q0, 2):
                            last = pe.transpose(t_ps[t_now % 2][:, col + (q - q0) * P:col + (q - q0 + 1) * P],
                                                probs[u % 2][:, q, kb * P:(kb + 1) * P], ident[:, :])
                    last.then_inc(t_filled, 1)
                    t[0] += 1
                    return t_now

                def values(u, m, t_now):
                    j, r = u // RANGES, u % RANGES
                    pe.wait_ge(ptl_ready, i * T_PAIR + (t_now + 1))
                    for kb, q0, col in blocks_of(r, m):
                        v = vs[:, j, kb, :, :].rearrange("p a d -> p (a d)")
                        n = (2 - q0) * P
                        for pt in (pth, ptl):
                            last = pe.matmul(o_ps[u % 2][:, q0 * P:2 * P], v, pt[t_now % 2][:, col:col + n],
                                             start=(kb == 0 and pt is pth),
                                             stop=(kb == 2 * r + 1 and pt is ptl))
                    last.then_inc(o_filled if m == r else pt_used, 1)

                pe.wait_ge(kdup_ready, i * 4 + 4)
                pe.wait_ge(ql_ready, i * 2 + 2)
                pe.wait_ge(sel_ready, i * 2 + 2)
                scores(seg, first, i, 0)
                for back in (2, 1):
                    slot, n = tiles.use(seg, first - back, i)
                    pe.wait_ge(drained[slot], n)
                for u in range(UNITS):
                    if u + 1 < UNITS:
                        scores(seg, first, i, u + 1)
                    r = u % RANGES
                    pe.wait_ge(p_ready, i * 2 * QB + 2 * (u + 1))
                    if u >= 2:
                        pe.wait_ge(o_added, i * UNITS + (u - 1))
                    t_prev = transposes(u, 0)
                    for m in range(r + 1):
                        t_next = transposes(u, m + 1) if m < r else None
                        values(u, m, t_prev)
                        t_prev = t_next

            def wo_tile(piece, tile, m):
                slot, n = piece
                acc = claim(tile)
                pe.wait_ge(lo_ready[slot], n)
                split_product(acc, [(wh[slot][:, m * P:(m + 1) * P], wl[slot][:, m * P:(m + 1) * P],
                                     oh[:, :], ol[:, :])]).then_inc(out_filled, 1)

            project("attA", 0)
            pe.wait_ge(c_ready, 2)
            attend("attA", 4, 0)
            with pe.Fori(1, PAIRS) as i:
                project("attL", i)
                pe.wait_ge(ol_ready, i)
                for m in range(KT):
                    wo_tile(pieces.use("attL", 3, i), tiles.use("attL", 4 + m, i), m)
                attend("attL", 12, i)
            pe.wait_ge(ol_ready, PAIRS)
            pe.wait_ge(ptl_ready, PAIRS * T_PAIR)
            pe.wait_ge(o_added, PAIRS * UNITS)
            out_and_stat("attE", lambda m: wo_tile(pieces.use("attE", 0), tiles.use("attE", m), m))

            ffn(1)

            pe.wait_ge(y_final, KT)
            for b in range(QB):
                if b < 4:
                    acc = claim(tiles.use("final", b))
                else:
                    pe.wait_ge(rows_ready, b - 3)
                    acc = ps[b % 4]
                for k in range(KT):
                    last = pe.transpose(acc[:, k * P:(k + 1) * P], resid[:, k, b * P:(b + 1) * P], ident[:, :])
                last.then_inc(rows_filled, 1)

        @block.scalar
        def _(act):
            def split_hi(use, free, gain=None):
                slot, n = use
                act.wait_ge(loaded[slot], n * 16)
                if free is not None:
                    act.wait_ge(*free)
                if gain is None:
                    act.activation(wh[slot][:, :], raw[slot][:, :], ACT.Copy).then_inc(hi_ready[slot], 1)
                    return
                for k in range(KT):
                    last = act.activation(wh[slot][:, k * P:(k + 1) * P], raw[slot][:, k * P:(k + 1) * P],
                                          ACT.Copy, scale=vec[:, gain + k:gain + k + 1])
                last.then_inc(hi_ready[slot], 1)

            def halves_of_resid(seg, k):
                slot, t = tiles.use(seg, k)
                act.wait_ge(drained[slot], t)
                if seg != "ffn1E":
                    act.activation(xh[:, k, :], resid[:, k, :], ACT.Copy).then_inc(xh_ready, 1)
                if k >= 2:
                    act.wait_ge(sq_used, STAT[seg] * (KT - 1) + k - 1)
                act.activation(sq(seg, k), resid[:, k, :], ACT.Square).then_inc(sq_ready, 1)

            def root(seg):
                slot, n = tiles.use(seg, 8)
                act.wait_ge(drained[slot], n)
                act.activation(rstd[:, :], rstd[:, :], ACT.Sqrt).then_inc(root_ready, 1)

            act.wait_ge(lru_step, 1)
            act.activation(lru[:, 1, :], lru[:, 0, :], ACT.Exp).then_inc(lru_step, 1)
            act.wait_ge(lru_step, 3)
            act.activation(lru[:, 3, :], lru[:, 2, :], ACT.Ln).then_inc(lru_step, 1)

            for k in range(KT):
                halves_of_resid("start", k)
            for j in range(2):
                split_hi(pieces.use("recA", j), None, GAIN["rec"])
            root("start")

            def conv_high(b, t):
                act.wait_ge(conv_ready, b * 2 + (t + 1))
                act.activation(ch[:, t, :], tmp[1 + 2 * t][:, :], ACT.Copy).then_inc(ch_ready, 1)

            def gate_gelu(seg, b, t):
                slot, n = tiles.use(seg, 2 + t, b)
                act.wait_ge(drained[slot], n)
                act.activation(gelu[:, t, :], gelu[:, t, :], ACT.Gelu_apprx_tanh).then_inc(gelu_ready, 1)

            def lru_gates(seg, first, b, t):
                bias = V_GATEB
                r_slot, _ = tiles.use(seg, first + 2 * t, b)
                i_slot, _ = tiles.use(seg, first + 2 * t + 1, b)
                act.wait_ge(gates_filled, b * 4 + (2 * t + 1))
                if t == 1:
                    act.wait_ge(yh_ready, b * 2 + 1)
                    act.wait_ge(yl_ready, b * 2 + 1)
                else:
                    act.wait_ge(cl_ready, b * 2 + 2)
                act.activation(tmp[0][:, :], ps[r_slot][:, :], ACT.Sigmoid,
                               bias=vec[:, bass.ds(b * 4 + (bias + 2 + t), 1)]).then_inc(drained[r_slot], 1)
                act.wait_ge(gates_filled, b * 4 + (2 * t + 2))
                act.activation(tmp[2][:, :], ps[i_slot][:, :], ACT.Sigmoid,
                               bias=vec[:, bass.ds(b * 4 + (bias + t), 1)]).then_inc(drained[i_slot], 1)
                act.wait_ge(drained[r_slot], tiles.use(seg, first + 2 * t, b)[1])
                act.activation(tmp[0][:, :], tmp[0][:, :], ACT.Tanh,
                               scale=lru[:, 0, bass.ds(b * 2 + t, 1)]).then_inc(lru_act, 1)
                act.wait_ge(lru_act, b * 4 + (2 * t + 1))
                act.activation(tmp[1][:, :], tmp[0][:, :], ACT.Sqrt, bias=TINY).then_inc(lru_act, 1)

            def y_high(b, t):
                act.wait_ge(y_ready, b * 2 + (t + 1))
                act.activation(yh[:, t, :], tmp[2][:, :], ACT.Copy).then_inc(yh_ready, 1)

            g = GAIN["rec"]
            act.wait_ge(lru_step, LRU_STEPS)
            split_hi(pieces.use("recA", 2), None, g)
            conv_high(0, 0)
            split_hi(pieces.use("recA", 3), (in_filled, 1), g)
            conv_high(0, 1)

            def rec_gates(seg, first, b, last):
                gate_gelu(seg, b, 0)
                if seg == "recL":
                    split_hi(pieces.use("recL", 5, b), rec_free(5, b))
                gate_gelu(seg, b, 1)
                split_hi(pieces.use("gates", 0, b), (gates_filled, b * 4))
                if last:
                    for j in range(2):
                        split_hi(pieces.use("recE", j), REC_END[j])
                else:
                    for j in range(3):
                        split_hi(pieces.use("recL", j, b + 1), rec_free(j, b + 1), g)
                for t in range(2):
                    lru_gates(seg, first, b, t)
                    y_high(b, t)
                    if t == 0 and not last:
                        split_hi(pieces.use("recL", 3, b + 1), rec_free(3, b + 1), g)

            def rec_body(b, last):
                conv_high(b, 0)
                conv_high(b, 1)
                split_hi(pieces.use("recL", 4, b), rec_free(4, b))
                rec_gates("recL", 12, b, last)

            rec_gates("recA", 4, 0, False)
            with act.Fori(1, BLOCKS - 1) as b:
                rec_body(b, False)
            rec_body(BLOCKS - 1, True)

            def epilogue(seg, nexts):
                nexts[0]()
                for k in range(KT):
                    halves_of_resid(seg, k)
                    if k == 4:
                        nexts[1]()
                root(seg)

            def ffn(f):
                g = GAIN[f"ffn{f}"]
                seg0, seg = f"ffn{f}A", f"ffn{f}L"

                def silu(sg, tile, grp, t):
                    slot, n = tiles.use(sg, tile, grp)
                    act.wait_ge(drained[slot], n)
                    act.activation(tmp[t][:, :], tmp[t][:, :], ACT.Silu).then_inc(silu_ready, 1)

                def h_high(grp, t):
                    act.wait_ge(h_ready, grp * 2 + (2 * f * GROUPS + t + 1))
                    act.activation(hh[:, t, :], tmp[2 + t][:, :], ACT.Copy).then_inc(hh_ready, 1)

                split_hi(pieces.use(seg0, 2), FFN_START[f][2], g)
                silu(seg0, 0, 0, 0)
                split_hi(pieces.use(seg0, 3), FFN_START[f][3], g)
                h_high(0, 0)
                split_hi(pieces.use(seg, 0, 1), ffn_free(f, 0, 1), g)
                silu(seg0, 2, 0, 1)
                split_hi(pieces.use(seg, 1, 1), ffn_free(f, 1, 1))
                h_high(0, 1)

                def body(grp, last):
                    split_hi(pieces.use(seg, 2, grp), ffn_free(f, 2, grp))
                    silu(seg, 0, grp, 0)
                    split_hi(pieces.use(seg, 3, grp), ffn_free(f, 3, grp), g)
                    split_hi(pieces.use(seg, 4, grp), ffn_free(f, 4, grp), g)
                    split_hi(pieces.use(seg, 5, grp), ffn_free(f, 5, grp), g)
                    h_high(grp, 0)
                    if last:
                        split_hi(pieces.use(f"ffn{f}E", 0), FFN_END[f][0])
                    else:
                        split_hi(pieces.use(seg, 0, grp + 1), ffn_free(f, 0, grp + 1), g)
                    silu(seg, 10, grp, 1)
                    if last:
                        split_hi(pieces.use(f"ffn{f}E", 1), FFN_END[f][1])
                    else:
                        split_hi(pieces.use(seg, 1, grp + 1), ffn_free(f, 1, grp + 1))
                    h_high(grp, 1)

                with act.Fori(1, GROUPS - 1) as grp:
                    body(grp, False)
                body(GROUPS - 1, True)

            epilogue("recE", [lambda: split_hi(pieces.use("ffn0A", 0), FFN_START[0][0], GAIN["ffn0"]),
                              lambda: split_hi(pieces.use("ffn0A", 1), FFN_START[0][1], GAIN["ffn0"])])
            ffn(0)

            epilogue("ffn0E", [lambda: split_hi(pieces.use("forget", 0), (gates_filled, 4 * BLOCKS), V_KV),
                               lambda: split_hi(pieces.use("attA", 0), ATT_START[0], V_KV)])
            act.wait_ge(forget_dve, 3)
            act.activation(qo_tmp[0:HEADS, :], qo_tmp[0:HEADS, :], ACT.Exp).then_inc(forget_act, 1)
            act.wait_ge(forget_dve, 4)
            act.activation(probs[1][0:HEADS, 1, :], probs[0][0:HEADS, 0, :], ACT.Ln).then_inc(forget_act, 1)
            split_hi(pieces.use("attA", 1), ATT_START[1], V_KV)
            act.wait_ge(forget_dve, FORGET_STEPS)
            act.activation(c2[0:HEADS, :], qo_tmp[0:HEADS, :], ACT.Copy).then_inc(c_ready, 1)

            def high_halves(seg, i):
                k_slot, k_n = tiles.use(seg, 0, i)
                act.wait_ge(drained[k_slot], k_n)
                act.activation(kh[0:HD, 0, :], kv_tmp[0:HD, :], ACT.Copy)
                act.activation(kh[HD:P, 1, :], kv_tmp[HD:P, :], ACT.Copy).then_inc(kh_ready, 1)
                act.wait_ge(kh_ready, i + 1)
                act.activation(kh[HD:P, 0, :], kh[0:HD, 0, :].bitcast(F32), ACT.Copy).then_inc(kdup_ready, 1)
                act.activation(kh[0:HD, 1, :], kh[HD:P, 1, :].bitcast(F32), ACT.Copy).then_inc(kdup_ready, 1)
                act.wait_ge(kl_ready, i + 1)
                act.activation(kl[HD:P, 0, :], kl[0:HD, 0, :].bitcast(F32), ACT.Copy).then_inc(kdup_ready, 1)
                act.activation(kl[0:HD, 1, :], kl[HD:P, 1, :].bitcast(F32), ACT.Copy).then_inc(kdup_ready, 1)

            def high_q(seg, i):
                q_slot, q_n = tiles.use(seg, 2, i)
                act.wait_ge(drained[q_slot], q_n)
                act.activation(qs[0:HD, 0, :], qo_tmp[0:HD, :], ACT.Copy).then_inc(qh_ready, 1)
                act.activation(qs[HD:P, 1, :], qo_tmp[HD:P, :], ACT.Copy).then_inc(qh_ready, 1)

            def high_v(seg, i):
                act.wait_ge(vt_filled, i + 1)
                slot, _ = tiles.use(seg, 3, i)
                src = ps[slot][:, :].rearrange("p (b j d) -> p j b d", b=QB, j=2)
                act.activation(vs[:, 0, :, 0, :], src[:, 0], ACT.Copy)
                act.activation(vs[:, 1, :, 0, :], src[:, 1], ACT.Copy).then_inc(vh_ready, 1)

            def attend(seg, first, i):
                t = [0]

                def exps(u):
                    for half in range(2):
                        n, w = 2 * u + half, (2 * (u % RANGES) + half + 1) * P
                        slot, _ = tiles.use(seg, first + n, i)
                        act.wait_ge(nmax_ready, i * 2 * QB + (n + 1))
                        if u >= 2:
                            act.wait_ge(t_filled, i * T_PAIR + tiles_before(u - 1))
                        act.activation(probs[u % 2][:, half, 0:w], ps[slot][:, 0:w], ACT.Exp,
                                       bias=nmax[:, n:n + 1], accum_out=rsum[:, n:n + 1]).then_inc(drained[slot], 1)

                exps(0)
                for u in range(UNITS):
                    if u + 1 < UNITS:
                        exps(u + 1)
                    r = u % RANGES
                    for m in range(r + 1):
                        now = t[0]
                        t[0] += 1
                        width = 4 * P if m < r else 3 * P
                        act.wait_ge(t_filled, i * T_PAIR + (now + 1))
                        if now >= 2:
                            act.wait_ge(*pt_used_at(i, now - 2))
                        act.activation(pth[now % 2][:, 0:width], t_ps[now % 2][:, 0:width], ACT.Copy).then_inc(pth_ready, 1)
                    act.wait_ge(o_filled, i * UNITS + (u + 1))
                    if u >= 2:
                        act.wait_ge(o_added, i * UNITS + (u - 1))
                    act.activation(o_low[u % 2][:, :], o_ps[u % 2][HD:P, :], ACT.Copy).then_inc(o_low_ready, 1)
                act.wait_ge(o_added, i * UNITS + UNITS)
                act.activation(oh[:, :], qo_tmp[:, :], ACT.Copy).then_inc(oh_ready, 1)

            high_halves("attA", 0)
            split_hi(pieces.use("attA", 2), ATT_START[2], GAIN["Q"])
            high_q("attA", 0)
            high_v("attA", 0)

            def att_body(i, last):
                split_hi(pieces.use("attL", 2, i), att_free(2, i), GAIN["Q"])
                high_halves("attL", i)
                split_hi(pieces.use("attL", 3, i), att_free(3, i))
                high_q("attL", i)
                high_v("attL", i)
                after(i, last)

            def after(i, last):
                if last:
                    split_hi(pieces.use("attE", 0), ATT_END[0])
                else:
                    split_hi(pieces.use("attL", 0, i + 1), att_free(0, i + 1), V_KV)
                    split_hi(pieces.use("attL", 1, i + 1), att_free(1, i + 1), V_KV)

            after(0, False)
            attend("attA", 4, 0)
            with act.Fori(1, PAIRS - 1) as i:
                att_body(i, False)
                attend("attL", 12, i)
            att_body(PAIRS - 1, True)
            attend("attL", 12, PAIRS - 1)
            epilogue("attE", [lambda: split_hi(pieces.use("ffn1A", 0), FFN_START[1][0], GAIN["ffn1"]),
                              lambda: None])
            split_hi(pieces.use("ffn1A", 1), FFN_START[1][1], GAIN["ffn1"])
            ffn(1)
            for k in range(KT):
                halves_of_resid("ffn1E", k)
            root("ffn1E")
            for b in range(1, QB, 2):
                slot, n = tiles.use("final", b)
                act.wait_ge(rows_filled, b + 1)
                if b >= 4:
                    act.wait_ge(rows_stored[b % 4], 16)
                act.wait_ge(rows_ready, b)
                act.activation(tmp[b % 4][:, :], ps[slot][:, :], ACT.Copy).then_inc(rows_ready, 1)

        @block.vector
        def _(dve):
            def split_lo(use, gain=None):
                slot, n = use
                dve.wait_ge(hi_ready[slot], n)
                if gain is None:
                    dve.tensor_tensor(wl[slot][:, :], raw[slot][:, :], wh[slot][:, :].bitcast(F32),
                                      ALU.subtract).then_inc(lo_ready[slot], 1)
                    return
                for k in range(KT):
                    c = slice(k * P, (k + 1) * P)
                    last = dve.scalar_tensor_tensor(out=wl[slot][:, c], in0=raw[slot][:, c],
                                                    scalar=vec[:, gain + k:gain + k + 1],
                                                    in1=wh[slot][:, c].bitcast(F32), op0=ALU.mult, op1=ALU.subtract)
                last.then_inc(lo_ready[slot], 1)

            def low_half(seg, k):
                dve.wait_ge(xh_ready, STAT[seg] * KT + k + 1)
                dve.tensor_tensor(xl[:, k, :], resid[:, k, :], xh[:, k, :].bitcast(F32),
                                  ALU.subtract).then_inc(xl_ready, 1)

            def mean_square(seg):
                slot, _ = tiles.use(seg, 8)
                dve.wait_ge(stat_filled, STAT[seg] + 1)
                dve.tensor_scalar(rstd[:, :], ps[slot][:, :], 1.0 / D, EPS, ALU.mult, ALU.add).then_inc(drained[slot], 1)

            def inverse_root(seg):
                dve.wait_ge(root_ready, STAT[seg] + 1)
                dve.reciprocal(rstd[:, :], rstd[:, :]).then_inc(rstd_ready, 1)
                dve.wait_ge(rstd_ready, STAT[seg] + 1)

            def scaled(dst, tile, filled, count):
                slot, n = tile
                dve.wait_ge(filled, count)
                dve.tensor_tensor(dst, ps[slot][:, :], rstd[:, :], ALU.mult).then_inc(drained[slot], 1)

            def add_tile(tile, m, count):
                slot, _ = tile
                dve.wait_ge(out_filled, count)
                dve.tensor_tensor(resid[:, m, :], ps[slot][:, :], resid[:, m, :], ALU.add).then_inc(drained[slot], 1)

            dve.wait_ge(vec_filled, 1)
            dve.tensor_copy(vec[:, :], ps[3][:, 0:V_ALL]).then_inc(drained[3], 1)
            dve.wait_ge(drained[3], 1)
            lp = vec[:, V_LRU:V_LRU + KT]
            dve.scalar_tensor_tensor(out=lru[:, 0, :], in0=lp, scalar=-1.0, in1=lp, op0=ALU.mult,
                                     op1=ALU.min).then_inc(lru_step, 1)
            dve.wait_ge(lru_step, 2)
            steps = [2]

            def lru_next(ins, more=1):
                ins.then_inc(lru_step, 1)
                steps[0] += more
                dve.wait_ge(lru_step, steps[0])

            lru_next(dve.tensor_scalar(lru[:, 2, :], lru[:, 1, :], 1.0, None, ALU.add), 2)
            lru_next(dve.tensor_scalar(lru[:, 4, :], lru[:, 2, :], -1.0, None, ALU.add))
            lru_next(dve.tensor_scalar(lru[:, 5, :], lru[:, 4, :], 0.0, None, ALU.is_equal))
            lru_next(dve.tensor_tensor(lru[:, 4, :], lru[:, 4, :], lru[:, 5, :], ALU.add))
            lru_next(dve.reciprocal(lru[:, 4, :], lru[:, 4, :]))
            lru_next(dve.tensor_tensor(lru[:, 3, :], lru[:, 3, :], lru[:, 1, :], ALU.mult))
            lru_next(dve.tensor_tensor(lru[:, 3, :], lru[:, 3, :], lru[:, 4, :], ALU.mult))
            lru_next(dve.tensor_tensor(lru[:, 5, :], lru[:, 5, :], lru[:, 1, :], ALU.mult))
            lru_next(dve.tensor_tensor(lru[:, 3, :], lru[:, 3, :], lru[:, 5, :], ALU.add))
            lru_next(dve.tensor_scalar(lru[:, 2, :], lp, -1.0, 0.0, ALU.mult, ALU.max))
            lru_next(dve.tensor_tensor(lru[:, 3, :], lru[:, 3, :], lru[:, 2, :], ALU.add))
            lru_next(dve.tensor_scalar(lru[:, 0, :], lru[:, 3, :], LRU_C / 2, None, ALU.mult))
            assert steps[0] == LRU_STEPS, steps

            for k in range(KT):
                slot, _ = tiles.use("start", k)
                dve.wait_ge(xt_filled, k + 1)
                dve.tensor_copy(resid[:, k, :], ps[slot][:, :]).then_inc(drained[slot], 1)
                if k >= 1:
                    low_half("start", k - 1)
            low_half("start", KT - 1)
            mean_square("start")
            g = GAIN["rec"]
            for j in range(2):
                split_lo(pieces.use("recA", j), g)
            inverse_root("start")

            def conv(seg, b, t):
                r, acc = tmp[2 * t], tmp[2 * t + 1]
                tile = tiles.use(seg, t, b)
                scaled(r[:, :], tile, in_filled, b * 4 + (t + 1))
                dve.wait_ge(drained[tile[0]], tile[1])
                tap = lambda k: vec[:, bass.ds(b * 2 + (V_CONVW + (TAPS - 1 - k) * KT + t), 1)]
                dve.tensor_scalar(acc[:, :], r[:, :], tap(0), vec[:, bass.ds(b * 2 + (V_CONVB + t), 1)],
                                  ALU.mult, ALU.add).then_inc(conv_step, 1)
                for k in range(1, TAPS):
                    dve.wait_ge(conv_step, b * (2 * (TAPS - 1)) + (t * (TAPS - 1) + k))
                    dve.scalar_tensor_tensor(out=acc[:, k:], in0=r[:, :S - k], scalar=tap(k), in1=acc[:, k:],
                                             op0=ALU.mult, op1=ALU.add).then_inc(
                                                 conv_step if k < TAPS - 1 else conv_ready, 1)

            def conv_low(b, t):
                dve.wait_ge(ch_ready, b * 2 + (t + 1))
                dve.tensor_tensor(cl[:, t, :], tmp[2 * t + 1][:, :], ch[:, t, :].bitcast(F32),
                                  ALU.subtract).then_inc(cl_ready, 1)

            def lru_scan(seg, first, b, t):
                at = [0]

                def step(ins):
                    ins.then_inc(lru_dve, 1)
                    at[0] += 1

                def have(k):
                    dve.wait_ge(lru_dve, b * 16 + (8 * t + k))

                dve.wait_ge(lru_act, b * 4 + (2 * t + 2))
                step(dve.tensor_scalar(tmp[0][:, :], tmp[0][:, :], 1.0, None, ALU.add))
                step(dve.tensor_tensor(tmp[3][:, :], ch[:, t, :].bitcast(F32), cl[:, t, :].bitcast(F32), ALU.add))
                have(1)
                step(dve.reciprocal(tmp[0][:, :], tmp[0][:, :]))
                have(2)
                i_slot, i_n = tiles.use(seg, first + 2 * t + 1, b)
                dve.wait_ge(drained[i_slot], i_n)
                step(dve.tensor_tensor(tmp[3][:, :], tmp[3][:, :], tmp[2][:, :], ALU.mult))
                have(3)
                step(dve.scalar_tensor_tensor(out=tmp[1][:, :], in0=tmp[1][:, :], scalar=2.0, in1=tmp[0][:, :],
                                              op0=ALU.mult, op1=ALU.mult))
                step(dve.tensor_scalar(tmp[0][:, :], tmp[0][:, :], 2.0, -1.0, ALU.mult, ALU.add))
                have(5)
                step(dve.tensor_tensor(tmp[1][:, :], tmp[1][:, :], tmp[3][:, :], ALU.mult))
                have(7)
                step(dve.tensor_tensor_scan(tmp[2][:, :], tmp[0][:, :], tmp[1][:, :], 0.0, ALU.mult, ALU.add))
                have(8)
                dve.wait_ge(gelu_ready, b * 2 + (t + 1))
                dve.tensor_tensor(tmp[2][:, :], tmp[2][:, :], gelu[:, t, :], ALU.mult).then_inc(y_ready, 1)

            def y_low(b, t):
                dve.wait_ge(yh_ready, b * 2 + (t + 1))
                dve.tensor_tensor(yl[:, t, :], tmp[2][:, :], yh[:, t, :].bitcast(F32), ALU.subtract).then_inc(yl_ready, 1)

            def rec_rest(seg, first, b, last):
                for t in range(2):
                    scaled(gelu[:, t, :], tiles.use(seg, 2 + t, b), in_filled, b * 4 + (3 + t))
                    if t == 0 and seg == "recL":
                        split_lo(pieces.use("recL", 5, b))
                split_lo(pieces.use("gates", 0, b))
                if seg == "recL":
                    for m in range(KT):
                        add_tile(tiles.use(seg, 4 + m, b), m, b * KT + (m + 1 - KT))
                if last:
                    for j in range(2):
                        split_lo(pieces.use("recE", j))
                else:
                    for j in range(3):
                        split_lo(pieces.use("recL", j, b + 1), g)
                for t in range(2):
                    lru_scan(seg, first, b, t)
                    y_low(b, t)
                    if t == 0 and not last:
                        split_lo(pieces.use("recL", 3, b + 1), g)

            def rec_body(b, last):
                conv("recL", b, 0)
                conv("recL", b, 1)
                conv_low(b, 0)
                conv_low(b, 1)
                split_lo(pieces.use("recL", 4, b))
                rec_rest("recL", 12, b, last)

            split_lo(pieces.use("recA", 2), g)
            conv("recA", 0, 0)
            split_lo(pieces.use("recA", 3), g)
            conv_low(0, 0)
            conv("recA", 0, 1)
            conv_low(0, 1)
            rec_rest("recA", 4, 0, False)
            with dve.Fori(1, BLOCKS - 1) as b:
                rec_body(b, False)
            rec_body(BLOCKS - 1, True)
            slot, _ = pieces.use("forget", 0)
            dve.memset(raw[slot][:, :], 0.0).then_inc(forget_dve, 1)

            def epilogue(seg, out_count, nexts):
                nexts[0]()
                for k in range(KT):
                    add_tile(tiles.use(seg, k), k, out_count + k + 1)
                    if seg != "ffn1E" and k >= 1:
                        low_half(seg, k - 1)
                    if k == 5:
                        nexts[1]()
                if seg != "ffn1E":
                    low_half(seg, KT - 1)
                mean_square(seg)
                inverse_root(seg)

            def ffn(f):
                gain = GAIN[f"ffn{f}"]
                seg0, seg = f"ffn{f}A", f"ffn{f}L"

                def gate(sg, tile, grp, t):
                    scaled(tmp[t][:, :], tiles.use(sg, tile, grp), in_filled, grp * 4 + (IN_FFN[f] + 2 * t + 1))

                def hidden(sg, tile, grp, t):
                    use = tiles.use(sg, tile, grp)
                    scaled(tmp[2 + t][:, :], use, in_filled, grp * 4 + (IN_FFN[f] + 2 * t + 2))
                    dve.wait_ge(drained[use[0]], use[1])
                    dve.wait_ge(silu_ready, grp * 2 + (2 * f * GROUPS + t + 1))
                    dve.tensor_tensor(tmp[2 + t][:, :], tmp[2 + t][:, :], tmp[t][:, :], ALU.mult).then_inc(h_ready, 1)

                def h_low(grp, t):
                    dve.wait_ge(hh_ready, grp * 2 + (2 * f * GROUPS + t + 1))
                    dve.tensor_tensor(hl[:, t, :], tmp[2 + t][:, :], hh[:, t, :].bitcast(F32),
                                      ALU.subtract).then_inc(hl_ready, 1)

                split_lo(pieces.use(seg0, 2), gain)
                gate(seg0, 0, 0, 0)
                split_lo(pieces.use(seg0, 3), gain)
                hidden(seg0, 1, 0, 0)
                h_low(0, 0)
                split_lo(pieces.use(seg, 0, 1), gain)
                gate(seg0, 2, 0, 1)
                split_lo(pieces.use(seg, 1, 1))
                hidden(seg0, 3, 0, 1)
                h_low(0, 1)

                def body(grp, last):
                    split_lo(pieces.use(seg, 2, grp))
                    gate(seg, 0, grp, 0)
                    for j in range(2):
                        split_lo(pieces.use(seg, 3 + j, grp), gain)
                        for m in range(4 * j, 4 * j + 4):
                            add_tile(tiles.use(seg, 1 + m, grp), m, grp * KT + (OUT_FFN[f] + m + 1 - KT))
                    split_lo(pieces.use(seg, 5, grp), gain)
                    hidden(seg, 9, grp, 0)
                    h_low(grp, 0)
                    if last:
                        split_lo(pieces.use(f"ffn{f}E", 0))
                    else:
                        split_lo(pieces.use(seg, 0, grp + 1), gain)
                    gate(seg, 10, grp, 1)
                    if last:
                        split_lo(pieces.use(f"ffn{f}E", 1))
                    else:
                        split_lo(pieces.use(seg, 1, grp + 1))
                    hidden(seg, 11, grp, 1)
                    h_low(grp, 1)

                with dve.Fori(1, GROUPS - 1) as grp:
                    body(grp, False)
                body(GROUPS - 1, True)

            epilogue("recE", 8 * (BLOCKS - 1), [lambda: split_lo(pieces.use("ffn0A", 0), GAIN["ffn0"]),
                                                lambda: split_lo(pieces.use("ffn0A", 1), GAIN["ffn0"])])
            ffn(0)
            epilogue("ffn0E", OUT_FFN[0] + 8 * (GROUPS - 1), [lambda: split_lo(pieces.use("forget", 0), V_KV),
                                                              lambda: split_lo(pieces.use("attA", 0), V_KV)])

            z, e = kv_tmp[0:HEADS, :], qo_tmp[0:HEADS, :]
            one_e, d = probs[0][0:HEADS, 0, :], probs[0][0:HEADS, 1, :]
            lost, log1p = probs[1][0:HEADS, 0, :], probs[1][0:HEADS, 1, :]
            done = [1]

            def chain(ins):
                ins.then_inc(forget_dve, 1)
                done[0] += 1
                dve.wait_ge(forget_dve, done[0])

            f_slot, f_n = tiles.use("forget", 0)
            dve.memset(c2[:, :].bitcast(F32), 0.0)
            dve.wait_ge(forget_filled, 1)
            dve.tensor_tensor(z, ps[f_slot][0:HEADS, :], rstd[0:HEADS, :], ALU.mult).then_inc(drained[f_slot], 1)
            dve.wait_ge(drained[f_slot], f_n)
            dve.wait_ge(bforget_loaded, 16)
            chain(dve.tensor_scalar(z, z, bforget[:, 0:1], None, ALU.add))
            chain(dve.scalar_tensor_tensor(out=e, in0=z, scalar=-1.0, in1=z, op0=ALU.mult, op1=ALU.min))
            dve.wait_ge(forget_act, 1)
            chain(dve.tensor_scalar(one_e, e, 1.0, None, ALU.add))
            chain(dve.tensor_scalar(d, one_e, -1.0, None, ALU.add))
            chain(dve.tensor_scalar(lost, d, 0.0, None, ALU.is_equal))
            chain(dve.tensor_tensor(d, d, lost, ALU.add))
            chain(dve.reciprocal(d, d))
            dve.wait_ge(forget_act, 2)
            chain(dve.tensor_tensor(log1p, log1p, e, ALU.mult))
            chain(dve.tensor_tensor(log1p, log1p, d, ALU.mult))
            chain(dve.tensor_tensor(lost, lost, e, ALU.mult))
            chain(dve.tensor_tensor(log1p, log1p, lost, ALU.add))
            chain(dve.tensor_scalar(z, z, 0.0, None, ALU.min))
            chain(dve.tensor_tensor(z, z, log1p, ALU.subtract))
            chain(dve.memset(one_e, 1.0))
            chain(dve.tensor_tensor_scan(e, one_e, z, 0.0, ALU.mult, ALU.add))
            assert done[0] == FORGET_STEPS, done
            split_lo(pieces.use("attA", 1), V_KV)
            dve.wait_ge(c_ready, 1)
            dve.tensor_tensor(c2[32:32 + HEADS, :], e, c2[0:HEADS, :].bitcast(F32), ALU.subtract).then_inc(c_ready, 1)

            def project(seg, i, before_q):
                scaled(kv_tmp[:, :], tiles.use(seg, 0, i), in_filled, i * 3 + (IN_ATT + 1))
                dve.wait_ge(kh_ready, i + 1)
                dve.tensor_tensor(kl[0:HD, 0, :], kv_tmp[0:HD, :], kh[0:HD, 0, :].bitcast(F32), ALU.subtract)
                dve.tensor_tensor(kl[HD:P, 1, :], kv_tmp[HD:P, :], kh[HD:P, 1, :].bitcast(F32),
                                  ALU.subtract).then_inc(kl_ready, 1)
                dve.wait_ge(kl_ready, i + 1)
                scaled(kv_tmp[:, :], tiles.use(seg, 1, i), in_filled, i * 3 + (IN_ATT + 2))
                before_q()
                slot, _ = tiles.use(seg, 2, i)
                dve.wait_ge(in_filled, i * 3 + (IN_ATT + 3))
                dve.scalar_tensor_tensor(out=qo_tmp[:, :], in0=ps[slot][:, :], scalar=float(HD) ** -0.5,
                                         in1=rstd[:, :], op0=ALU.mult, op1=ALU.mult).then_inc(drained[slot], 1)
                for j in range(2):
                    dve.tensor_scalar(sel[:, j, :], ones[:, :], negsel[:, bass.ds(i * 2 + j, 1)], None,
                                      ALU.mult).then_inc(sel_ready, 1)
                for j in range(2):
                    mine = slice(j * HD, (j + 1) * HD)
                    other = slice((1 - j) * HD, (2 - j) * HD)
                    dve.wait_ge(qh_ready, i * 2 + (j + 1))
                    dve.tensor_tensor(qs[other, j, :], qo_tmp[mine, :], qs[mine, j, :].bitcast(F32),
                                      ALU.subtract).then_inc(ql_ready, 1)
                slot, _ = tiles.use(seg, 3, i)
                dve.wait_ge(vh_ready, i + 1)
                src = ps[slot][:, :].rearrange("p (b j d) -> p j b d", b=QB, j=2)
                dve.tensor_tensor(vs[:, 0, :, 1, :], src[:, 0], vs[:, 0, :, 0, :].bitcast(F32), ALU.subtract)
                dve.tensor_tensor(vs[:, 1, :, 1, :], src[:, 1], vs[:, 1, :, 0, :].bitcast(F32),
                                  ALU.subtract).then_inc(drained[slot], 1)

            def attend(seg, first, i):
                t = [0]

                def row_max(u):
                    for half in range(2):
                        n, w = 2 * u + half, (2 * (u % RANGES) + half + 1) * P
                        slot, _ = tiles.use(seg, first + n, i)
                        dve.wait_ge(s_filled, i * 2 * QB + (n + 1))
                        dve.tensor_reduce(nmax[:, n:n + 1], ps[slot][:, 0:w], AX.X, ALU.max,
                                          negate=True).then_inc(nmax_ready, 1)

                def normalise(u):
                    for half in range(2):
                        n, w = 2 * u + half, (2 * (u % RANGES) + half + 1) * P
                        slot, s_n = tiles.use(seg, first + n, i)
                        dve.wait_ge(drained[slot], s_n)
                        dve.reciprocal(rinv[:, n:n + 1], rsum[:, n:n + 1]).then_inc(rinv_ready, 1)
                    for half in range(2):
                        n, w = 2 * u + half, (2 * (u % RANGES) + half + 1) * P
                        dve.wait_ge(rinv_ready, i * 2 * QB + (n + 1))
                        dve.tensor_scalar(probs[u % 2][:, half, 0:w], probs[u % 2][:, half, 0:w],
                                          rinv[:, n:n + 1], None, ALU.mult).then_inc(p_ready, 1)

                row_max(0)
                normalise(0)
                for u in range(UNITS):
                    if u + 1 < UNITS:
                        row_max(u + 1)
                    j, r = u // RANGES, u % RANGES
                    for m in range(r + 1):
                        now = t[0]
                        t[0] += 1
                        width = 4 * P if m < r else 3 * P
                        dve.wait_ge(pth_ready, i * T_PAIR + (now + 1))
                        dve.tensor_tensor(ptl[now % 2][:, 0:width], t_ps[now % 2][:, 0:width],
                                          pth[now % 2][:, 0:width].bitcast(F32), ALU.subtract).then_inc(ptl_ready, 1)
                        if m == 0 and u + 1 < UNITS:
                            normalise(u + 1)
                    dve.wait_ge(o_low_ready, i * UNITS + (u + 1))
                    dve.tensor_tensor(qo_tmp[j * HD:(j + 1) * HD, r * 2 * P:(r + 1) * 2 * P], o_ps[u % 2][0:HD, :],
                                      o_low[u % 2][:, :], ALU.add).then_inc(o_added, 1)
                dve.wait_ge(oh_ready, i + 1)
                dve.tensor_tensor(ol[:, :], qo_tmp[:, :], oh[:, :].bitcast(F32), ALU.subtract).then_inc(ol_ready, 1)

            def after(i, last):
                if last:
                    split_lo(pieces.use("attE", 0))
                else:
                    split_lo(pieces.use("attL", 0, i + 1), V_KV)
                    split_lo(pieces.use("attL", 1, i + 1), V_KV)

            def att_body(i, last):
                split_lo(pieces.use("attL", 2, i), GAIN["Q"])
                project("attL", i, lambda: split_lo(pieces.use("attL", 3, i)))
                for m in range(KT):
                    add_tile(tiles.use("attL", 4 + m, i), m, i * KT + (OUT_ATT + m + 1 - KT))
                after(i, last)
                attend("attL", 12, i)

            project("attA", 0, lambda: split_lo(pieces.use("attA", 2), GAIN["Q"]))
            after(0, False)
            attend("attA", 4, 0)
            with dve.Fori(1, PAIRS - 1) as i:
                att_body(i, False)
            att_body(PAIRS - 1, True)
            epilogue("attE", OUT_ATT + 8 * (PAIRS - 1),
                     [lambda: split_lo(pieces.use("ffn1A", 0), GAIN["ffn1"]), lambda: None])
            split_lo(pieces.use("ffn1A", 1), GAIN["ffn1"])
            ffn(1)
            epilogue("ffn1E", OUT_FFN[1] + 8 * (GROUPS - 1), [lambda: None, lambda: None])

            for k in range(KT):
                dve.scalar_tensor_tensor(out=resid[:, k, :], in0=resid[:, k, :],
                                         scalar=vec[:, V_FINAL + k:V_FINAL + k + 1], in1=rstd[:, :],
                                         op0=ALU.mult, op1=ALU.mult).then_inc(y_final, 1)
            for b in range(0, QB, 2):
                dve.wait_ge(rows_filled, b + 1)
                if b >= 4:
                    dve.wait_ge(rows_stored[b % 4], 16)
                if b >= 1:
                    dve.wait_ge(rows_ready, b)
                dve.tensor_copy(tmp[b % 4][:, :], ps[tiles.use("final", b)[0]][:, :]).then_inc(rows_ready, 1)


_INS = ["x", "norm_mix", "norm_ffn", "w_ffn_in", "w_ffn_out", "w_rec_in", "conv_w", "conv_b", "w_lru_gates",
        "b_lru_gates", "lru_param", "w_rec_out", "norm_kv", "w_kvf", "b_forget", "w_q", "w_o", "norm_final"]


def kernel(**inputs):
    import numpy as np
    import concourse.bacc as bacc
    from concourse.bass_utils import run_bass_kernel_spmd

    nc = bacc.Bacc("TRN2", target_bir_lowering=False, num_devices=1)
    arrays, args = {}, []
    for name in _INS:
        a = np.ascontiguousarray(inputs[name])
        arrays[f"in_{name}"] = a
        args.append(nc.dram_tensor(f"in_{name}", a.shape, mybir.dt.from_np(a.dtype), kind="ExternalInput").ap())
    out = nc.dram_tensor("out", inputs["x"].shape, F32, kind="ExternalOutput").ap()
    hawk_fox_yoco(nc, *args, out)
    r = run_bass_kernel_spmd(nc, [arrays], core_ids=[0])
    return r.results[0]["out"]
```

```python
import concourse.bass as bass
from concourse import mybir
from contextlib import ExitStack

F32 = mybir.dt.float32
F32R = mybir.dt.float32r
BF16 = mybir.dt.bfloat16
ALU = mybir.AluOpType
ACT = mybir.ActivationFunctionType
AX = mybir.AxisListType

P = 128
BANK = 512
EPS = 1e-6
LRU_C = 8.0
NEG = -1e30
TINY = 1e-34


class Turns:

    def __init__(self, slots):
        self.total = [0] * slots
        self.segments = {}

    def plan(self, name, order, iters=1, first=0, stride=1):
        assert all(order.count(s) % stride == 0 for s in order)
        self.segments[name] = (list(self.total), order, first, stride)
        for s in order:
            self.total[s] += iters
        return self

    def use(self, name, j, i=0):
        base, order, first, stride = self.segments[name]
        s = order[j]
        per = order.count(s) // stride
        return s, i * per + (base[s] - first * per + order[:j].count(s) + 1)


RANGE_ORDER = [3, 0, 2, 1]
UNIT_STEPS = {
    3: "O T0 S0 T1 V0 S1 w T2 V1 N0 w T3 V2 N1 w V3",
    0: "O T0 S0 p p p V0 S1 N0 N1 p p p p p",
    2: "O T0 S0 T1 V0 S1 w T2 V1 N0 w V2 N1 w",
    1: "O T0 S0 T1 V0 S1 p p p V1 N0 N1 p p p p p",
}
PAIR_START = "V S0 S1 w X N0 w w N1 w"


HI_AT = {(0, "T0"): ("K", 0, 2), (0, "S0"): ("K", 2, 4), (0, "T1"): ("K", 4, 6), (0, "S1"): ("K", 6, 8),
         (4, "T0"): ("Q", 0, 2), (4, "S0"): ("Q", 2, 4), (4, "T1"): ("Q", 4, 6), (4, "S1"): ("Q", 6, 8),
         (7, "T1"): ("nextV", 0, 8)}
LO_AT = {(0, "T2"): ("K", 0, 2), (0, "N0"): ("K", 2, 4), (0, "T3"): ("K", 4, 6), (0, "N1"): ("K", 6, 8),
         (4, "T2"): ("Q", 0, 2), (4, "N0"): ("Q", 2, 4), (4, "T3"): ("Q", 4, 6), (4, "N1"): ("Q", 6, 8),
         (7, "T1"): ("nextV", 0, 8)}


def pair_steps(with_w, with_p):
    steps = [(-1, s) for s in PAIR_START.split()]
    units = 2 * len(RANGE_ORDER)
    for u in range(units):
        for s in UNIT_STEPS[RANGE_ORDER[u % len(RANGE_ORDER)]].split():
            if u == 0 and s == "O" or u == units - 1 and s[0] in "SN":
                continue
            steps.append((u, s))
    steps.append((units, "O"))
    return [x for x in steps if (x[1] != "w" or with_w) and (x[1] != "p" or with_p)]


def hawk_fox_yoco(nc, x, norm_mix, norm_ffn, w_ffn_in, w_ffn_out, w_rec_in, conv_w, conv_b,
                  w_lru_gates, b_lru_gates, lru_param, w_rec_out, norm_kv, w_kvf, b_forget,
                  w_q, w_o, norm_final, out):
    S, D = x.shape[1], x.shape[2]
    KT = D // P
    FF = w_ffn_out.shape[1]
    GROUPS = FF // (2 * P)
    BLOCKS, LW = w_lru_gates.shape[1], w_lru_gates.shape[2]
    TAPS = conv_w.shape[1]
    HEADS = w_kvf.shape[1] - 2 * D
    HD = D // HEADS
    PAIRS = HEADS * HD // P
    QB = S // P
    RANGES = QB // 2
    UNITS = 2 * RANGES
    assert KT == 8 and S == 2 * BANK and LW == 2 * P and HD == 64 and FF % (2 * P) == 0

    V_MIX, V_FFN, V_KV, V_FINAL = 0, 2 * KT, 4 * KT, 5 * KT
    V_CONVB, V_LRU, V_CONVW, V_GATEB = 6 * KT, 7 * KT, 8 * KT, (8 + TAPS) * KT
    V_ALL = V_GATEB + BLOCKS * 2 * LW // P

    GATE_SLOT = 3
    pieces = Turns(4)
    pieces.plan("recA", [0, 1, 2, 0]).plan("recL", [1, 2, 0, 1, 2, 0], BLOCKS - 1, 1).plan("recE", [1, 2])
    pieces.plan("gates", [3], BLOCKS)
    for f in range(2):
        pieces.plan(f"ffn{f}A", [0, 1, 2, 0]).plan(f"ffn{f}L", [1, 2, 0, 1, 2, 0], GROUPS - 1, 1)
        pieces.plan(f"ffn{f}E", [1, 2])
        if f == 0:
            pieces.plan("forget", [3])
            pieces.plan("attA", [0, 1, 0, 0, 0]).plan("attL", [1, 0, 1, 1, 0, 1, 0, 0], (PAIRS - 2) // 2, 1, 2)
            pieces.plan("attZ", [1, 0]).plan("attE", [1])
    tiles = Turns(4)
    OUT_STAT = [0, 1, 2, 0, 1, 2, 0, 1, 3]
    tiles.plan("vec", [3]).plan("start", OUT_STAT)
    tiles.plan("recA", [0, 1, 2, 3] * 2).plan("recL", [0, 1, 2, 3] * 4, BLOCKS - 1, 1).plan("recE", OUT_STAT)
    for f in range(2):
        tiles.plan(f"ffn{f}A", [0, 1, 2, 3]).plan(f"ffn{f}L", [0, 1, 2, 3] * 3, GROUPS - 1, 1)
        tiles.plan(f"ffn{f}E", OUT_STAT)
        if f == 0:
            tiles.plan("forget", [3])
            tiles.plan("att", [0] + [1, 0] * QB + [2], PAIRS).plan("attE", OUT_STAT)
    tiles.plan("final", [0, 1, 2, 3] * 2)

    IN_FFN = [4 * BLOCKS, 4 * (BLOCKS + GROUPS)]
    OUT_FFN, OUT_ATT = [8 * BLOCKS, 8 * (BLOCKS + GROUPS + 1)], 8 * (BLOCKS + GROUPS)
    STAT = {"start": 0, "recE": 1, "ffn0E": 2, "attE": 3, "ffn1E": 4}
    LRU_STEPS, FORGET_STEPS = 16, 16
    T_PAIR = RANGES * (RANGES + 1)

    with ExitStack() as life:
        def sb(name, shape, dt, at=life):
            return at.enter_context(nc.sbuf_tensor(name, shape, dt))

        def sem(name):
            return life.enter_context(nc.semaphore(name))

        resid = sb("resid", [P, KT, S], F32)
        xh = sb("xh", [P, KT, S], F32R)
        xl = sb("xl", [P, KT, S], F32R)
        rstd = sb("rstd", [P, S], F32)
        raw = [sb(f"raw{s}", [P, 1024], F32) for s in range(2)]
        wh = [sb(f"wh{s}", [P, 1024], F32R) for s in range(2)]
        wl = [sb(f"wl{s}", [P, 1024], F32R) for s in range(2)]
        ident = sb("ident", [P, P], F32)
        ones = sb("ones", [P, P], F32)
        identb = sb("identb", [P, P], BF16)
        maskb = sb("maskb", [P, P], BF16)
        vec = sb("vec", [P, V_ALL], F32)
        lru = sb("lru", [P, 6, KT], F32)
        bforget = sb("bforget", [HEADS, 1], F32)
        negsel = sb("negsel", [P, HEADS], F32)

        with ExitStack() as att:
            kh = sb("kh", [P, 2, S], F32R, att)
            kl = sb("kl", [P, 2, S], F32R, att)
            qs = sb("qs", [P, 2, S], F32R, att)
            vs = sb("vs", [P, 2, QB, 2, HD], F32R, att)
            probs = [sb(f"probs{b}", [P, 2, S // (b + 1)], F32, att) for b in range(2)]
            pth = [sb(f"pth{b}", [P, BANK], F32R, att) for b in range(2)]
            ptl = [sb(f"ptl{b}", [P, BANK], F32R, att) for b in range(2)]
            oh = sb("oh", [P, S], F32R, att)
            ol = sb("ol", [P, S], F32R, att)
            kv_tmp = sb("kv_tmp", [P, S], F32, att)
            q_tmp = sb("q_tmp", [P, S], F32, att)
            o_tmp = sb("o_tmp", [P, S], F32, att)
            c2 = sb("c2", [P, S], F32R, att)
            sel = sb("sel", [P, 2, P], F32R, att)
            o_low = [sb(f"o_low{b}", [HD, 2 * P], F32, att) for b in range(2)]
            nmax = sb("nmax", [P, 2 * QB], F32, att)
            rsum = sb("rsum", [P, 2 * QB], F32, att)
            rinv = sb("rinv", [P, 2 * QB], F32, att)

        raw += [sb(f"raw{s}", [P, 1024], F32) for s in (2, 3)]
        wh += [sb(f"wh{s}", [P, 1024], F32R) for s in (2, 3)]
        wl += [sb(f"wl{s}", [P, 1024], F32R) for s in (2, 3)]
        tmp = [sb(f"tmp{b}", [P, S], F32) for b in range(4)]
        with ExitStack() as load:
            vrow = sb("vrow", [V_ALL, P], F32, load)
            xin = sb("xin", [P, QB, D], F32, load)
        with ExitStack() as rec:
            gelu = sb("gelu", [P, 2, S], F32, rec)
            ch = sb("ch", [P, 2, S], F32R, rec)
            cl = sb("cl", [P, 2, S], F32R, rec)
            yh = sb("yh", [P, 2, S], F32R, rec)
            yl = sb("yl", [P, 2, S], F32R, rec)
        hh = sb("hh", [P, 2, S], F32R)
        hl = sb("hl", [P, 2, S], F32R)

        ps = [life.enter_context(nc.psum_tensor(f"ps{s}", [P, S], F32)) for s in range(4)]
        t_ps = [ps[2][:, b * BANK:(b + 1) * BANK] for b in range(2)]
        o_ps = ps[3][:, 0:2 * P]
        f_ps = ps[3][:, BANK:2 * BANK]

        vec_loaded = sem("vec_loaded")
        bforget_loaded = sem("bforget_loaded")
        x_loaded = sem("x_loaded")
        loaded = [sem(f"loaded{s}") for s in range(4)]
        hi_ready = [sem(f"hi_ready{s}") for s in range(4)]
        lo_ready = [sem(f"lo_ready{s}") for s in range(4)]
        drained = [sem(f"drained{s}") for s in range(4)]
        const_ready = sem("const_ready")
        const_zero = sem("const_zero")
        vec_filled = sem("vec_filled")
        vec_ready = sem("vec_ready")
        lru_step = sem("lru_step")
        xt_filled = sem("xt_filled")
        in_filled = sem("in_filled")
        gates_filled = sem("gates_filled")
        kq_filled = sem("kq_filled")
        v_filled = sem("v_filled")
        w_filled = sem("w_filled")
        f_drained = sem("f_drained")
        out_filled = sem("out_filled")
        stat_filled = sem("stat_filled")
        xh_ready = sem("xh_ready")
        sq_ready = sem("sq_ready")
        sq_used = sem("sq_used")
        xl_ready = sem("xl_ready")
        root_ready = sem("root_ready")
        rstd_ready = sem("rstd_ready")
        conv_step = sem("conv_step")
        conv_ready = sem("conv_ready")
        ch_ready = sem("ch_ready")
        cl_ready = sem("cl_ready")
        gelu_ready = sem("gelu_ready")
        sig_ready = sem("sig_ready")
        lru_act = sem("lru_act")
        lru_dve = sem("lru_dve")
        y_ready = sem("y_ready")
        yh_ready = sem("yh_ready")
        yl_ready = sem("yl_ready")
        silu_ready = sem("silu_ready")
        h_ready = sem("h_ready")
        hh_ready = sem("hh_ready")
        hl_ready = sem("hl_ready")
        forget_filled = sem("forget_filled")
        forget_dve = sem("forget_dve")
        forget_act = sem("forget_act")
        c_ready = sem("c_ready")
        vt_filled = sem("vt_filled")
        s_filled = sem("s_filled")
        t_filled = sem("t_filled")
        o_filled = sem("o_filled")
        kh_ready = sem("kh_ready")
        kl_ready = sem("kl_ready")
        kdup_ready = sem("kdup_ready")
        qh_ready = sem("qh_ready")
        ql_ready = sem("ql_ready")
        vh_ready = sem("vh_ready")
        sel_ready = sem("sel_ready")
        nmax_ready = sem("nmax_ready")
        rinv_ready = sem("rinv_ready")
        p_ready = sem("p_ready")
        pth_ready = sem("pth_ready")
        ptl_ready = sem("ptl_ready")
        pt_used = sem("pt_used")
        o_low_ready = sem("o_low_ready")
        o_added = sem("o_added")
        oh_ready = sem("oh_ready")
        ol_ready = sem("ol_ready")
        y_final = sem("y_final")
        rows_filled = sem("rows_filled")
        rows_ready = sem("rows_ready")
        rows_stored = [sem(f"rows_stored{b}") for b in range(4)]

        def cols(w, c0):
            return w[:, bass.ds(c0, P)].rearrange("(k p) n -> p k n", p=P)

        def rows(w, r0, c0, n):
            return w[bass.ds(r0, 2 * P), c0:c0 + n].rearrange("(k p) n -> p k n", p=P)

        def rec_piece(j, first):
            if j < 2:
                return cols(w_rec_in[0], first + (D + j * P))
            return cols(w_rec_in[0], first + (j - 2) * P)

        def rec_out_piece(j, first):
            return rows(w_rec_out[0], first, j * BANK, BANK)

        def ffn_piece(f, kind, g):
            what, j = kind[0], int(kind[1])
            if what == "O":
                return rows(w_ffn_out[f], g * (2 * P), j * BANK, BANK)
            return cols(w_ffn_in[f], g * (2 * P) + (j * P + (FF if what == "U" else 0)))

        def att_piece(kind, i):
            if kind == "O":
                return w_o[0][bass.ds(i * P, P), :]
            return cols(w_q[0] if kind == "Q" else w_kvf, i * P + (D if kind == "V" else 0))

        def sq(seg, k):
            if seg == "attE":
                return (kv_tmp, q_tmp)[k % 2][:, :]
            return tmp[k % 2][:, :]

        GAIN = {"rec": V_MIX, "ffn0": V_FFN, "ffn1": V_FFN + KT, "K": V_KV, "V": V_KV, "Q": V_MIX + KT}

        def rec_free(j, b):
            first = isinstance(b, int) and b == 1
            return [(in_filled, 2) if first else (out_filled, b * 8 - 12),
                    (in_filled, 3) if first else (out_filled, b * 8 - 8),
                    (in_filled, b * 4), (in_filled, b * 4 + 1), (in_filled, b * 4 + 2), (in_filled, b * 4 + 3)][j]

        def ffn_free(f, j, g):
            i0, o0 = IN_FFN[f], OUT_FFN[f]
            return [(in_filled, g * 4 + (i0 - 2)), (in_filled, g * 4 + (i0 - 1)), (in_filled, g * 4 + i0),
                    (in_filled, g * 4 + (i0 + 1)), (out_filled, g * 8 + (o0 - 4)), (out_filled, g * 8 + o0)][j]

        def att_free(kind, i):
            return {"V": (w_filled, i * 16 - 16), "O": (kq_filled, i * 4 + 4),
                    "K": (v_filled, i + 1), "Q": (kq_filled, i * 4 + 6)}[kind]

        FFN_START = [
            [(out_filled, 8 * (BLOCKS - 1)), (out_filled, 8 * BLOCKS - 4), (out_filled, 8 * BLOCKS),
             (in_filled, IN_FFN[0] + 1)],
            [(w_filled, 16 * (PAIRS - 1)), (out_filled, OUT_FFN[1]), (out_filled, OUT_FFN[1]),
             (in_filled, IN_FFN[1] + 1)]]
        FFN_END = [[(in_filled, IN_FFN[f] + 4 * GROUPS - 2), (in_filled, IN_FFN[f] + 4 * GROUPS - 1)] for f in range(2)]
        REC_END = [(out_filled, 8 * (BLOCKS - 1) - 4), (out_filled, 8 * (BLOCKS - 1))]
        ATT_START = [(in_filled, IN_FFN[1]), (out_filled, OUT_ATT - 4)]

        def att_uses(i, loop=None, d=0):
            if loop is None and d == 0:
                return {"V": pieces.use("attA", 2), "K": pieces.use("attA", 3), "Q": pieces.use("attA", 4),
                        "nextV": pieces.use("attL", 0, 1), "nextO": pieces.use("attL", 1, 1)}
            if loop is None:
                return {"V": pieces.use("attZ", 0), "O": pieces.use("attZ", 1), "nextO": pieces.use("attE", 0)}
            at, nxt = 4 * d, (4, loop) if d == 0 else (0, loop + 2)
            return {"V": pieces.use("attL", at, loop), "O": pieces.use("attL", at + 1, loop),
                    "K": pieces.use("attL", at + 2, loop), "Q": pieces.use("attL", at + 3, loop),
                    "nextV": pieces.use("attL", *nxt), "nextO": pieces.use("attL", nxt[0] + 1, nxt[1])}

        def gate_tile(seg, t):
            return 2 + t if seg == "recA" else (2, 11)[t]

        def range_of(u):
            return RANGE_ORDER[u % RANGES]

        def s_tile(i, u, half):
            return tiles.use("att", 1 + 2 * u + half, i)

        def f_before(i):
            return i * 20 - 12 if not isinstance(i, int) or i > 0 else 4

        def kq_count(i, j, half):
            return i * 4 + (2 * j + half + 1)

        def tiles_before(u):
            return sum(range_of(v) + 1 for v in range(u))

        def pt_used_at(i, t):
            u = max(v for v in range(UNITS) if tiles_before(v) <= t)
            if t - tiles_before(u) == range_of(u):
                return o_filled, i * UNITS + (u + 1)
            return pt_used, i * (T_PAIR - UNITS) + (t + 1 - u)

        block = life.enter_context(nc.Block())

        @block.sync
        def _(sp):
            def load(use, src, k=KT, wait=True):
                slot, n = use
                if wait:
                    sp.wait_ge(lo_ready[slot], n - 1)
                dst = raw[slot][:, :] if k == 1 else raw[slot][:, :].rearrange("p (k n) -> p k n", k=k)
                sp.dma_start(dst, src).then_inc(loaded[slot], 16)

            for first, v in ((V_MIX, norm_mix.rearrange("l (k p) -> (l k) p", p=P)),
                             (V_FFN, norm_ffn.rearrange("l (k p) -> (l k) p", p=P)),
                             (V_KV, norm_kv.rearrange("(k p) -> k p", p=P)),
                             (V_FINAL, norm_final.rearrange("(k p) -> k p", p=P)),
                             (V_CONVB, conv_b[0].rearrange("(k p) -> k p", p=P)),
                             (V_LRU, lru_param[0].rearrange("(k p) -> k p", p=P)),
                             (V_CONVW, conv_w[0].rearrange("t (k p) -> (t k) p", p=P)),
                             (V_GATEB, b_lru_gates[0].rearrange("b (m p) -> (b m) p", p=P))):
                sp.dma_start(vrow[first:first + v.shape[0], :], v).then_inc(vec_loaded, 16)
            for b in range(QB):
                sp.dma_start(xin[:, b, :], x[0, b * P:(b + 1) * P, :]).then_inc(x_loaded, 16)
            sp.dma_start(bforget[:, :], b_forget.rearrange("(h a) -> h a", a=1)).then_inc(bforget_loaded, 16)

            for j in range(4):
                load(pieces.use("recA", j), rec_piece(j, 0))
            load(pieces.use("gates", 0, 0), w_lru_gates[0, 0].rearrange("(k p) n -> p k n", p=P), 2)
            with sp.Fori(1, BLOCKS) as b:
                first = b * LW
                slot, n = pieces.use("recL", 2, b)
                for j in range(3):
                    if j == 1:
                        sp.wait_ge(lo_ready[slot], n - 1)
                    load(pieces.use("recL", j, b), rec_piece(j, first), wait=(j != 2))
                for j in range(2):
                    load(pieces.use("recL", 3 + j, b), rec_out_piece(j, first - LW), 2)
                load(pieces.use("recL", 5, b), rec_piece(3, first))
                load(pieces.use("gates", 0, b), w_lru_gates[0, bass.ds(b, 1)].rearrange("b (k p) n -> p (b k) n", p=P), 2)
            for j in range(2):
                load(pieces.use("recE", j), rec_out_piece(j, (BLOCKS - 1) * LW), 2)

            def load_ffn(f):
                for j, kind in enumerate(("G0", "U0", "G1", "U1")):
                    if f == 1 and j == 2:
                        sp.wait_ge(out_filled, OUT_FFN[1])
                    load(pieces.use(f"ffn{f}A", j), ffn_piece(f, kind, 0))
                with sp.Fori(1, GROUPS) as g:
                    for j, kind in enumerate(("G0", "O0", "O1", "U0", "G1", "U1")):
                        is_out = kind[0] == "O"
                        load(pieces.use(f"ffn{f}L", j, g), ffn_piece(f, kind, g - 1 if is_out else g),
                             2 if is_out else KT)
                for j, kind in enumerate(("O0", "O1")):
                    load(pieces.use(f"ffn{f}E", j), ffn_piece(f, kind, GROUPS - 1), 2)

            load_ffn(0)

            slot, n = pieces.use("forget", 0)
            sp.wait_ge(forget_dve, 1)
            sp.dma_start(raw[slot][:, :].rearrange("p (k n) -> p k n", k=KT)[:, :, 0:HEADS],
                         w_kvf[:, 2 * D:].rearrange("(k p) n -> p k n", p=P)).then_inc(loaded[slot], 16)
            for j, (kind, i) in enumerate((("K", 0), ("Q", 0), ("V", 0), ("K", 1), ("Q", 1))):
                load(pieces.use("attA", j), att_piece(kind, i))
            with sp.Fori(1, PAIRS - 2, 2) as i:
                for d in range(2):
                    for j, (kind, ahead) in enumerate((("V", 0), ("O", -1), ("K", 1), ("Q", 1))):
                        load(pieces.use("attL", 4 * d + j, i), att_piece(kind, i + (d + ahead)), 1 if kind == "O" else KT)
            load(pieces.use("attZ", 0), att_piece("V", PAIRS - 1))
            load(pieces.use("attZ", 1), att_piece("O", PAIRS - 2), 1)
            load(pieces.use("attE", 0), att_piece("O", PAIRS - 1), 1)

            load_ffn(1)

            for b in range(QB):
                sp.wait_ge(rows_ready, b + 1)
                sp.dma_start(out[0, b * P:(b + 1) * P, :], tmp[b % 4][:, :]).then_inc(rows_stored[b % 4], 16)
            for b in range(4):
                sp.wait_ge(rows_stored[b], 16 * (QB // 4))

        @block.gpsimd
        def _(pool):
            pool.memset(ident[:, :], 0.0)
            pool.memset(ones[:, :], 1.0)
            pool.memset(identb[:, :], 0.0)
            pool.memset(maskb[:, :], 0.0)
            pool.memset(negsel[:, :], 0.0).then_inc(const_zero, 1)
            pool.wait_ge(const_zero, 1)
            for m in (ident, identb):
                pool.affine_select(out=m[:, :], in_=m[:, :], compare_op=ALU.not_equal, fill=1.0, base=0,
                                   pattern=[[-1, P]], channel_multiplier=1)
            pool.affine_select(out=maskb[:, :], in_=maskb[:, :], compare_op=ALU.is_ge, fill=NEG, base=0,
                               pattern=[[-1, P]], channel_multiplier=1)
            pool.affine_select(out=negsel[:, :], in_=negsel[:, :], compare_op=ALU.not_equal, fill=-1.0, base=0,
                               pattern=[[-1, HEADS]], channel_multiplier=1).then_inc(const_zero, 1)
            pool.wait_ge(const_zero, 2)
            pool.affine_select(out=negsel[:, :], in_=negsel[:, :], compare_op=ALU.not_equal, fill=-1.0, base=-32,
                               pattern=[[-1, HEADS]], channel_multiplier=1).then_inc(const_ready, 1)

            def low_k(i):
                pool.wait_ge(kh_ready, i + 1)
                for j in range(2):
                    mine = slice(j * HD, (j + 1) * HD)
                    pool.wait_ge(*((ol_ready, i) if j == 0 else (kl_ready, i * 2 + 1)))
                    pool.tensor_tensor(kl[mine, j, :], kv_tmp[mine, :], kh[mine, j, :].bitcast(F32),
                                       ALU.subtract).then_inc(kl_ready, 1)

            def low_o(i):
                pool.wait_ge(oh_ready, i + 1)
                pool.wait_ge(kl_ready, i * 2 + 2)
                pool.tensor_tensor(ol[:, :], o_tmp[:, :], oh[:, :].bitcast(F32), ALU.subtract).then_inc(ol_ready, 1)

            low_k(0)
            with pool.Fori(1, PAIRS) as i:
                low_o(i - 1)
                low_k(i)
            low_o(PAIRS - 1)

        @block.tensor
        def _(pe):
            halves = [slice(0, BANK), slice(BANK, S)]

            def claim(use):
                slot, n = use
                pe.wait_ge(drained[slot], n - 1)
                return ps[slot]

            def split_product(acc, terms):
                last = None
                for k, (w_hi, w_lo, x_hi, x_lo) in enumerate(terms):
                    for p, (w, v) in enumerate(((w_hi, x_hi), (w_hi, x_lo), (w_lo, x_hi))):
                        for h in halves:
                            last = pe.matmul(acc[:, h], w, v[:, h], start=(k == 0 and p == 0),
                                             stop=(k == len(terms) - 1 and p == 2))
                return last

            def stationary(slot, k, n, width):
                at = k * width + n * P
                return wh[slot][:, at:at + P], wl[slot][:, at:at + P]

            def in_tile(piece, tile):
                slot, n = piece
                acc = claim(tile)
                pe.wait_ge(lo_ready[slot], n)
                split_product(acc, [(*stationary(slot, k, 0, P), xh[:, k, :], xl[:, k, :])
                                    for k in range(KT)]).then_inc(in_filled, 1)

            def out_tiles(piece, tile_uses, hi, lo):
                slot, n = piece
                for m, tile in enumerate(tile_uses):
                    acc = claim(tile)
                    if m == 0:
                        pe.wait_ge(lo_ready[slot], n)
                    split_product(acc, [(*stationary(slot, k, m, BANK), hi[:, k, :], lo[:, k, :])
                                        for k in range(2)]).then_inc(out_filled, 1)

            def stat(seg, k):
                if k == 0:
                    claim(tiles.use(seg, 8))
                pe.wait_ge(sq_ready, STAT[seg] * KT + k + 1)
                for h in halves:
                    last = pe.matmul(ps[3][:, h], ones[:, :], sq(seg, k)[:, h], start=(k == 0), stop=(k == KT - 1))
                last.then_inc(stat_filled if k == KT - 1 else sq_used, 1)

            def out_and_stat(seg, tile_of):
                for m in range(KT):
                    tile_of(m)
                    if m >= 2:
                        stat(seg, m - 2)
                stat(seg, KT - 2)
                stat(seg, KT - 1)
                if seg != "ffn1E":
                    pe.wait_ge(xl_ready, (STAT[seg] + 1) * KT)

            def out_epilogue(seg, piece_seg, hi, lo):
                def tile_of(m):
                    slot, n = pieces.use(piece_seg, m // 4)
                    acc = claim(tiles.use(seg, m))
                    pe.wait_ge(lo_ready[slot], n)
                    split_product(acc, [(*stationary(slot, k, m % 4, BANK), hi[:, k, :], lo[:, k, :])
                                        for k in range(2)]).then_inc(out_filled, 1)
                out_and_stat(seg, tile_of)

            pe.wait_ge(const_ready, 1)
            pe.wait_ge(vec_loaded, 16 * 8)
            claim(tiles.use("vec", 0))
            pe.transpose(ps[3][:, 0:V_ALL], vrow[:, :], ident[0:V_ALL, 0:V_ALL]).then_inc(vec_filled, 1)
            pe.wait_ge(x_loaded, 16 * QB)

            def x_tile(m):
                acc = claim(tiles.use("start", m))
                for b in range(QB):
                    last = pe.transpose(acc[:, b * P:(b + 1) * P], xin[:, b, m * P:(m + 1) * P], ident[:, :])
                last.then_inc(xt_filled, 1)
            out_and_stat("start", x_tile)


            def rec_gates(seg, b, first):
                slot, n = pieces.use("gates", 0, b)
                pe.wait_ge(lo_ready[slot], n)
                pe.wait_ge(cl_ready, 2 * b + 2)
                for j, m in enumerate((2, 0, 3, 1)):
                    acc = claim(tiles.use(seg, first + j, b))
                    split_product(acc, [(*stationary(slot, k, m, BANK), ch[:, k, :], cl[:, k, :])
                                        for k in range(2)]).then_inc(gates_filled, 1)

            for j in range(4):
                in_tile(pieces.use("recA", j), tiles.use("recA", j))
            rec_gates("recA", 0, 4)
            with pe.Fori(1, BLOCKS) as b:
                for j in range(3):
                    in_tile(pieces.use("recL", j, b), tiles.use("recL", j, b))
                pe.wait_ge(yl_ready, 2 * b)
                for j in range(2):
                    out_tiles(pieces.use("recL", 3 + j, b),
                              [tiles.use("recL", 3 + 4 * j + m, b) for m in range(4)], yh, yl)
                in_tile(pieces.use("recL", 5, b), tiles.use("recL", 11, b))
                rec_gates("recL", b, 12)
            pe.wait_ge(yl_ready, 2 * BLOCKS)
            out_epilogue("recE", "recE", yh, yl)

            def ffn(f):
                def step(seg, j, t, g):
                    in_tile(pieces.use(seg, j, g), tiles.use(seg, t, g))
                for j in range(4):
                    step(f"ffn{f}A", j, j, 0)
                with pe.Fori(1, GROUPS) as g:
                    seg = f"ffn{f}L"
                    step(seg, 0, 0, g)
                    pe.wait_ge(hl_ready, g * 2 + 2 * f * GROUPS)
                    for j in range(2):
                        out_tiles(pieces.use(seg, 1 + j, g),
                                  [tiles.use(seg, 1 + 4 * j + m, g) for m in range(4)], hh, hl)
                    for j in range(3):
                        step(seg, 3 + j, 9 + j, g)
                pe.wait_ge(hl_ready, (f + 1) * 2 * GROUPS)
                out_epilogue(f"ffn{f}E", f"ffn{f}E", hh, hl)

            ffn(0)

            slot, n = pieces.use("forget", 0)
            acc = claim(tiles.use("forget", 0))
            pe.wait_ge(lo_ready[slot], n)
            split_product(acc, [(*stationary(slot, k, 0, P), xh[:, k, :], xl[:, k, :])
                                for k in range(KT)]).then_inc(forget_filled, 1)

            def projection_part(piece, half, k):
                slot, n = piece
                if k == 0:
                    pe.wait_ge(lo_ready[slot], n)
                w_hi, w_lo = stationary(slot, k, 0, P)
                h = halves[half]
                for p, (w, v) in enumerate(((w_hi, xh), (w_hi, xl), (w_lo, xh))):
                    last = pe.matmul(f_ps, w, v[:, k, h], start=(k == 0 and p == 0), stop=(k == KT - 1 and p == 2))
                if k == KT - 1:
                    last.then_inc(kq_filled, 1)

            def output_part(piece, m, half):
                slot, _ = piece
                w_hi, w_lo = stationary(slot, 0, m, BANK)
                h = halves[half]
                for p, (w, v) in enumerate(((w_hi, oh), (w_hi, ol), (w_lo, oh))):
                    last = pe.matmul(f_ps, w, v[:, h], start=(p == 0), stop=(p == 2))
                last.then_inc(w_filled, 1)

            def scores(i, u, half):
                j, n = u // RANGES, 2 * range_of(u) + half
                acc = claim(s_tile(i, u, half))
                w = (n + 1) * P
                for c0 in range(0, w, BANK):
                    c1 = min(w, c0 + BANK)
                    pe.matmul(acc[:, c0:c1], sel[:, j, :], c2[:, c0:c1], start=True, stop=False)
                    if c1 == w:
                        pe.matmul(acc[:, w - P:w], identb[:, :], maskb[:, :], start=False, stop=False)
                    q = qs[:, j, n * P:(n + 1) * P]
                    pe.matmul(acc[:, c0:c1], q, kh[:, j, c0:c1], start=False, stop=False)
                    last = pe.matmul(acc[:, c0:c1], q, kl[:, j, c0:c1], start=False, stop=True)
                last.then_inc(s_filled, 1)

            def blocks_of(r, m):
                if m < r:
                    return [(2 * m, 0, 0), (2 * m + 1, 0, 2 * P)]
                return [(2 * m, 0, 0), (2 * m + 1, 1, 2 * P)]

            def transposes(i, u, m):
                t = tiles_before(u) + m
                if m == 0:
                    pe.wait_ge(p_ready, i * 2 * QB + 2 * (u + 1))
                if t == 0:
                    slot, n = tiles.use("att", 1 + 2 * QB, i)
                    pe.wait_ge(drained[slot], n)
                if t >= 2:
                    pe.wait_ge(ptl_ready, i * T_PAIR + (t - 1))
                for kb, q0, col in blocks_of(range_of(u), m):
                    for q in range(q0, 2):
                        last = pe.transpose(t_ps[t % 2][:, col + (q - q0) * P:col + (q - q0 + 1) * P],
                                            probs[u % 2][:, q, kb * P:(kb + 1) * P], ident[:, :])
                last.then_inc(t_filled, 1)

            def values(i, u, m):
                j, r, t = u // RANGES, range_of(u), tiles_before(u) + m
                if m == 0:
                    pe.wait_ge(o_added, i * UNITS + u)
                pe.wait_ge(ptl_ready, i * T_PAIR + (t + 1))
                for kb, q0, col in blocks_of(r, m):
                    v = vs[:, j, kb, :, :].rearrange("p a d -> p (a d)")
                    n = (2 - q0) * P
                    for pt in (pth, ptl):
                        last = pe.matmul(o_ps[:, q0 * P:2 * P], v, pt[t % 2][:, col:col + n],
                                         start=(kb == 0 and pt is pth), stop=(kb == 2 * r + 1 and pt is ptl))
                last.then_inc(o_filled if m == r else pt_used, 1)

            def pair(i, uses, with_w=True, with_p=True):
                w = p = f = 0
                for u, step in pair_steps(with_w, with_p):
                    m = int(step[1]) if len(step) > 1 else 0
                    if step == "V":
                        acc = claim(tiles.use("att", 0, i))
                        slot, n = uses["V"]
                        pe.wait_ge(lo_ready[slot], n)
                        split_product(acc, [(*stationary(slot, k, 0, P), xh[:, k, :], xl[:, k, :])
                                            for k in range(KT)]).then_inc(v_filled, 1)
                        pe.wait_ge(kdup_ready, i * 4 + 4)
                        pe.wait_ge(ql_ready, i * 2 + 2)
                        pe.wait_ge(sel_ready, i * 2 + 2)
                    elif step == "X":
                        acc = claim(tiles.use("att", 1 + 2 * QB, i))
                        pe.wait_ge(ptl_ready, i * T_PAIR)
                        slot, n = tiles.use("att", 0, i)
                        pe.wait_ge(drained[slot], n)
                        for b in range(QB):
                            last = pe.transpose(acc[:, b * P:(b + 1) * P], kv_tmp[:, b * P:(b + 1) * P], ident[:, :])
                        last.then_inc(vt_filled, 1)
                    elif step[0] == "S":
                        scores(i, u + 1, m)
                    elif step[0] == "T":
                        transposes(i, u, m)
                    elif step[0] == "V":
                        values(i, u, m)
                    elif step == "w":
                        if w == 0:
                            slot, n = uses["O"]
                            pe.wait_ge(lo_ready[slot], n)
                            pe.wait_ge(ol_ready, i)
                        pe.wait_ge(f_drained, f_before(i) + f)
                        output_part(uses["O"], w // 2, w % 2)
                        w, f = w + 1, f + 1
                    elif step == "p":
                        if p % KT == 0:
                            pe.wait_ge(f_drained, f_before(i) + f)
                            f += 1
                        projection_part(uses["K" if p < 2 * KT else "Q"], p // KT % 2, p % KT)
                        p += 1

            def wo_tile(piece, tile, m):
                slot, n = piece
                acc = claim(tile)
                pe.wait_ge(lo_ready[slot], n)
                split_product(acc, [(wh[slot][:, m * P:(m + 1) * P], wl[slot][:, m * P:(m + 1) * P],
                                     oh[:, :], ol[:, :])]).then_inc(out_filled, 1)

            pe.wait_ge(drained[3], tiles.use("forget", 0)[1])
            for j in range(2):
                for half in range(2):
                    pe.wait_ge(f_drained, 2 * j + half)
                    for k in range(KT):
                        projection_part(pieces.use("attA", j), half, k)
            pe.wait_ge(c_ready, 2)
            pair(0, att_uses(0), with_w=False)
            with pe.Fori(1, PAIRS - 2, 2) as i:
                for d in range(2):
                    pair(i + d, att_uses(i + d, i, d))
            pair(PAIRS - 1, att_uses(PAIRS - 1, None, 1), with_p=False)
            pe.wait_ge(ol_ready, PAIRS)
            pe.wait_ge(ptl_ready, PAIRS * T_PAIR)
            pe.wait_ge(o_added, PAIRS * UNITS)
            pe.wait_ge(f_drained, f_before(PAIRS - 1) + 16)
            out_and_stat("attE", lambda m: wo_tile(pieces.use("attE", 0), tiles.use("attE", m), m))

            ffn(1)

            pe.wait_ge(y_final, KT)
            for b in range(QB):
                if b < 4:
                    acc = claim(tiles.use("final", b))
                else:
                    pe.wait_ge(rows_ready, b - 3)
                    acc = ps[b % 4]
                for k in range(KT):
                    last = pe.transpose(acc[:, k * P:(k + 1) * P], resid[:, k, b * P:(b + 1) * P], ident[:, :])
                last.then_inc(rows_filled, 1)

        @block.scalar
        def _(act):
            def split_hi(use, free, gain=None, k0=0, k1=KT):
                slot, n = use
                if k0 == 0:
                    act.wait_ge(loaded[slot], n * 16)
                    if free is not None:
                        act.wait_ge(*free)
                if gain is None:
                    act.activation(wh[slot][:, :], raw[slot][:, :], ACT.Copy).then_inc(hi_ready[slot], 1)
                    return
                for k in range(k0, k1):
                    last = act.activation(wh[slot][:, k * P:(k + 1) * P], raw[slot][:, k * P:(k + 1) * P],
                                          ACT.Copy, scale=vec[:, gain + k:gain + k + 1])
                if k1 == KT:
                    last.then_inc(hi_ready[slot], 1)

            def halves_of_resid(seg, k):
                slot, t = tiles.use(seg, k)
                act.wait_ge(drained[slot], t)
                if seg != "ffn1E":
                    act.activation(xh[:, k, :], resid[:, k, :], ACT.Copy).then_inc(xh_ready, 1)
                if k >= 2:
                    act.wait_ge(sq_used, STAT[seg] * (KT - 1) + k - 1)
                act.activation(sq(seg, k), resid[:, k, :], ACT.Square).then_inc(sq_ready, 1)

            def root(seg):
                slot, n = tiles.use(seg, 8)
                act.wait_ge(drained[slot], n)
                act.activation(rstd[:, :], rstd[:, :], ACT.Sqrt).then_inc(root_ready, 1)

            act.wait_ge(lru_step, 1)
            act.activation(lru[:, 1, :], lru[:, 0, :], ACT.Exp).then_inc(lru_step, 1)
            act.wait_ge(lru_step, 3)
            act.activation(lru[:, 3, :], lru[:, 2, :], ACT.Ln).then_inc(lru_step, 1)

            for k in range(KT):
                halves_of_resid("start", k)
            for j in range(2):
                split_hi(pieces.use("recA", j), None, GAIN["rec"])
            root("start")

            def conv_high(b, t):
                act.wait_ge(conv_ready, b * 2 + (t + 1))
                act.activation(ch[:, t, :], tmp[1 + 2 * t][:, :], ACT.Copy).then_inc(ch_ready, 1)

            def gate_gelu(seg, b, t):
                slot, n = tiles.use(seg, gate_tile(seg, t), b)
                act.wait_ge(drained[slot], n)
                act.activation(gelu[:, t, :], gelu[:, t, :], ACT.Gelu_apprx_tanh).then_inc(gelu_ready, 1)

            def lru_gates(seg, first, b, t):
                bias = V_GATEB
                r_slot, _ = tiles.use(seg, first + 2 * t, b)
                i_slot, _ = tiles.use(seg, first + 2 * t + 1, b)
                act.wait_ge(gates_filled, b * 4 + (2 * t + 1))
                if t == 1:
                    act.wait_ge(yh_ready, b * 2 + 1)
                    act.wait_ge(yl_ready, b * 2 + 1)
                else:
                    act.wait_ge(cl_ready, b * 2 + 2)
                act.activation(tmp[0][:, :], ps[r_slot][:, :], ACT.Sigmoid,
                               bias=vec[:, bass.ds(b * 4 + (bias + 2 + t), 1)]).then_inc(drained[r_slot], 1)
                act.wait_ge(gates_filled, b * 4 + (2 * t + 2))
                act.activation(tmp[2][:, :], ps[i_slot][:, :], ACT.Sigmoid,
                               bias=vec[:, bass.ds(b * 4 + (bias + t), 1)]).then_inc(drained[i_slot], 1)
                act.wait_ge(drained[r_slot], tiles.use(seg, first + 2 * t, b)[1])
                act.activation(tmp[1][:, :], tmp[0][:, :], ACT.Tanh,
                               scale=lru[:, 0, bass.ds(b * 2 + t, 1)]).then_inc(lru_act, 1)
                act.wait_ge(lru_act, b * 6 + (3 * t + 1))
                act.activation(tmp[0][:, :], tmp[0][:, :], ACT.Exp,
                               scale=lru[:, 1, bass.ds(b * 2 + t, 1)]).then_inc(lru_act, 1)
                act.activation(tmp[1][:, :], tmp[1][:, :], ACT.Sqrt, bias=TINY).then_inc(lru_act, 1)

            def y_high(b, t):
                act.wait_ge(y_ready, b * 2 + (t + 1))
                act.activation(yh[:, t, :], tmp[2][:, :], ACT.Copy).then_inc(yh_ready, 1)

            g = GAIN["rec"]
            act.wait_ge(lru_step, LRU_STEPS)
            split_hi(pieces.use("recA", 2), None, g)
            conv_high(0, 0)
            split_hi(pieces.use("recA", 3), (in_filled, 1), g)
            conv_high(0, 1)

            def rec_gates(seg, first, b, last):
                for j in range(2 if last else 3):
                    if last:
                        split_hi(pieces.use("recE", j), REC_END[j])
                    else:
                        split_hi(pieces.use("recL", j, b + 1), rec_free(j, b + 1), g)
                lru_gates(seg, first, b, 0)
                y_high(b, 0)
                if not last:
                    split_hi(pieces.use("recL", 3, b + 1), rec_free(3, b + 1))
                lru_gates(seg, first, b, 1)
                if not last:
                    split_hi(pieces.use("recL", 4, b + 1), rec_free(4, b + 1))
                y_high(b, 1)

            def rec_body(b, last):
                conv_high(b, 0)
                conv_high(b, 1)
                gate_gelu("recL", b, 0)
                split_hi(pieces.use("recL", 5, b), rec_free(5, b), g)
                split_hi(pieces.use("gates", 0, b), (gates_filled, b * 4))
                gate_gelu("recL", b, 1)
                rec_gates("recL", 12, b, last)

            for t in range(2):
                gate_gelu("recA", 0, t)
            split_hi(pieces.use("gates", 0, 0), None)
            rec_gates("recA", 4, 0, False)
            with act.Fori(1, BLOCKS - 1) as b:
                rec_body(b, False)
            rec_body(BLOCKS - 1, True)

            def epilogue(seg, nexts):
                nexts[0]()
                for k in range(KT):
                    halves_of_resid(seg, k)
                    if k == 4:
                        nexts[1]()
                root(seg)

            def ffn(f):
                g = GAIN[f"ffn{f}"]
                seg0, seg = f"ffn{f}A", f"ffn{f}L"

                def silu(sg, tile, grp, t):
                    slot, n = tiles.use(sg, tile, grp)
                    act.wait_ge(drained[slot], n)
                    act.activation(tmp[t][:, :], tmp[t][:, :], ACT.Silu).then_inc(silu_ready, 1)

                def h_high(grp, t):
                    act.wait_ge(h_ready, grp * 2 + (2 * f * GROUPS + t + 1))
                    act.activation(hh[:, t, :], tmp[2 + t][:, :], ACT.Copy).then_inc(hh_ready, 1)

                split_hi(pieces.use(seg0, 2), FFN_START[f][2], g)
                silu(seg0, 0, 0, 0)
                split_hi(pieces.use(seg0, 3), FFN_START[f][3], g)
                h_high(0, 0)
                split_hi(pieces.use(seg, 0, 1), ffn_free(f, 0, 1), g)
                silu(seg0, 2, 0, 1)
                split_hi(pieces.use(seg, 1, 1), ffn_free(f, 1, 1))
                h_high(0, 1)

                def body(grp, last):
                    split_hi(pieces.use(seg, 2, grp), ffn_free(f, 2, grp))
                    silu(seg, 0, grp, 0)
                    split_hi(pieces.use(seg, 3, grp), ffn_free(f, 3, grp), g)
                    split_hi(pieces.use(seg, 4, grp), ffn_free(f, 4, grp), g)
                    split_hi(pieces.use(seg, 5, grp), ffn_free(f, 5, grp), g)
                    h_high(grp, 0)
                    if last:
                        split_hi(pieces.use(f"ffn{f}E", 0), FFN_END[f][0])
                    else:
                        split_hi(pieces.use(seg, 0, grp + 1), ffn_free(f, 0, grp + 1), g)
                    silu(seg, 10, grp, 1)
                    if last:
                        split_hi(pieces.use(f"ffn{f}E", 1), FFN_END[f][1])
                    else:
                        split_hi(pieces.use(seg, 1, grp + 1), ffn_free(f, 1, grp + 1))
                    h_high(grp, 1)

                with act.Fori(1, GROUPS - 1) as grp:
                    body(grp, False)
                body(GROUPS - 1, True)

            epilogue("recE", [lambda: split_hi(pieces.use("ffn0A", 0), FFN_START[0][0], GAIN["ffn0"]),
                              lambda: split_hi(pieces.use("ffn0A", 1), FFN_START[0][1], GAIN["ffn0"])])
            ffn(0)

            epilogue("ffn0E", [lambda: split_hi(pieces.use("forget", 0), (gates_filled, 4 * BLOCKS), V_KV),
                               lambda: split_hi(pieces.use("attA", 0), ATT_START[0], V_KV)])
            split_hi(pieces.use("attA", 1), ATT_START[1], GAIN["Q"])
            act.wait_ge(forget_dve, 3)
            act.activation(o_tmp[0:HEADS, :], o_tmp[0:HEADS, :], ACT.Exp).then_inc(forget_act, 1)
            act.wait_ge(forget_dve, 4)
            act.activation(ps[1][0:HEADS, :], probs[0][0:HEADS, 0, :], ACT.Ln).then_inc(forget_act, 1)
            split_hi(pieces.use("attA", 2), (kq_filled, 2), V_KV)
            act.wait_ge(forget_dve, FORGET_STEPS)
            act.activation(c2[0:HEADS, :], o_tmp[0:HEADS, :], ACT.Copy).then_inc(c_ready, 1)

            def high_kq(i, static):
                act.wait_ge(s_filled, i * 2 * QB)
                act.wait_ge(f_drained, 2 if static else f_before(i))
                for j in range(2):
                    mine = slice(j * HD, (j + 1) * HD)
                    last = act.activation(kh[mine, j, :], kv_tmp[mine, :], ACT.Copy)
                last.then_inc(kh_ready, 1)
                act.wait_ge(kh_ready, i + 1)
                for j in range(2):
                    mine, other = slice(j * HD, (j + 1) * HD), slice((1 - j) * HD, (2 - j) * HD)
                    act.activation(kh[other, j, :], kh[mine, j, :].bitcast(F32), ACT.Copy).then_inc(kdup_ready, 1)
                if static:
                    act.wait_ge(f_drained, 4)
                for j in range(2):
                    mine = slice(j * HD, (j + 1) * HD)
                    act.activation(qs[mine, j, :], q_tmp[mine, :], ACT.Copy).then_inc(qh_ready, 1)
                for j in range(2):
                    mine, other = slice(j * HD, (j + 1) * HD), slice((1 - j) * HD, (2 - j) * HD)
                    act.wait_ge(kl_ready, i * 2 + (j + 1))
                    act.activation(kl[other, j, :], kl[mine, j, :].bitcast(F32), ACT.Copy).then_inc(kdup_ready, 1)

            def exponentials(i, u, half):
                n, w = 2 * u + half, (2 * range_of(u) + half + 1) * P
                slot, _ = s_tile(i, u, half)
                act.wait_ge(nmax_ready, i * 2 * QB + (n + 1))
                if u >= 2:
                    act.wait_ge(t_filled, i * T_PAIR + tiles_before(u - 1))
                act.activation(probs[u % 2][:, half, 0:w], ps[slot][:, 0:w], ACT.Exp,
                               bias=nmax[:, n:n + 1], accum_out=rsum[:, n:n + 1]).then_inc(drained[slot], 1)

            def pair(i, uses, with_w=True, with_p=True, static=False):
                high_kq(i, static)
                if with_w:
                    split_hi(uses["O"], att_free("O", i - 1))
                for u, step in pair_steps(False, False):
                    m = int(step[1]) if len(step) > 1 else 0
                    if step == "X":
                        act.wait_ge(vt_filled, i + 1)
                        slot, _ = tiles.use("att", 1 + 2 * QB, i)
                        src = ps[slot][:, :].rearrange("p (b j d) -> p j b d", b=QB, j=2)
                        act.activation(vs[:, 0, :, 0, :], src[:, 0], ACT.Copy)
                        act.activation(vs[:, 1, :, 0, :], src[:, 1], ACT.Copy).then_inc(vh_ready, 1)
                    elif step[0] == "S":
                        exponentials(i, u + 1, m)
                    elif step[0] == "T":
                        t = tiles_before(u) + m
                        width = 4 * P if m < range_of(u) else 3 * P
                        act.wait_ge(t_filled, i * T_PAIR + (t + 1))
                        if t >= 2:
                            act.wait_ge(*pt_used_at(i, t - 2))
                        act.activation(pth[t % 2][:, 0:width], t_ps[t % 2][:, 0:width], ACT.Copy).then_inc(pth_ready, 1)
                    elif step == "O":
                        act.wait_ge(o_filled, i * UNITS + u)
                        if u >= 3:
                            act.wait_ge(o_added, i * UNITS + (u - 2))
                        act.activation(o_low[(u - 1) % 2][:, :], o_ps[HD:P, :], ACT.Copy).then_inc(o_low_ready, 1)
                    if with_p and (u, step) in HI_AT:
                        kind, k0, k1 = HI_AT[u, step]
                        free = {"K": att_free("K", i), "Q": att_free("Q", i),
                                "nextV": (kq_filled, 4) if static else att_free("V", i + 1)}[kind]
                        split_hi(uses[kind], free, GAIN[kind[-1]], k0, k1)
                act.wait_ge(o_added, i * UNITS + UNITS)
                act.activation(oh[:, :], o_tmp[:, :], ACT.Copy).then_inc(oh_ready, 1)

            pair(0, att_uses(0), with_w=False, static=True)
            with act.Fori(1, PAIRS - 2, 2) as i:
                for d in range(2):
                    pair(i + d, att_uses(i + d, i, d))
            pair(PAIRS - 1, att_uses(PAIRS - 1, None, 1), with_p=False)
            split_hi(pieces.use("attE", 0), (v_filled, PAIRS))
            epilogue("attE", [lambda: split_hi(pieces.use("ffn1A", 0), FFN_START[1][0], GAIN["ffn1"]),
                              lambda: None])
            split_hi(pieces.use("ffn1A", 1), FFN_START[1][1], GAIN["ffn1"])
            ffn(1)
            for k in range(KT):
                halves_of_resid("ffn1E", k)
            root("ffn1E")
            for b in range(1, QB, 2):
                slot, n = tiles.use("final", b)
                act.wait_ge(rows_filled, b + 1)
                if b >= 4:
                    act.wait_ge(rows_stored[b % 4], 16)
                act.wait_ge(rows_ready, b)
                act.activation(tmp[b % 4][:, :], ps[slot][:, :], ACT.Copy).then_inc(rows_ready, 1)

        @block.vector
        def _(dve):
            def split_lo(use, gain=None, k0=0, k1=KT):
                slot, n = use
                if k0 == 0:
                    dve.wait_ge(hi_ready[slot], n)
                if gain is None:
                    dve.tensor_tensor(wl[slot][:, :], raw[slot][:, :], wh[slot][:, :].bitcast(F32),
                                      ALU.subtract).then_inc(lo_ready[slot], 1)
                    return
                for k in range(k0, k1):
                    c = slice(k * P, (k + 1) * P)
                    last = dve.scalar_tensor_tensor(out=wl[slot][:, c], in0=raw[slot][:, c],
                                                    scalar=vec[:, gain + k:gain + k + 1],
                                                    in1=wh[slot][:, c].bitcast(F32), op0=ALU.mult, op1=ALU.subtract)
                if k1 == KT:
                    last.then_inc(lo_ready[slot], 1)

            def low_half(seg, k):
                dve.wait_ge(xh_ready, STAT[seg] * KT + k + 1)
                dve.tensor_tensor(xl[:, k, :], resid[:, k, :], xh[:, k, :].bitcast(F32),
                                  ALU.subtract).then_inc(xl_ready, 1)

            def mean_square(seg):
                slot, _ = tiles.use(seg, 8)
                dve.wait_ge(stat_filled, STAT[seg] + 1)
                dve.tensor_scalar(rstd[:, :], ps[slot][:, :], 1.0 / D, EPS, ALU.mult, ALU.add).then_inc(drained[slot], 1)

            def inverse_root(seg):
                dve.wait_ge(root_ready, STAT[seg] + 1)
                dve.reciprocal(rstd[:, :], rstd[:, :]).then_inc(rstd_ready, 1)
                dve.wait_ge(rstd_ready, STAT[seg] + 1)

            def scaled(dst, tile, filled, count):
                slot, n = tile
                dve.wait_ge(filled, count)
                dve.tensor_tensor(dst, ps[slot][:, :], rstd[:, :], ALU.mult).then_inc(drained[slot], 1)

            def add_tile(tile, m, count):
                slot, _ = tile
                dve.wait_ge(out_filled, count)
                dve.tensor_tensor(resid[:, m, :], ps[slot][:, :], resid[:, m, :], ALU.add).then_inc(drained[slot], 1)

            dve.wait_ge(vec_filled, 1)
            dve.tensor_copy(vec[:, :], ps[3][:, 0:V_ALL]).then_inc(drained[3], 1)
            dve.wait_ge(drained[3], 1)
            lp = vec[:, V_LRU:V_LRU + KT]
            dve.scalar_tensor_tensor(out=lru[:, 0, :], in0=lp, scalar=-1.0, in1=lp, op0=ALU.mult,
                                     op1=ALU.min).then_inc(lru_step, 1)
            dve.wait_ge(lru_step, 2)
            steps = [2]

            def lru_next(ins, more=1):
                ins.then_inc(lru_step, 1)
                steps[0] += more
                dve.wait_ge(lru_step, steps[0])

            lru_next(dve.tensor_scalar(lru[:, 2, :], lru[:, 1, :], 1.0, None, ALU.add), 2)
            lru_next(dve.tensor_scalar(lru[:, 4, :], lru[:, 2, :], -1.0, None, ALU.add))
            lru_next(dve.tensor_scalar(lru[:, 5, :], lru[:, 4, :], 0.0, None, ALU.is_equal))
            lru_next(dve.tensor_tensor(lru[:, 4, :], lru[:, 4, :], lru[:, 5, :], ALU.add))
            lru_next(dve.reciprocal(lru[:, 4, :], lru[:, 4, :]))
            lru_next(dve.tensor_tensor(lru[:, 3, :], lru[:, 3, :], lru[:, 1, :], ALU.mult))
            lru_next(dve.tensor_tensor(lru[:, 3, :], lru[:, 3, :], lru[:, 4, :], ALU.mult))
            lru_next(dve.tensor_tensor(lru[:, 5, :], lru[:, 5, :], lru[:, 1, :], ALU.mult))
            lru_next(dve.tensor_tensor(lru[:, 3, :], lru[:, 3, :], lru[:, 5, :], ALU.add))
            lru_next(dve.tensor_scalar(lru[:, 2, :], lp, -1.0, 0.0, ALU.mult, ALU.max))
            lru_next(dve.tensor_tensor(lru[:, 3, :], lru[:, 3, :], lru[:, 2, :], ALU.add))
            lru_next(dve.tensor_scalar(lru[:, 0, :], lru[:, 3, :], LRU_C / 2, None, ALU.mult))
            lru_next(dve.tensor_scalar(lru[:, 1, :], lru[:, 3, :], -LRU_C, None, ALU.mult))
            assert steps[0] == LRU_STEPS, steps

            for k in range(KT):
                slot, _ = tiles.use("start", k)
                dve.wait_ge(xt_filled, k + 1)
                dve.tensor_copy(resid[:, k, :], ps[slot][:, :]).then_inc(drained[slot], 1)
                if k >= 1:
                    low_half("start", k - 1)
            low_half("start", KT - 1)
            mean_square("start")
            g = GAIN["rec"]
            for j in range(2):
                split_lo(pieces.use("recA", j), g)
            inverse_root("start")

            def conv_scaled(seg, b, t):
                slot, n = tiles.use(seg, t, b)
                return drained[slot], n

            def conv_in(seg, b, t):
                scaled(tmp[2 * t][:, :], tiles.use(seg, t, b), in_filled, b * 4 + (t + 1))

            def conv(seg, b, t):
                r, acc = tmp[2 * t], tmp[2 * t + 1]
                dve.wait_ge(*conv_scaled(seg, b, t))
                tap = lambda k: vec[:, bass.ds(b * 2 + (V_CONVW + (TAPS - 1 - k) * KT + t), 1)]
                dve.tensor_scalar(acc[:, :], r[:, :], tap(0), vec[:, bass.ds(b * 2 + (V_CONVB + t), 1)],
                                  ALU.mult, ALU.add).then_inc(conv_step, 1)
                for k in range(1, TAPS):
                    dve.wait_ge(conv_step, b * (2 * (TAPS - 1)) + (t * (TAPS - 1) + k))
                    dve.scalar_tensor_tensor(out=acc[:, k:], in0=r[:, :S - k], scalar=tap(k), in1=acc[:, k:],
                                             op0=ALU.mult, op1=ALU.add).then_inc(
                                                 conv_step if k < TAPS - 1 else conv_ready, 1)

            def conv_low(b, t):
                dve.wait_ge(ch_ready, b * 2 + (t + 1))
                dve.tensor_tensor(cl[:, t, :], tmp[2 * t + 1][:, :], ch[:, t, :].bitcast(F32),
                                  ALU.subtract).then_inc(cl_ready, 1)

            def lru_scan(seg, first, b, t):
                def have(k):
                    dve.wait_ge(lru_dve, b * 10 + (5 * t + k))

                dve.tensor_tensor(tmp[3][:, :], ch[:, t, :].bitcast(F32), cl[:, t, :].bitcast(F32),
                                  ALU.add).then_inc(lru_dve, 1)
                i_slot, i_n = tiles.use(seg, first + 2 * t + 1, b)
                dve.wait_ge(drained[i_slot], i_n)
                have(1)
                dve.tensor_tensor(tmp[3][:, :], tmp[3][:, :], tmp[2][:, :], ALU.mult).then_inc(lru_dve, 1)
                dve.wait_ge(lru_act, b * 6 + (3 * t + 3))
                dve.scalar_tensor_tensor(out=tmp[1][:, :], in0=tmp[0][:, :], scalar=1.0, in1=tmp[1][:, :],
                                         op0=ALU.add, op1=ALU.mult).then_inc(lru_dve, 1)
                have(3)
                dve.tensor_tensor(tmp[1][:, :], tmp[1][:, :], tmp[3][:, :], ALU.mult).then_inc(lru_dve, 1)
                have(4)
                dve.tensor_tensor_scan(tmp[2][:, :], tmp[0][:, :], tmp[1][:, :], 0.0,
                                       ALU.mult, ALU.add).then_inc(lru_dve, 1)
                have(5)
                dve.wait_ge(gelu_ready, b * 2 + (t + 1))
                dve.tensor_tensor(tmp[2][:, :], tmp[2][:, :], gelu[:, t, :], ALU.mult).then_inc(y_ready, 1)

            def y_low(b, t):
                dve.wait_ge(yh_ready, b * 2 + (t + 1))
                dve.tensor_tensor(yl[:, t, :], tmp[2][:, :], yh[:, t, :].bitcast(F32), ALU.subtract).then_inc(yl_ready, 1)

            def gate_scaled(seg, b, t):
                scaled(gelu[:, t, :], tiles.use(seg, gate_tile(seg, t), b), in_filled, b * 4 + (3 + t))

            def rec_lru(seg, first, b, last):
                for j in range(2 if last else 3):
                    if last:
                        split_lo(pieces.use("recE", j))
                    else:
                        split_lo(pieces.use("recL", j, b + 1), g)
                lru_scan(seg, first, b, 0)
                y_low(b, 0)
                if not last:
                    split_lo(pieces.use("recL", 3, b + 1))
                lru_scan(seg, first, b, 1)
                if not last:
                    split_lo(pieces.use("recL", 4, b + 1))
                y_low(b, 1)

            def rec_body(b, last):
                def add(*which):
                    for m in which:
                        add_tile(tiles.use("recL", 3 + m, b), m, b * KT + (m + 1 - KT))

                conv_in("recL", b, 0)
                dve.wait_ge(yl_ready, b * 2)
                conv_in("recL", b, 1)
                gate_scaled("recL", b, 0)
                add(0)
                conv("recL", b, 0)
                add(1, 2)
                conv_low(b, 0)
                conv("recL", b, 1)
                add(3, 4)
                conv_low(b, 1)
                add(5)
                split_lo(pieces.use("recL", 5, b), g)
                add(6)
                split_lo(pieces.use("gates", 0, b))
                add(7)
                gate_scaled("recL", b, 1)
                rec_lru("recL", 12, b, last)

            split_lo(pieces.use("recA", 2), g)
            conv_in("recA", 0, 0)
            conv("recA", 0, 0)
            split_lo(pieces.use("recA", 3), g)
            conv_low(0, 0)
            conv_in("recA", 0, 1)
            conv("recA", 0, 1)
            conv_low(0, 1)
            for t in range(2):
                gate_scaled("recA", 0, t)
            split_lo(pieces.use("gates", 0, 0))
            rec_lru("recA", 4, 0, False)
            with dve.Fori(1, BLOCKS - 1) as b:
                rec_body(b, False)
            rec_body(BLOCKS - 1, True)
            slot, _ = pieces.use("forget", 0)
            dve.memset(raw[slot][:, :], 0.0).then_inc(forget_dve, 1)

            def epilogue(seg, out_count, nexts):
                nexts[0]()
                for k in range(KT):
                    add_tile(tiles.use(seg, k), k, out_count + k + 1)
                    if seg != "ffn1E" and k >= 1:
                        low_half(seg, k - 1)
                    if k == 5:
                        nexts[1]()
                if seg != "ffn1E":
                    low_half(seg, KT - 1)
                mean_square(seg)
                inverse_root(seg)

            def ffn(f):
                gain = GAIN[f"ffn{f}"]
                seg0, seg = f"ffn{f}A", f"ffn{f}L"

                def gate(sg, tile, grp, t):
                    scaled(tmp[t][:, :], tiles.use(sg, tile, grp), in_filled, grp * 4 + (IN_FFN[f] + 2 * t + 1))

                def hidden(sg, tile, grp, t):
                    use = tiles.use(sg, tile, grp)
                    scaled(tmp[2 + t][:, :], use, in_filled, grp * 4 + (IN_FFN[f] + 2 * t + 2))
                    dve.wait_ge(drained[use[0]], use[1])
                    dve.wait_ge(silu_ready, grp * 2 + (2 * f * GROUPS + t + 1))
                    dve.tensor_tensor(tmp[2 + t][:, :], tmp[2 + t][:, :], tmp[t][:, :], ALU.mult).then_inc(h_ready, 1)

                def h_low(grp, t):
                    dve.wait_ge(hh_ready, grp * 2 + (2 * f * GROUPS + t + 1))
                    dve.tensor_tensor(hl[:, t, :], tmp[2 + t][:, :], hh[:, t, :].bitcast(F32),
                                      ALU.subtract).then_inc(hl_ready, 1)

                split_lo(pieces.use(seg0, 2), gain)
                gate(seg0, 0, 0, 0)
                split_lo(pieces.use(seg0, 3), gain)
                hidden(seg0, 1, 0, 0)
                h_low(0, 0)
                split_lo(pieces.use(seg, 0, 1), gain)
                gate(seg0, 2, 0, 1)
                split_lo(pieces.use(seg, 1, 1))
                hidden(seg0, 3, 0, 1)
                h_low(0, 1)

                def body(grp, last):
                    split_lo(pieces.use(seg, 2, grp))
                    gate(seg, 0, grp, 0)
                    for j in range(2):
                        split_lo(pieces.use(seg, 3 + j, grp), gain)
                        for m in range(4 * j, 4 * j + 4):
                            add_tile(tiles.use(seg, 1 + m, grp), m, grp * KT + (OUT_FFN[f] + m + 1 - KT))
                    split_lo(pieces.use(seg, 5, grp), gain)
                    hidden(seg, 9, grp, 0)
                    h_low(grp, 0)
                    if last:
                        split_lo(pieces.use(f"ffn{f}E", 0))
                    else:
                        split_lo(pieces.use(seg, 0, grp + 1), gain)
                    gate(seg, 10, grp, 1)
                    if last:
                        split_lo(pieces.use(f"ffn{f}E", 1))
                    else:
                        split_lo(pieces.use(seg, 1, grp + 1))
                    hidden(seg, 11, grp, 1)
                    h_low(grp, 1)

                with dve.Fori(1, GROUPS - 1) as grp:
                    body(grp, False)
                body(GROUPS - 1, True)

            epilogue("recE", 8 * (BLOCKS - 1), [lambda: split_lo(pieces.use("ffn0A", 0), GAIN["ffn0"]),
                                                lambda: split_lo(pieces.use("ffn0A", 1), GAIN["ffn0"])])
            ffn(0)
            epilogue("ffn0E", OUT_FFN[0] + 8 * (GROUPS - 1), [lambda: split_lo(pieces.use("forget", 0), V_KV),
                                                              lambda: split_lo(pieces.use("attA", 0), V_KV)])

            z, e = probs[1][0:HEADS].rearrange("p a n -> p (a n)"), o_tmp[0:HEADS, :]
            one_e, d = probs[0][0:HEADS, 0, :], probs[0][0:HEADS, 1, :]
            log1p, lost = ps[1][0:HEADS, :], ps[2][0:HEADS, :]
            done = [1]

            def chain(ins):
                ins.then_inc(forget_dve, 1)
                done[0] += 1
                dve.wait_ge(forget_dve, done[0])

            def project_half(i, j, half, count):
                h = slice(half * BANK, (half + 1) * BANK)
                dve.wait_ge(kq_filled, count)
                if j == 0:
                    dve.tensor_tensor(kv_tmp[:, h], f_ps, rstd[:, h], ALU.mult).then_inc(f_drained, 1)
                else:
                    dve.scalar_tensor_tensor(out=q_tmp[:, h], in0=f_ps, scalar=float(HD) ** -0.5, in1=rstd[:, h],
                                             op0=ALU.mult, op1=ALU.mult).then_inc(f_drained, 1)

            split_lo(pieces.use("attA", 1), GAIN["Q"])
            f_slot, f_n = tiles.use("forget", 0)
            dve.memset(c2[:, :].bitcast(F32), 0.0)
            dve.wait_ge(forget_filled, 1)
            dve.tensor_tensor(z, ps[f_slot][0:HEADS, :], rstd[0:HEADS, :], ALU.mult).then_inc(drained[f_slot], 1)
            dve.wait_ge(drained[f_slot], f_n)
            dve.wait_ge(bforget_loaded, 16)
            chain(dve.tensor_scalar(z, z, bforget[:, 0:1], None, ALU.add))
            evac_kq = lambda j, half: project_half(0, j, half, kq_count(0, j, half))
            chain(dve.scalar_tensor_tensor(out=e, in0=z, scalar=-1.0, in1=z, op0=ALU.mult, op1=ALU.min))
            dve.wait_ge(forget_act, 1)
            chain(dve.tensor_scalar(one_e, e, 1.0, None, ALU.add))
            chain(dve.tensor_scalar(d, one_e, -1.0, None, ALU.add))
            chain(dve.tensor_scalar(lost, d, 0.0, None, ALU.is_equal))
            evac_kq(0, 0)
            chain(dve.tensor_tensor(d, d, lost, ALU.add))
            chain(dve.reciprocal(d, d))
            dve.wait_ge(forget_act, 2)
            chain(dve.tensor_tensor(log1p, log1p, e, ALU.mult))
            chain(dve.tensor_tensor(log1p, log1p, d, ALU.mult))
            evac_kq(0, 1)
            chain(dve.tensor_tensor(d, lost, e, ALU.mult))
            chain(dve.tensor_tensor(log1p, log1p, d, ALU.add))
            chain(dve.tensor_scalar(z, z, 0.0, None, ALU.min))
            chain(dve.tensor_tensor(z, z, log1p, ALU.subtract))
            evac_kq(1, 0)
            chain(dve.memset(one_e, 1.0))
            chain(dve.tensor_tensor_scan(e, one_e, z, 0.0, ALU.mult, ALU.add))
            assert done[0] == FORGET_STEPS, done
            evac_kq(1, 1)
            split_lo(pieces.use("attA", 2), V_KV)
            dve.wait_ge(c_ready, 1)
            dve.tensor_tensor(c2[32:32 + HEADS, :], e, c2[0:HEADS, :].bitcast(F32), ALU.subtract).then_inc(c_ready, 1)

            def pair(i, uses, with_w=True, with_p=True, static=False):
                for j in range(2):
                    mine, other = slice(j * HD, (j + 1) * HD), slice((1 - j) * HD, (2 - j) * HD)
                    dve.wait_ge(qh_ready, i * 2 + (j + 1))
                    dve.tensor_tensor(qs[other, j, :], q_tmp[mine, :], qs[mine, j, :].bitcast(F32),
                                      ALU.subtract).then_inc(ql_ready, 1)
                    dve.tensor_scalar(sel[:, j, :], ones[:, :], negsel[:, bass.ds(i * 2 + j, 1)], None,
                                      ALU.mult).then_inc(sel_ready, 1)
                if with_w:
                    split_lo(uses["O"])
                w = p = 0
                for u, step in pair_steps(with_w, with_p):
                    m = int(step[1]) if len(step) > 1 else 0
                    if step == "V":
                        dve.wait_ge(kl_ready, i * 2 + 2)
                        scaled(kv_tmp[:, :], tiles.use("att", 0, i), v_filled, i + 1)
                    elif step == "X":
                        slot, _ = tiles.use("att", 1 + 2 * QB, i)
                        dve.wait_ge(vh_ready, i + 1)
                        src = ps[slot][:, :].rearrange("p (b j d) -> p j b d", b=QB, j=2)
                        dve.tensor_tensor(vs[:, 0, :, 1, :], src[:, 0], vs[:, 0, :, 0, :].bitcast(F32), ALU.subtract)
                        dve.tensor_tensor(vs[:, 1, :, 1, :], src[:, 1], vs[:, 1, :, 0, :].bitcast(F32),
                                          ALU.subtract).then_inc(drained[slot], 1)
                    elif step[0] == "S":
                        n, wide = 2 * (u + 1) + m, (2 * range_of(u + 1) + m + 1) * P
                        slot, _ = s_tile(i, u + 1, m)
                        dve.wait_ge(s_filled, i * 2 * QB + (n + 1))
                        dve.tensor_reduce(nmax[:, n:n + 1], ps[slot][:, 0:wide], AX.X, ALU.max,
                                          negate=True).then_inc(nmax_ready, 1)
                    elif step[0] == "N":
                        n, wide = 2 * (u + 1) + m, (2 * range_of(u + 1) + m + 1) * P
                        slot, s_n = s_tile(i, u + 1, m)
                        dve.wait_ge(drained[slot], s_n)
                        dve.reciprocal(rinv[:, n:n + 1], rsum[:, n:n + 1]).then_inc(rinv_ready, 1)
                        dve.wait_ge(rinv_ready, i * 2 * QB + (n + 1))
                        pr = probs[(u + 1) % 2][:, m, 0:wide]
                        dve.tensor_scalar(pr, pr, rinv[:, n:n + 1], None, ALU.mult).then_inc(p_ready, 1)
                    elif step[0] == "T":
                        t = tiles_before(u) + m
                        width = 4 * P if m < range_of(u) else 3 * P
                        dve.wait_ge(pth_ready, i * T_PAIR + (t + 1))
                        dve.tensor_tensor(ptl[t % 2][:, 0:width], t_ps[t % 2][:, 0:width],
                                          pth[t % 2][:, 0:width].bitcast(F32), ALU.subtract).then_inc(ptl_ready, 1)
                    elif step == "O":
                        v = u - 1
                        j, r = v // RANGES, range_of(v)
                        dve.wait_ge(o_low_ready, i * UNITS + u)
                        dve.tensor_tensor(o_tmp[j * HD:(j + 1) * HD, r * 2 * P:(r + 1) * 2 * P], o_ps[0:HD, :],
                                          o_low[v % 2][:, :], ALU.add).then_inc(o_added, 1)
                    elif step == "w":
                        h = slice(w % 2 * BANK, (w % 2 + 1) * BANK)
                        dve.wait_ge(w_filled, i * 16 + (w + 1 - 16))
                        dve.tensor_tensor(resid[:, w // 2, h], f_ps, resid[:, w // 2, h], ALU.add).then_inc(f_drained, 1)
                        w += 1
                    elif step == "p":
                        p += 1
                        if p % KT == 0:
                            q = p // KT - 1
                            project_half(i + 1, q // 2, q % 2, kq_count(i + 1, q // 2, q % 2))
                    if with_p and (u, step) in LO_AT:
                        kind, k0, k1 = LO_AT[u, step]
                        split_lo(uses[kind], GAIN[kind[-1]], k0, k1)

            pair(0, att_uses(0), with_w=False, static=True)
            with dve.Fori(1, PAIRS - 2, 2) as i:
                for d in range(2):
                    pair(i + d, att_uses(i + d, i, d))
            pair(PAIRS - 1, att_uses(PAIRS - 1, None, 1), with_p=False)
            split_lo(pieces.use("attE", 0))
            epilogue("attE", OUT_ATT,
                     [lambda: split_lo(pieces.use("ffn1A", 0), GAIN["ffn1"]), lambda: None])
            split_lo(pieces.use("ffn1A", 1), GAIN["ffn1"])
            ffn(1)
            epilogue("ffn1E", OUT_FFN[1] + 8 * (GROUPS - 1), [lambda: None, lambda: None])

            for k in range(KT):
                dve.scalar_tensor_tensor(out=resid[:, k, :], in0=resid[:, k, :],
                                         scalar=vec[:, V_FINAL + k:V_FINAL + k + 1], in1=rstd[:, :],
                                         op0=ALU.mult, op1=ALU.mult).then_inc(y_final, 1)
            for b in range(0, QB, 2):
                dve.wait_ge(rows_filled, b + 1)
                if b >= 4:
                    dve.wait_ge(rows_stored[b % 4], 16)
                if b >= 1:
                    dve.wait_ge(rows_ready, b)
                dve.tensor_copy(tmp[b % 4][:, :], ps[tiles.use("final", b)[0]][:, :]).then_inc(rows_ready, 1)


_INS = ["x", "norm_mix", "norm_ffn", "w_ffn_in", "w_ffn_out", "w_rec_in", "conv_w", "conv_b", "w_lru_gates",
        "b_lru_gates", "lru_param", "w_rec_out", "norm_kv", "w_kvf", "b_forget", "w_q", "w_o", "norm_final"]


def kernel(**inputs):
    import numpy as np
    import concourse.bacc as bacc
    from concourse.bass_utils import run_bass_kernel_spmd

    nc = bacc.Bacc("TRN2", target_bir_lowering=False, num_devices=1)
    arrays, args = {}, []
    for name in _INS:
        a = np.ascontiguousarray(inputs[name])
        arrays[f"in_{name}"] = a
        args.append(nc.dram_tensor(f"in_{name}", a.shape, mybir.dt.from_np(a.dtype), kind="ExternalInput").ap())
    out = nc.dram_tensor("out", inputs["x"].shape, F32, kind="ExternalOutput").ap()
    hawk_fox_yoco(nc, *args, out)
    r = run_bass_kernel_spmd(nc, [arrays], core_ids=[0])
    return r.results[0]["out"]
```

```python
import concourse.bass as bass
from concourse import mybir
from contextlib import ExitStack

F32 = mybir.dt.float32
F32R = mybir.dt.float32r
BF16 = mybir.dt.bfloat16
ALU = mybir.AluOpType
ACT = mybir.ActivationFunctionType
AX = mybir.AxisListType

P = 128
BANK = 512
EPS = 1e-6
LRU_C = 8.0
NEG = -1e30
TINY = 1e-34


class Turns:

    def __init__(self, slots):
        self.total = [0] * slots
        self.segments = {}

    def plan(self, name, order, iters=1, first=0, stride=1):
        assert all(order.count(s) % stride == 0 for s in order)
        self.segments[name] = (list(self.total), order, first, stride)
        for s in order:
            self.total[s] += iters
        return self

    def use(self, name, j, i=0):
        base, order, first, stride = self.segments[name]
        s = order[j]
        per = order.count(s) // stride
        return s, i * per + (base[s] - first * per + order[:j].count(s) + 1)


RANGE_ORDER = [3, 0, 2, 1]
UNIT_STEPS = {
    3: "O T0 T1 S0 a S1 V0 T2 V1 T3 N0 w V2 N1 V3",
    0: "O T0 a S0 p p p V0 S1 N0 N1 p p p p p",
    2: "O T0 T1 S0 a S1 V0 T2 V1 N0 w V2 N1 a",
    1: "O T0 T1 S0 p V0 S1 p V1 p N0 N1 p p p p p",
}
PAIR_START = "A S0 S1 N0 N1 B a X w Y a w"

HI_AT = {(0, "T0"): ("K", 0, 2), (0, "T1"): ("K", 2, 4), (0, "S0"): ("K", 4, 6), (0, "T2"): ("K", 6, 8),
         (4, "T0"): ("Q", 0, 2), (4, "T1"): ("Q", 2, 4), (4, "S0"): ("Q", 4, 6), (4, "T2"): ("Q", 6, 8),
         (7, "T1"): ("nextV", 0, 8)}
LO_AT = {(0, "T3"): ("K", 0, 2), (0, "N1"): ("K", 2, 4), (0, "V3"): ("K", 4, 8),
         (4, "T3"): ("Q", 0, 2), (4, "N1"): ("Q", 2, 4), (4, "V3"): ("Q", 4, 8),
         (7, "T1"): ("nextV", 0, 8)}


def pair_steps(with_w, with_p):
    steps = [(-1, s) for s in PAIR_START.split()]
    units = 2 * len(RANGE_ORDER)
    for u in range(units):
        for s in UNIT_STEPS[RANGE_ORDER[u % len(RANGE_ORDER)]].split():
            if u == 0 and s == "O" or u == units - 1 and s[0] in "SN":
                continue
            steps.append((u, s))
    steps.append((units, "O"))
    return [x for x in steps if (x[1] not in "aw" or with_w) and (x[1] != "p" or with_p)]


def hawk_fox_yoco(nc, x, norm_mix, norm_ffn, w_ffn_in, w_ffn_out, w_rec_in, conv_w, conv_b,
                  w_lru_gates, b_lru_gates, lru_param, w_rec_out, norm_kv, w_kvf, b_forget,
                  w_q, w_o, norm_final, out):
    S, D = x.shape[1], x.shape[2]
    KT = D // P
    FF = w_ffn_out.shape[1]
    GROUPS = FF // (2 * P)
    BLOCKS, LW = w_lru_gates.shape[1], w_lru_gates.shape[2]
    TAPS = conv_w.shape[1]
    HEADS = w_kvf.shape[1] - 2 * D
    HD = D // HEADS
    PAIRS = HEADS * HD // P
    QB = S // P
    RANGES = QB // 2
    UNITS = 2 * RANGES
    assert KT == 8 and S == 2 * BANK and LW == 2 * P and HD == 64 and FF % (2 * P) == 0

    V_MIX, V_FFN, V_KV, V_FINAL = 0, 2 * KT, 4 * KT, 5 * KT
    V_CONVB, V_LRU, V_CONVW, V_GATEB = 6 * KT, 7 * KT, 8 * KT, (8 + TAPS) * KT
    V_ALL = V_GATEB + BLOCKS * 2 * LW // P

    GATE_SLOT = 3
    pieces = Turns(4)
    pieces.plan("recA", [0, 1, 2, 0]).plan("recL", [1, 2, 0, 1, 2, 0], BLOCKS - 1, 1).plan("recE", [1, 2])
    pieces.plan("gates", [3], BLOCKS)
    for f in range(2):
        pieces.plan(f"ffn{f}A", [0, 1, 2, 0]).plan(f"ffn{f}L", [1, 2, 0, 1, 2, 0], GROUPS - 1, 1)
        pieces.plan(f"ffn{f}E", [1, 2])
        if f == 0:
            pieces.plan("forget", [3])
            pieces.plan("attA", [0, 1, 0, 0, 0]).plan("attL", [1, 0, 1, 1, 0, 1, 0, 0], (PAIRS - 2) // 2, 1, 2)
            pieces.plan("attZ", [1, 0]).plan("attE", [1])
    tiles = Turns(4)
    OUT_STAT = [0, 1, 2, 0, 1, 2, 0, 1, 3]
    tiles.plan("vec", [3]).plan("start", OUT_STAT)
    tiles.plan("recA", [0, 1, 2, 3] * 2).plan("recL", [0, 1, 2, 3] * 4, BLOCKS - 1, 1).plan("recE", OUT_STAT)
    for f in range(2):
        tiles.plan(f"ffn{f}A", [0, 1, 2, 3]).plan(f"ffn{f}L", [0, 1, 2, 3] * 3, GROUPS - 1, 1)
        tiles.plan(f"ffn{f}E", OUT_STAT)
        if f == 0:
            tiles.plan("forget", [3])
            tiles.plan("att", [1, 0] * QB + [2], PAIRS).plan("attE", OUT_STAT)
    tiles.plan("final", [0, 1, 2, 3] * 2)

    IN_FFN = [4 * BLOCKS, 4 * (BLOCKS + GROUPS)]
    OUT_FFN, OUT_ATT = [8 * BLOCKS, 8 * (BLOCKS + GROUPS + 1)], 8 * (BLOCKS + GROUPS)
    STAT = {"start": 0, "recE": 1, "ffn0E": 2, "attE": 3, "ffn1E": 4}
    LRU_STEPS, FORGET_STEPS = 16, 10
    T_PAIR = RANGES * (RANGES + 1)

    with ExitStack() as life:
        def sb(name, shape, dt, at=life):
            return at.enter_context(nc.sbuf_tensor(name, shape, dt))

        def sem(name):
            return life.enter_context(nc.semaphore(name))

        resid = sb("resid", [P, KT, S], F32)
        xh = sb("xh", [P, KT, S], F32R)
        xl = sb("xl", [P, KT, S], F32R)
        rstd = sb("rstd", [P, S], F32)
        raw = [sb(f"raw{s}", [P, 1024], F32) for s in range(2)]
        wh = [sb(f"wh{s}", [P, 1024], F32R) for s in range(2)]
        wl = [sb(f"wl{s}", [P, 1024], F32R) for s in range(2)]
        ident = sb("ident", [P, P], F32)
        ones = sb("ones", [P, P], F32)
        identb = sb("identb", [P, P], BF16)
        maskb = sb("maskb", [P, P], BF16)
        vec = sb("vec", [P, V_ALL], F32)
        lru = sb("lru", [P, 6, KT], F32)
        row_rstd = sb("row_rstd", [P, QB], F32)
        bforget = sb("bforget", [HEADS, 1], F32)
        negsel = sb("negsel", [P, HEADS], F32)

        with ExitStack() as att:
            kh = sb("kh", [P, 2, S], F32R, att)
            kl = sb("kl", [P, 2, S], F32R, att)
            qs = sb("qs", [P, 2, S], F32R, att)
            vs = sb("vs", [P, 2, QB, 2, HD], F32R, att)
            probs = [sb(f"probs{b}", [P, 2, S // (b + 1)], F32, att) for b in range(2)]
            pth = [sb(f"pth{b}", [P, BANK], F32R, att) for b in range(2)]
            ptl = [sb(f"ptl{b}", [P, BANK], F32R, att) for b in range(2)]
            oh = sb("oh", [P, S], F32R, att)
            ol = sb("ol", [P, S], F32R, att)
            kv_tmp = sb("kv_tmp", [P, S], F32, att)
            q_tmp = sb("q_tmp", [P, S], F32, att)
            o_tmp = sb("o_tmp", [P, S], F32, att)
            c2 = sb("c2", [P, S], F32R, att)
            sel = sb("sel", [P, 2, P], F32R, att)
            o_low = [sb(f"o_low{b}", [HD, 2 * P], F32, att) for b in range(2)]
            nmax = sb("nmax", [P, 2 * QB], F32, att)
            rsum = sb("rsum", [P, 2 * QB], F32, att)
            rinv = sb("rinv", [P, 2 * QB], F32, att)

        raw += [sb(f"raw{s}", [P, 1024], F32) for s in (2, 3)]
        wh += [sb(f"wh{s}", [P, 1024], F32R) for s in (2, 3)]
        wl += [sb(f"wl{s}", [P, 1024], F32R) for s in (2, 3)]
        tmp = [sb(f"tmp{b}", [P, S], F32) for b in range(4)]
        with ExitStack() as load:
            vrow = sb("vrow", [V_ALL, P], F32, load)
            xin = sb("xin", [P, QB, D], F32, load)
        with ExitStack() as rec:
            gelu = sb("gelu", [P, 2, S], F32, rec)
            ch = sb("ch", [P, 2, S], F32R, rec)
            cl = sb("cl", [P, 2, S], F32R, rec)
            yh = sb("yh", [P, 2, S], F32R, rec)
            yl = sb("yl", [P, 2, S], F32R, rec)
        hh = sb("hh", [P, 2, S], F32R)
        hl = sb("hl", [P, 2, S], F32R)

        ps = [life.enter_context(nc.psum_tensor(f"ps{s}", [P, S], F32)) for s in range(4)]
        t_ps = [ps[2][:, b * BANK:(b + 1) * BANK] for b in range(2)]
        o_ps = ps[3][:, 0:2 * P]
        f_ps = ps[3][:, BANK:2 * BANK]
        f_alt = ps[0][:, BANK:2 * BANK]

        vec_loaded = sem("vec_loaded")
        bforget_loaded = sem("bforget_loaded")
        x_loaded = sem("x_loaded")
        loaded = [sem(f"loaded{s}") for s in range(4)]
        hi_ready = [sem(f"hi_ready{s}") for s in range(4)]
        lo_ready = [sem(f"lo_ready{s}") for s in range(4)]
        drained = [sem(f"drained{s}") for s in range(4)]
        const_ready = sem("const_ready")
        const_zero = sem("const_zero")
        vec_filled = sem("vec_filled")
        lru_step = sem("lru_step")
        xt_filled = sem("xt_filled")
        in_filled = sem("in_filled")
        gates_filled = sem("gates_filled")
        kq_filled = sem("kq_filled")
        v_filled = sem("v_filled")
        w_filled = sem("w_filled")
        f_drained = sem("f_drained")
        out_filled = sem("out_filled")
        stat_filled = sem("stat_filled")
        xh_ready = sem("xh_ready")
        sq_ready = sem("sq_ready")
        sq_used = sem("sq_used")
        xl_ready = sem("xl_ready")
        root_ready = sem("root_ready")
        rstd_ready = sem("rstd_ready")
        conv_step = sem("conv_step")
        conv_ready = sem("conv_ready")
        ch_ready = sem("ch_ready")
        cl_ready = sem("cl_ready")
        gelu_ready = sem("gelu_ready")
        lru_act = sem("lru_act")
        lru_dve = sem("lru_dve")
        y_ready = sem("y_ready")
        yh_ready = sem("yh_ready")
        yl_ready = sem("yl_ready")
        silu_ready = sem("silu_ready")
        h_ready = sem("h_ready")
        hh_ready = sem("hh_ready")
        hl_ready = sem("hl_ready")
        forget_filled = sem("forget_filled")
        forget_dve = sem("forget_dve")
        forget_act = sem("forget_act")
        c_ready = sem("c_ready")
        vt_filled = sem("vt_filled")
        s_filled = sem("s_filled")
        t_filled = sem("t_filled")
        o_filled = sem("o_filled")
        kh_ready = sem("kh_ready")
        kl_ready = sem("kl_ready")
        kdup_ready = sem("kdup_ready")
        qh_ready = sem("qh_ready")
        ql_ready = sem("ql_ready")
        vh_ready = sem("vh_ready")
        sel_ready = sem("sel_ready")
        nmax_ready = sem("nmax_ready")
        rinv_ready = sem("rinv_ready")
        p_ready = sem("p_ready")
        pth_ready = sem("pth_ready")
        ptl_ready = sem("ptl_ready")
        pt_used = sem("pt_used")
        o_low_ready = sem("o_low_ready")
        o_added = sem("o_added")
        oh_ready = sem("oh_ready")
        ol_ready = sem("ol_ready")
        gained = sem("gained")
        rows_filled = sem("rows_filled")
        rows_ready = [sem(f"rows_ready{j}") for j in range(2)]
        rows_stored = [sem(f"rows_stored{b}") for b in range(4)]

        def cols(w, c0):
            return w[:, bass.ds(c0, P)].rearrange("(k p) n -> p k n", p=P)

        def rows(w, r0, c0, n):
            return w[bass.ds(r0, 2 * P), c0:c0 + n].rearrange("(k p) n -> p k n", p=P)

        def rec_piece(j, first):
            if j < 2:
                return cols(w_rec_in[0], first + (D + j * P))
            return cols(w_rec_in[0], first + (j - 2) * P)

        def rec_out_piece(j, first):
            return rows(w_rec_out[0], first, j * BANK, BANK)

        def ffn_piece(f, kind, g):
            what, j = kind[0], int(kind[1])
            if what == "O":
                return rows(w_ffn_out[f], g * (2 * P), j * BANK, BANK)
            return cols(w_ffn_in[f], g * (2 * P) + (j * P + (FF if what == "U" else 0)))

        def att_piece(kind, i):
            if kind == "O":
                return w_o[0][bass.ds(i * P, P), :]
            return cols(w_q[0] if kind == "Q" else w_kvf, i * P + (D if kind == "V" else 0))

        def sq(seg, k):
            if seg == "attE":
                return (kv_tmp, q_tmp)[k % 2][:, :]
            return tmp[k % 2][:, :]

        GAIN = {"rec": V_MIX, "ffn0": V_FFN, "ffn1": V_FFN + KT, "K": V_KV, "V": V_KV, "Q": V_MIX + KT}

        def rec_free(j, b):
            first = isinstance(b, int) and b == 1
            return [(in_filled, 2) if first else (out_filled, b * 8 - 12),
                    (in_filled, 3) if first else (out_filled, b * 8 - 8),
                    (in_filled, b * 4), (in_filled, b * 4 + 1), (in_filled, b * 4 + 2), (in_filled, b * 4 + 3)][j]

        def ffn_free(f, j, g):
            i0, o0 = IN_FFN[f], OUT_FFN[f]
            return [(in_filled, g * 4 + (i0 - 2)), (in_filled, g * 4 + (i0 - 1)), (in_filled, g * 4 + i0),
                    (in_filled, g * 4 + (i0 + 1)), (out_filled, g * 8 + (o0 - 4)), (out_filled, g * 8 + o0)][j]

        def att_free(kind, i):
            return {"V": (w_filled, i * 16 - 16), "O": (kq_filled, i * 4 + 4),
                    "K": (v_filled, i * 2 + 2), "Q": (kq_filled, i * 4 + 6)}[kind]

        FFN_START = [
            [(out_filled, 8 * (BLOCKS - 1)), (out_filled, 8 * BLOCKS - 4), (out_filled, 8 * BLOCKS),
             (in_filled, IN_FFN[0] + 1)],
            [(w_filled, 16 * (PAIRS - 1)), (out_filled, OUT_FFN[1]), (out_filled, OUT_FFN[1]),
             (in_filled, IN_FFN[1] + 1)]]
        FFN_END = [[(in_filled, IN_FFN[f] + 4 * GROUPS - 2), (in_filled, IN_FFN[f] + 4 * GROUPS - 1)] for f in range(2)]
        REC_END = [(out_filled, 8 * (BLOCKS - 1) - 4), (out_filled, 8 * (BLOCKS - 1))]
        ATT_START = [(in_filled, IN_FFN[1]), (out_filled, OUT_ATT - 4)]

        def att_uses(i, loop=None, d=0):
            if loop is None and d == 0:
                return {"V": pieces.use("attA", 2), "K": pieces.use("attA", 3), "Q": pieces.use("attA", 4),
                        "nextV": pieces.use("attL", 0, 1)}
            if loop is None:
                return {"V": pieces.use("attZ", 0), "O": pieces.use("attZ", 1), "lastO": pieces.use("attE", 0)}
            at, nxt = 4 * d, (4, loop) if d == 0 else (0, loop + 2)
            return {"V": pieces.use("attL", at, loop), "O": pieces.use("attL", at + 1, loop),
                    "K": pieces.use("attL", at + 2, loop), "Q": pieces.use("attL", at + 3, loop),
                    "nextV": pieces.use("attL", *nxt)}

        def mean_of(seg):
            if seg == "ffn1E":
                return row_rstd[:, :], ps[3][:, 0:QB]
            return rstd[:, :], ps[3][:, :]

        def gate_tile(seg, t):
            return 2 + t if seg == "recA" else (2, 11)[t]

        def range_of(u):
            return RANGE_ORDER[u % RANGES]

        def s_tile(i, u, half):
            return tiles.use("att", 2 * u + half, i)

        def f_before(i):
            return i * 22 - 12 if not isinstance(i, int) or i > 0 else 4

        def kq_count(i, j, half):
            return i * 4 + (2 * j + half + 1)

        def tiles_before(u):
            return sum(range_of(v) + 1 for v in range(u))

        def pt_used_at(i, t):
            u = max(v for v in range(UNITS) if tiles_before(v) <= t)
            if t - tiles_before(u) == range_of(u):
                return o_filled, i * UNITS + (u + 1)
            return pt_used, i * (T_PAIR - UNITS) + (t + 1 - u)

        def f_bank(step):
            return f_alt if step in "aA" else f_ps

        block = life.enter_context(nc.Block())

        @block.sync
        def _(sp):
            def load(use, src, k=KT, wait=True):
                slot, n = use
                if wait:
                    sp.wait_ge(lo_ready[slot], n - 1)
                dst = raw[slot][:, :] if k == 1 else raw[slot][:, :].rearrange("p (k n) -> p k n", k=k)
                sp.dma_start(dst, src).then_inc(loaded[slot], 16)

            for b in range(QB):
                sp.dma_start(xin[:, b, :], x[0, b * P:(b + 1) * P, :]).then_inc(x_loaded, 16)
            for first, v in ((V_MIX, norm_mix.rearrange("l (k p) -> (l k) p", p=P)),
                             (V_FFN, norm_ffn.rearrange("l (k p) -> (l k) p", p=P)),
                             (V_KV, norm_kv.rearrange("(k p) -> k p", p=P)),
                             (V_FINAL, norm_final.rearrange("(k p) -> k p", p=P)),
                             (V_CONVB, conv_b[0].rearrange("(k p) -> k p", p=P)),
                             (V_LRU, lru_param[0].rearrange("(k p) -> k p", p=P)),
                             (V_CONVW, conv_w[0].rearrange("t (k p) -> (t k) p", p=P)),
                             (V_GATEB, b_lru_gates[0].rearrange("b (m p) -> (b m) p", p=P))):
                sp.dma_start(vrow[first:first + v.shape[0], :], v).then_inc(vec_loaded, 16)
            sp.dma_start(bforget[:, :], b_forget.rearrange("(h a) -> h a", a=1)).then_inc(bforget_loaded, 16)

            for j in range(4):
                load(pieces.use("recA", j), rec_piece(j, 0))
            load(pieces.use("gates", 0, 0), w_lru_gates[0, 0].rearrange("(k p) n -> p k n", p=P), 2)
            with sp.Fori(1, BLOCKS) as b:
                first = b * LW
                slot, n = pieces.use("recL", 2, b)
                for j in range(3):
                    if j == 1:
                        sp.wait_ge(lo_ready[slot], n - 1)
                    load(pieces.use("recL", j, b), rec_piece(j, first), wait=(j != 2))
                for j in range(2):
                    load(pieces.use("recL", 3 + j, b), rec_out_piece(j, first - LW), 2)
                load(pieces.use("recL", 5, b), rec_piece(3, first))
                load(pieces.use("gates", 0, b),
                     w_lru_gates[0, bass.ds(b, 1)].rearrange("b (k p) n -> p (b k) n", p=P), 2)
            for j in range(2):
                load(pieces.use("recE", j), rec_out_piece(j, (BLOCKS - 1) * LW), 2)

            def load_ffn(f):
                for j, kind in enumerate(("G0", "U0", "G1", "U1")):
                    if f == 1 and j == 2:
                        sp.wait_ge(out_filled, OUT_FFN[1])
                    load(pieces.use(f"ffn{f}A", j), ffn_piece(f, kind, 0))
                with sp.Fori(1, GROUPS) as g:
                    for j, kind in enumerate(("G0", "O0", "O1", "U0", "G1", "U1")):
                        is_out = kind[0] == "O"
                        load(pieces.use(f"ffn{f}L", j, g), ffn_piece(f, kind, g - 1 if is_out else g),
                             2 if is_out else KT)
                for j, kind in enumerate(("O0", "O1")):
                    load(pieces.use(f"ffn{f}E", j), ffn_piece(f, kind, GROUPS - 1), 2)

            load_ffn(0)

            slot, n = pieces.use("forget", 0)
            sp.wait_ge(forget_dve, 1)
            sp.dma_start(raw[slot][:, :].rearrange("p (k n) -> p k n", k=KT)[:, :, 0:HEADS],
                         w_kvf[:, 2 * D:].rearrange("(k p) n -> p k n", p=P)).then_inc(loaded[slot], 16)
            for j, (kind, i) in enumerate((("K", 0), ("Q", 0), ("V", 0), ("K", 1), ("Q", 1))):
                load(pieces.use("attA", j), att_piece(kind, i))
            with sp.Fori(1, PAIRS - 2, 2) as i:
                for d in range(2):
                    for j, (kind, ahead) in enumerate((("V", 0), ("O", -1), ("K", 1), ("Q", 1))):
                        load(pieces.use("attL", 4 * d + j, i), att_piece(kind, i + (d + ahead)),
                             1 if kind == "O" else KT)
            load(pieces.use("attZ", 0), att_piece("V", PAIRS - 1))
            load(pieces.use("attZ", 1), att_piece("O", PAIRS - 2), 1)
            load(pieces.use("attE", 0), att_piece("O", PAIRS - 1), 1)

            load_ffn(1)

            for b in range(QB):
                for j in range(2):
                    sp.wait_ge(rows_ready[j], b + 1)
                sp.dma_start(out[0, b * P:(b + 1) * P, :], tmp[b % 4][:, :]).then_inc(rows_stored[b % 4], 16)
            for b in range(4):
                sp.wait_ge(rows_stored[b], 16 * (QB // 4))

        @block.gpsimd
        def _(pool):
            pool.memset(ident[:, :], 0.0)
            pool.memset(ones[:, :], 1.0)
            pool.memset(identb[:, :], 0.0)
            pool.memset(maskb[:, :], 0.0)
            pool.memset(negsel[:, :], 0.0).then_inc(const_zero, 1)
            pool.wait_ge(const_zero, 1)
            for m in (ident, identb):
                pool.affine_select(out=m[:, :], in_=m[:, :], compare_op=ALU.not_equal, fill=1.0, base=0,
                                   pattern=[[-1, P]], channel_multiplier=1)
            pool.affine_select(out=maskb[:, :], in_=maskb[:, :], compare_op=ALU.is_ge, fill=NEG, base=0,
                               pattern=[[-1, P]], channel_multiplier=1)
            pool.affine_select(out=negsel[:, :], in_=negsel[:, :], compare_op=ALU.not_equal, fill=-1.0, base=0,
                               pattern=[[-1, HEADS]], channel_multiplier=1).then_inc(const_zero, 1)
            pool.wait_ge(const_zero, 2)
            pool.affine_select(out=negsel[:, :], in_=negsel[:, :], compare_op=ALU.not_equal, fill=-1.0, base=-32,
                               pattern=[[-1, HEADS]], channel_multiplier=1).then_inc(const_ready, 1)

            with pool.Fori(0, PAIRS) as i:
                pool.wait_ge(oh_ready, i + 1)
                pool.tensor_tensor(ol[:, :], o_tmp[:, :], oh[:, :].bitcast(F32), ALU.subtract).then_inc(ol_ready, 1)

        @block.tensor
        def _(pe):
            halves = [slice(0, BANK), slice(BANK, S)]

            def claim(use):
                slot, n = use
                pe.wait_ge(drained[slot], n - 1)
                return ps[slot]

            def split_product(acc, terms):
                last = None
                for k, (w_hi, w_lo, x_hi, x_lo) in enumerate(terms):
                    for p, (w, v) in enumerate(((w_hi, x_hi), (w_hi, x_lo), (w_lo, x_hi))):
                        for h in halves:
                            last = pe.matmul(acc[:, h], w, v[:, h], start=(k == 0 and p == 0),
                                             stop=(k == len(terms) - 1 and p == 2))
                return last

            def stationary(slot, k, n, width):
                at = k * width + n * P
                return wh[slot][:, at:at + P], wl[slot][:, at:at + P]

            def in_tile(piece, tile):
                slot, n = piece
                acc = claim(tile)
                pe.wait_ge(lo_ready[slot], n)
                split_product(acc, [(*stationary(slot, k, 0, P), xh[:, k, :], xl[:, k, :])
                                    for k in range(KT)]).then_inc(in_filled, 1)

            def out_tiles(piece, tile_uses, hi, lo):
                slot, n = piece
                for m, tile in enumerate(tile_uses):
                    acc = claim(tile)
                    if m == 0:
                        pe.wait_ge(lo_ready[slot], n)
                    split_product(acc, [(*stationary(slot, k, m, BANK), hi[:, k, :], lo[:, k, :])
                                        for k in range(2)]).then_inc(out_filled, 1)

            def stat(seg, k):
                if k == 0:
                    claim(tiles.use(seg, 8))
                pe.wait_ge(sq_ready, STAT[seg] * KT + k + 1)
                if seg == "ffn1E":
                    for b in range(QB):
                        last = pe.matmul(ps[3][:, b:b + 1], sq(seg, k)[:, b * P:(b + 1) * P], ones[:, 0:1],
                                         start=(k == 0 and b == 0), stop=(k == KT - 1 and b == QB - 1))
                else:
                    for h in halves:
                        last = pe.matmul(ps[3][:, h], ones[:, :], sq(seg, k)[:, h], start=(k == 0), stop=(k == KT - 1))
                last.then_inc(stat_filled if k == KT - 1 else sq_used, 1)

            def out_and_stat(seg, tile_of):
                for m in range(KT):
                    tile_of(m)
                    if m >= 2:
                        stat(seg, m - 2)
                stat(seg, KT - 2)
                stat(seg, KT - 1)
                if seg != "ffn1E":
                    pe.wait_ge(xl_ready, (STAT[seg] + 1) * KT)

            def out_epilogue(seg, piece_seg, hi, lo):
                def tile_of(m):
                    slot, n = pieces.use(piece_seg, m // 4)
                    acc = claim(tiles.use(seg, m))
                    pe.wait_ge(lo_ready[slot], n)
                    split_product(acc, [(*stationary(slot, k, m % 4, BANK), hi[:, k, :], lo[:, k, :])
                                        for k in range(2)]).then_inc(out_filled, 1)
                out_and_stat(seg, tile_of)

            pe.wait_ge(const_ready, 1)
            pe.wait_ge(x_loaded, 16 * QB)

            def x_tile(m):
                acc = claim(tiles.use("start", m))
                for b in range(QB):
                    last = pe.transpose(acc[:, b * P:(b + 1) * P], xin[:, b, m * P:(m + 1) * P], ident[:, :])
                last.then_inc(xt_filled, 1)
                if m == 1:
                    pe.wait_ge(vec_loaded, 16 * 8)
                    claim(tiles.use("vec", 0))
                    pe.transpose(ps[3][:, 0:V_ALL], vrow[:, :], ident[0:V_ALL, 0:V_ALL]).then_inc(vec_filled, 1)
            out_and_stat("start", x_tile)


            def rec_gates(seg, b, first):
                slot, n = pieces.use("gates", 0, b)
                pe.wait_ge(lo_ready[slot], n)
                pe.wait_ge(cl_ready, 2 * b + 2)
                for j, m in enumerate((2, 0, 3, 1)):
                    acc = claim(tiles.use(seg, first + j, b))
                    split_product(acc, [(*stationary(slot, k, m, BANK), ch[:, k, :], cl[:, k, :])
                                        for k in range(2)]).then_inc(gates_filled, 1)

            for j in range(4):
                in_tile(pieces.use("recA", j), tiles.use("recA", j))
            rec_gates("recA", 0, 4)
            with pe.Fori(1, BLOCKS) as b:
                for j in range(3):
                    in_tile(pieces.use("recL", j, b), tiles.use("recL", j, b))
                pe.wait_ge(yl_ready, 2 * b)
                for j in range(2):
                    out_tiles(pieces.use("recL", 3 + j, b),
                              [tiles.use("recL", 3 + 4 * j + m, b) for m in range(4)], yh, yl)
                in_tile(pieces.use("recL", 5, b), tiles.use("recL", 11, b))
                rec_gates("recL", b, 12)
            pe.wait_ge(yl_ready, 2 * BLOCKS)
            out_epilogue("recE", "recE", yh, yl)

            def ffn(f):
                def step(seg, j, t, g):
                    in_tile(pieces.use(seg, j, g), tiles.use(seg, t, g))
                for j in range(4):
                    step(f"ffn{f}A", j, j, 0)
                with pe.Fori(1, GROUPS) as g:
                    seg = f"ffn{f}L"
                    step(seg, 0, 0, g)
                    pe.wait_ge(hl_ready, g * 2 + 2 * f * GROUPS)
                    for j in range(2):
                        out_tiles(pieces.use(seg, 1 + j, g),
                                  [tiles.use(seg, 1 + 4 * j + m, g) for m in range(4)], hh, hl)
                    for j in range(3):
                        step(seg, 3 + j, 9 + j, g)
                pe.wait_ge(hl_ready, (f + 1) * 2 * GROUPS)
                out_epilogue(f"ffn{f}E", f"ffn{f}E", hh, hl)

            ffn(0)

            slot, n = pieces.use("forget", 0)
            acc = claim(tiles.use("forget", 0))
            pe.wait_ge(lo_ready[slot], n)
            split_product(acc, [(*stationary(slot, k, 0, P), xh[:, k, :], xl[:, k, :])
                                for k in range(KT)]).then_inc(forget_filled, 1)

            def projection_part(acc, piece, half, k, filled=kq_filled):
                slot, n = piece
                if k == 0:
                    pe.wait_ge(lo_ready[slot], n)
                w_hi, w_lo = stationary(slot, k, 0, P)
                h = halves[half]
                for p, (w, v) in enumerate(((w_hi, xh), (w_hi, xl), (w_lo, xh))):
                    last = pe.matmul(acc, w, v[:, k, h], start=(k == 0 and p == 0), stop=(k == KT - 1 and p == 2))
                if k == KT - 1:
                    last.then_inc(filled, 1)

            def output_part(acc, piece, m, half):
                slot, _ = piece
                w_hi, w_lo = stationary(slot, 0, m, BANK)
                h = halves[half]
                for p, (w, v) in enumerate(((w_hi, oh), (w_hi, ol), (w_lo, oh))):
                    last = pe.matmul(acc, w, v[:, h], start=(p == 0), stop=(p == 2))
                last.then_inc(w_filled, 1)

            def scores(i, u, half):
                j, n = u // RANGES, 2 * range_of(u) + half
                acc = claim(s_tile(i, u, half))
                w = (n + 1) * P
                for c0 in range(0, w, BANK):
                    c1 = min(w, c0 + BANK)
                    pe.matmul(acc[:, c0:c1], sel[:, j, :], c2[:, c0:c1], start=True, stop=False)
                    if c1 == w:
                        pe.matmul(acc[:, w - P:w], identb[:, :], maskb[:, :], start=False, stop=False)
                    q = qs[:, j, n * P:(n + 1) * P]
                    pe.matmul(acc[:, c0:c1], q, kh[:, j, c0:c1], start=False, stop=False)
                    last = pe.matmul(acc[:, c0:c1], q, kl[:, j, c0:c1], start=False, stop=True)
                last.then_inc(s_filled, 1)

            def blocks_of(r, m):
                if m < r:
                    return [(2 * m, 0, 0), (2 * m + 1, 0, 2 * P)]
                return [(2 * m, 0, 0), (2 * m + 1, 1, 2 * P)]

            def transposes(i, u, m):
                t = tiles_before(u) + m
                if m == 0:
                    pe.wait_ge(p_ready, i * 2 * QB + 2 * (u + 1))
                if t == 0:
                    slot, n = tiles.use("att", 2 * QB, i)
                    pe.wait_ge(drained[slot], n)
                if t >= 2:
                    pe.wait_ge(ptl_ready, i * T_PAIR + (t - 1))
                for kb, q0, col in blocks_of(range_of(u), m):
                    for q in range(q0, 2):
                        last = pe.transpose(t_ps[t % 2][:, col + (q - q0) * P:col + (q - q0 + 1) * P],
                                            probs[u % 2][:, q, kb * P:(kb + 1) * P], ident[:, :])
                last.then_inc(t_filled, 1)

            def values(i, u, m):
                j, r, t = u // RANGES, range_of(u), tiles_before(u) + m
                if m == 0:
                    pe.wait_ge(o_added, i * UNITS + u)
                pe.wait_ge(ptl_ready, i * T_PAIR + (t + 1))
                for kb, q0, col in blocks_of(r, m):
                    v = vs[:, j, kb, :, :].rearrange("p a d -> p (a d)")
                    n = (2 - q0) * P
                    for pt in (pth, ptl):
                        last = pe.matmul(o_ps[:, q0 * P:2 * P], v, pt[t % 2][:, col:col + n],
                                         start=(kb == 0 and pt is pth), stop=(kb == 2 * r + 1 and pt is ptl))
                last.then_inc(o_filled if m == r else pt_used, 1)

            def pair(i, uses, with_w=True, with_p=True):
                w = p = f = 0
                read = {"a": f_before(i) - 1, "f": f_before(i)}
                for u, step in pair_steps(with_w, with_p):
                    m = int(step[1]) if len(step) > 1 else 0
                    if step in "AB":
                        half, bank = ("AB".index(step), "af"["AB".index(step)])
                        pe.wait_ge(f_drained, read[bank])
                        for k in range(KT):
                            projection_part(f_bank(step), uses["V"], half, k, v_filled)
                        f += 1
                        read[bank] = f_before(i) + f
                        if half == 0:
                            pe.wait_ge(kdup_ready, i * 4 + 4)
                            pe.wait_ge(ql_ready, i * 2 + 2)
                            pe.wait_ge(sel_ready, i * 2 + 2)
                    elif step == "X":
                        acc = claim(tiles.use("att", 2 * QB, i))
                        pe.wait_ge(ptl_ready, i * T_PAIR)
                        pe.wait_ge(f_drained, f_before(i) + 2)
                        for b in range(QB):
                            last = pe.transpose(acc[:, b * P:(b + 1) * P], kv_tmp[:, b * P:(b + 1) * P], ident[:, :])
                        last.then_inc(vt_filled, 1)
                    elif step[0] == "S":
                        if m == 1 and range_of(u + 1) >= 2:
                            pe.wait_ge(f_drained, read["a"])
                        scores(i, u + 1, m)
                    elif step[0] == "T":
                        transposes(i, u, m)
                    elif step[0] == "V":
                        values(i, u, m)
                    elif step in "aw":
                        bank = "a" if step == "a" else "f"
                        if w == 0:
                            slot, n = uses["O"]
                            pe.wait_ge(lo_ready[slot], n)
                            pe.wait_ge(ol_ready, i)
                            slot, n = s_tile(i, 0, 1)
                            pe.wait_ge(drained[slot], n)
                        pe.wait_ge(f_drained, read[bank])
                        output_part(f_bank(step), uses["O"], w // 2, w % 2)
                        w, f = w + 1, f + 1
                        read[bank] = f_before(i) + f
                    elif step == "p":
                        if p % KT == 0:
                            pe.wait_ge(f_drained, read["f"])
                            f += 1
                            read["f"] = f_before(i) + f
                        projection_part(f_ps, uses["K" if p < 2 * KT else "Q"], p // KT % 2, p % KT)
                        p += 1

            def wo_tile(piece, tile, m):
                slot, n = piece
                acc = claim(tile)
                pe.wait_ge(lo_ready[slot], n)
                split_product(acc, [(wh[slot][:, m * P:(m + 1) * P], wl[slot][:, m * P:(m + 1) * P],
                                     oh[:, :], ol[:, :])]).then_inc(out_filled, 1)

            pe.wait_ge(drained[3], tiles.use("forget", 0)[1])
            for j in range(2):
                for half in range(2):
                    pe.wait_ge(f_drained, 2 * j + half)
                    for k in range(KT):
                        projection_part(f_ps, pieces.use("attA", j), half, k)
            pe.wait_ge(c_ready, 2)
            pair(0, att_uses(0), with_w=False)
            with pe.Fori(1, PAIRS - 2, 2) as i:
                for d in range(2):
                    pair(i + d, att_uses(i + d, i, d))
            pair(PAIRS - 1, att_uses(PAIRS - 1, None, 1), with_p=False)
            pe.wait_ge(ol_ready, PAIRS)
            pe.wait_ge(ptl_ready, PAIRS * T_PAIR)
            pe.wait_ge(o_added, PAIRS * UNITS)
            pe.wait_ge(f_drained, f_before(PAIRS - 1) + 16)
            out_and_stat("attE", lambda m: wo_tile(pieces.use("attE", 0), tiles.use("attE", m), m))

            ffn(1)

            pe.wait_ge(gained, KT)
            for b in range(QB):
                if b < 4:
                    acc = claim(tiles.use("final", b))
                else:
                    for j in range(2):
                        pe.wait_ge(rows_ready[j], b - 3)
                    acc = ps[b % 4]
                for k in range(KT):
                    last = pe.transpose(acc[:, k * P:(k + 1) * P], resid[:, k, b * P:(b + 1) * P], ident[:, :])
                last.then_inc(rows_filled, 1)

        @block.scalar
        def _(act):
            def split_hi(use, free, gain=None, k0=0, k1=KT):
                slot, n = use
                if k0 == 0:
                    act.wait_ge(loaded[slot], n * 16)
                    if free is not None:
                        act.wait_ge(*free)
                if gain is None:
                    act.activation(wh[slot][:, :], raw[slot][:, :], ACT.Copy).then_inc(hi_ready[slot], 1)
                    return
                for k in range(k0, k1):
                    last = act.activation(wh[slot][:, k * P:(k + 1) * P], raw[slot][:, k * P:(k + 1) * P],
                                          ACT.Copy, scale=vec[:, gain + k:gain + k + 1])
                if k1 == KT:
                    last.then_inc(hi_ready[slot], 1)

            def halves_of_resid(seg, k):
                slot, t = tiles.use(seg, k)
                act.wait_ge(drained[slot], t)
                if seg != "ffn1E":
                    act.activation(xh[:, k, :], resid[:, k, :], ACT.Copy).then_inc(xh_ready, 1)
                if k >= 2:
                    act.wait_ge(sq_used, STAT[seg] * (KT - 1) + k - 1)
                act.activation(sq(seg, k), resid[:, k, :], ACT.Square).then_inc(sq_ready, 1)

            def root(seg):
                slot, n = tiles.use(seg, 8)
                act.wait_ge(drained[slot], n)
                act.activation(mean_of(seg)[0], mean_of(seg)[0], ACT.Sqrt).then_inc(root_ready, 1)

            for k in range(KT):
                halves_of_resid("start", k)
            act.wait_ge(drained[3], 1)
            for j in range(2):
                split_hi(pieces.use("recA", j), None, GAIN["rec"])
            root("start")

            def conv_high(b, t):
                act.wait_ge(conv_ready, b * 2 + (t + 1))
                act.activation(ch[:, t, :], tmp[1 + 2 * t][:, :], ACT.Copy).then_inc(ch_ready, 1)

            def gate_gelu(seg, b, t):
                slot, n = tiles.use(seg, gate_tile(seg, t), b)
                act.wait_ge(drained[slot], n)
                act.activation(gelu[:, t, :], gelu[:, t, :], ACT.Gelu_apprx_tanh).then_inc(gelu_ready, 1)

            def lru_gates(seg, first, b, t):
                bias = V_GATEB
                r_slot, _ = tiles.use(seg, first + 2 * t, b)
                i_slot, _ = tiles.use(seg, first + 2 * t + 1, b)
                act.wait_ge(gates_filled, b * 4 + (2 * t + 1))
                if t == 1:
                    act.wait_ge(yh_ready, b * 2 + 1)
                    act.wait_ge(yl_ready, b * 2 + 1)
                else:
                    act.wait_ge(cl_ready, b * 2 + 2)
                act.activation(tmp[0][:, :], ps[r_slot][:, :], ACT.Sigmoid,
                               bias=vec[:, bass.ds(b * 4 + (bias + 2 + t), 1)]).then_inc(drained[r_slot], 1)
                act.wait_ge(gates_filled, b * 4 + (2 * t + 2))
                act.activation(tmp[2][:, :], ps[i_slot][:, :], ACT.Sigmoid,
                               bias=vec[:, bass.ds(b * 4 + (bias + t), 1)]).then_inc(drained[i_slot], 1)
                act.wait_ge(drained[r_slot], tiles.use(seg, first + 2 * t, b)[1])
                act.activation(tmp[1][:, :], tmp[0][:, :], ACT.Tanh,
                               scale=lru[:, 0, bass.ds(b * 2 + t, 1)]).then_inc(lru_act, 1)
                act.wait_ge(lru_act, b * 6 + (3 * t + 1))
                act.activation(tmp[0][:, :], tmp[0][:, :], ACT.Exp,
                               scale=lru[:, 1, bass.ds(b * 2 + t, 1)]).then_inc(lru_act, 1)
                act.activation(tmp[1][:, :], tmp[1][:, :], ACT.Sqrt, bias=TINY).then_inc(lru_act, 1)

            def y_high(b, t):
                act.wait_ge(y_ready, b * 2 + (t + 1))
                act.activation(yh[:, t, :], tmp[2][:, :], ACT.Copy).then_inc(yh_ready, 1)

            g = GAIN["rec"]
            split_hi(pieces.use("recA", 2), None, g)
            act.wait_ge(lru_step, 1)
            act.activation(lru[:, 1, :], lru[:, 0, :], ACT.Exp).then_inc(lru_step, 1)
            act.wait_ge(lru_step, 3)
            act.activation(lru[:, 3, :], lru[:, 2, :], ACT.Ln).then_inc(lru_step, 1)

            conv_high(0, 0)
            split_hi(pieces.use("recA", 3), (in_filled, 1), g)
            split_hi(pieces.use("gates", 0, 0), None)
            conv_high(0, 1)

            def rec_gates(seg, first, b, last):
                for j in range(2 if last else 3):
                    if last:
                        split_hi(pieces.use("recE", j), REC_END[j])
                    else:
                        split_hi(pieces.use("recL", j, b + 1), rec_free(j, b + 1), g)
                lru_gates(seg, first, b, 0)
                y_high(b, 0)
                if not last:
                    split_hi(pieces.use("recL", 3, b + 1), rec_free(3, b + 1))
                lru_gates(seg, first, b, 1)
                if not last:
                    split_hi(pieces.use("recL", 4, b + 1), rec_free(4, b + 1))
                y_high(b, 1)

            def rec_body(b, last):
                conv_high(b, 0)
                split_hi(pieces.use("recL", 5, b), rec_free(5, b), g)
                conv_high(b, 1)
                gate_gelu("recL", b, 0)
                split_hi(pieces.use("gates", 0, b), (gates_filled, b * 4))
                gate_gelu("recL", b, 1)
                rec_gates("recL", 12, b, last)

            for t in range(2):
                gate_gelu("recA", 0, t)
            act.wait_ge(lru_step, LRU_STEPS)
            rec_gates("recA", 4, 0, False)
            with act.Fori(1, BLOCKS - 1) as b:
                rec_body(b, False)
            rec_body(BLOCKS - 1, True)

            def epilogue(seg, nexts):
                nexts[0]()
                for k in range(KT):
                    halves_of_resid(seg, k)
                    if k == 4:
                        nexts[1]()
                root(seg)

            def ffn(f):
                g = GAIN[f"ffn{f}"]
                seg0, seg = f"ffn{f}A", f"ffn{f}L"

                def silu(sg, tile, grp, t):
                    slot, n = tiles.use(sg, tile, grp)
                    act.wait_ge(drained[slot], n)
                    act.activation(tmp[t][:, :], tmp[t][:, :], ACT.Silu).then_inc(silu_ready, 1)

                def h_high(grp, t):
                    act.wait_ge(h_ready, grp * 2 + (2 * f * GROUPS + t + 1))
                    act.activation(hh[:, t, :], tmp[2 + t][:, :], ACT.Copy).then_inc(hh_ready, 1)

                split_hi(pieces.use(seg0, 2), FFN_START[f][2], g)
                silu(seg0, 0, 0, 0)
                split_hi(pieces.use(seg0, 3), FFN_START[f][3], g)
                h_high(0, 0)
                split_hi(pieces.use(seg, 0, 1), ffn_free(f, 0, 1), g)
                silu(seg0, 2, 0, 1)
                split_hi(pieces.use(seg, 1, 1), ffn_free(f, 1, 1))
                h_high(0, 1)

                def body(grp, last):
                    split_hi(pieces.use(seg, 2, grp), ffn_free(f, 2, grp))
                    silu(seg, 0, grp, 0)
                    split_hi(pieces.use(seg, 3, grp), ffn_free(f, 3, grp), g)
                    split_hi(pieces.use(seg, 4, grp), ffn_free(f, 4, grp), g)
                    split_hi(pieces.use(seg, 5, grp), ffn_free(f, 5, grp), g)
                    h_high(grp, 0)
                    if last:
                        split_hi(pieces.use(f"ffn{f}E", 0), FFN_END[f][0])
                    else:
                        split_hi(pieces.use(seg, 0, grp + 1), ffn_free(f, 0, grp + 1), g)
                    silu(seg, 10, grp, 1)
                    if last:
                        split_hi(pieces.use(f"ffn{f}E", 1), FFN_END[f][1])
                    else:
                        split_hi(pieces.use(seg, 1, grp + 1), ffn_free(f, 1, grp + 1))
                    h_high(grp, 1)

                with act.Fori(1, GROUPS - 1) as grp:
                    body(grp, False)
                body(GROUPS - 1, True)

            epilogue("recE", [lambda: split_hi(pieces.use("ffn0A", 0), FFN_START[0][0], GAIN["ffn0"]),
                              lambda: split_hi(pieces.use("ffn0A", 1), FFN_START[0][1], GAIN["ffn0"])])
            ffn(0)

            epilogue("ffn0E", [lambda: split_hi(pieces.use("forget", 0), (gates_filled, 4 * BLOCKS), V_KV),
                               lambda: split_hi(pieces.use("attA", 0), ATT_START[0], V_KV)])
            split_hi(pieces.use("attA", 1), ATT_START[1], GAIN["Q"])
            act.wait_ge(forget_dve, 3)
            act.activation(o_tmp[0:HEADS, :], o_tmp[0:HEADS, :], ACT.Exp).then_inc(forget_act, 1)
            act.wait_ge(forget_dve, 4)
            act.activation(ps[1][0:HEADS, :], probs[0][0:HEADS, 0, :], ACT.Ln).then_inc(forget_act, 1)
            act.wait_ge(forget_act, 2)
            act.activation(ps[2][0:HEADS, :], ps[1][0:HEADS, :], ACT.Exp, scale=-1.0).then_inc(forget_act, 1)
            split_hi(pieces.use("attA", 2), (kq_filled, 2), V_KV)

            def high_k(i, drains):
                act.wait_ge(s_filled, i * 2 * QB)
                act.wait_ge(f_drained, drains)
                for j in range(2):
                    mine = slice(j * HD, (j + 1) * HD)
                    last = act.activation(kh[mine, j, :], kv_tmp[mine, :], ACT.Copy)
                last.then_inc(kh_ready, 1)
                act.wait_ge(kh_ready, i + 1)
                for j in range(2):
                    mine, other = slice(j * HD, (j + 1) * HD), slice((1 - j) * HD, (2 - j) * HD)
                    act.activation(kh[other, j, :], kh[mine, j, :].bitcast(F32), ACT.Copy).then_inc(kdup_ready, 1)

            high_k(0, 2)
            act.wait_ge(forget_dve, FORGET_STEPS)
            act.activation(c2[0:HEADS, :], o_tmp[0:HEADS, :], ACT.Copy).then_inc(c_ready, 1)

            def high_q(i, drains):
                act.wait_ge(f_drained, drains)
                for j in range(2):
                    mine = slice(j * HD, (j + 1) * HD)
                    act.activation(qs[mine, j, :], q_tmp[mine, :], ACT.Copy).then_inc(qh_ready, 1)
                for j in range(2):
                    mine, other = slice(j * HD, (j + 1) * HD), slice((1 - j) * HD, (2 - j) * HD)
                    act.wait_ge(kl_ready, i * 2 + (j + 1))
                    act.activation(kl[other, j, :], kl[mine, j, :].bitcast(F32), ACT.Copy).then_inc(kdup_ready, 1)

            def high_o(i):
                act.wait_ge(o_added, i * UNITS + UNITS)
                act.activation(oh[:, :], o_tmp[:, :], ACT.Copy).then_inc(oh_ready, 1)

            def exponentials(i, u, half):
                n, w = 2 * u + half, (2 * range_of(u) + half + 1) * P
                slot, _ = s_tile(i, u, half)
                act.wait_ge(nmax_ready, i * 2 * QB + (n + 1))
                if u >= 2:
                    act.wait_ge(t_filled, i * T_PAIR + tiles_before(u - 1))
                act.activation(probs[u % 2][:, half, 0:w], ps[slot][:, 0:w], ACT.Exp,
                               bias=nmax[:, n:n + 1], accum_out=rsum[:, n:n + 1]).then_inc(drained[slot], 1)

            def pair(i, uses, with_w=True, with_p=True, static=False):
                high_q(i, 4 if static else f_before(i))
                if with_w:
                    high_o(i - 1)
                    split_hi(uses["O"], att_free("O", i))
                for u, step in pair_steps(False, False):
                    m = int(step[1]) if len(step) > 1 else 0
                    if step == "X":
                        act.wait_ge(vt_filled, i + 1)
                        slot, _ = tiles.use("att", 2 * QB, i)
                        src = ps[slot][:, :].rearrange("p (b j d) -> p j b d", b=QB, j=2)
                        act.activation(vs[:, 0, :, 0, :], src[:, 0], ACT.Copy)
                        act.activation(vs[:, 1, :, 0, :], src[:, 1], ACT.Copy).then_inc(vh_ready, 1)
                    elif step[0] == "S":
                        exponentials(i, u + 1, m)
                    elif step[0] == "T":
                        t = tiles_before(u) + m
                        width = 4 * P if m < range_of(u) else 3 * P
                        act.wait_ge(t_filled, i * T_PAIR + (t + 1))
                        if t >= 2:
                            act.wait_ge(*pt_used_at(i, t - 2))
                        act.activation(pth[t % 2][:, 0:width], t_ps[t % 2][:, 0:width], ACT.Copy).then_inc(pth_ready, 1)
                    elif step == "O":
                        act.wait_ge(o_filled, i * UNITS + u)
                        if u >= 3:
                            act.wait_ge(o_added, i * UNITS + (u - 2))
                        act.activation(o_low[(u - 1) % 2][:, :], o_ps[HD:P, :], ACT.Copy).then_inc(o_low_ready, 1)
                    if with_p and (u, step) in HI_AT:
                        kind, k0, k1 = HI_AT[u, step]
                        free = {"K": att_free("K", i), "Q": att_free("Q", i),
                                "nextV": (kq_filled, 4) if static else att_free("V", i + 1)}[kind]
                        split_hi(uses[kind], free, GAIN[kind[-1]], k0, k1)
                        if kind == "nextV":
                            high_k(i + 1, f_before(i + 1) - 1)
                    if not with_p and (u, step) == (UNITS - 1, "T1"):
                        split_hi(uses["lastO"], (v_filled, 2 * PAIRS))

            pair(0, att_uses(0), with_w=False, static=True)
            with act.Fori(1, PAIRS - 2, 2) as i:
                for d in range(2):
                    pair(i + d, att_uses(i + d, i, d))
            pair(PAIRS - 1, att_uses(PAIRS - 1, None, 1), with_p=False)
            high_o(PAIRS - 1)
            epilogue("attE", [lambda: split_hi(pieces.use("ffn1A", 0), FFN_START[1][0], GAIN["ffn1"]),
                              lambda: None])
            split_hi(pieces.use("ffn1A", 1), FFN_START[1][1], GAIN["ffn1"])
            ffn(1)
            for k in range(KT):
                halves_of_resid("ffn1E", k)
            root("ffn1E")
            act.wait_ge(rstd_ready, STAT["ffn1E"] + 1)
            for b in range(QB):
                act.wait_ge(rows_filled, b + 1)
                if b >= 4:
                    act.wait_ge(rows_stored[b % 4], 16)
                act.activation(tmp[b % 4][:, BANK:], ps[tiles.use("final", b)[0]][:, BANK:], ACT.Copy,
                               scale=row_rstd[:, b:b + 1]).then_inc(rows_ready[1], 1)

        @block.vector
        def _(dve):
            def split_lo(use, gain=None, k0=0, k1=KT):
                slot, n = use
                if k0 == 0:
                    dve.wait_ge(hi_ready[slot], n)
                if gain is None:
                    dve.tensor_tensor(wl[slot][:, :], raw[slot][:, :], wh[slot][:, :].bitcast(F32),
                                      ALU.subtract).then_inc(lo_ready[slot], 1)
                    return
                for k in range(k0, k1):
                    c = slice(k * P, (k + 1) * P)
                    last = dve.scalar_tensor_tensor(out=wl[slot][:, c], in0=raw[slot][:, c],
                                                    scalar=vec[:, gain + k:gain + k + 1],
                                                    in1=wh[slot][:, c].bitcast(F32), op0=ALU.mult, op1=ALU.subtract)
                if k1 == KT:
                    last.then_inc(lo_ready[slot], 1)

            def low_half(seg, k):
                dve.wait_ge(xh_ready, STAT[seg] * KT + k + 1)
                dve.tensor_tensor(xl[:, k, :], resid[:, k, :], xh[:, k, :].bitcast(F32),
                                  ALU.subtract).then_inc(xl_ready, 1)

            def mean_square(seg):
                slot, _ = tiles.use(seg, 8)
                dve.wait_ge(stat_filled, STAT[seg] + 1)
                mean, total = mean_of(seg)
                dve.tensor_scalar(mean, total, 1.0 / D, EPS, ALU.mult, ALU.add).then_inc(drained[slot], 1)

            def inverse_root(seg):
                dve.wait_ge(root_ready, STAT[seg] + 1)
                dve.reciprocal(mean_of(seg)[0], mean_of(seg)[0]).then_inc(rstd_ready, 1)
                dve.wait_ge(rstd_ready, STAT[seg] + 1)

            def scaled(dst, tile, filled, count):
                slot, n = tile
                dve.wait_ge(filled, count)
                dve.tensor_tensor(dst, ps[slot][:, :], rstd[:, :], ALU.mult).then_inc(drained[slot], 1)

            def add_tile(tile, m, count):
                slot, _ = tile
                dve.wait_ge(out_filled, count)
                dve.tensor_tensor(resid[:, m, :], ps[slot][:, :], resid[:, m, :], ALU.add).then_inc(drained[slot], 1)

            for k in range(KT):
                slot, _ = tiles.use("start", k)
                dve.wait_ge(xt_filled, k + 1)
                dve.tensor_copy(resid[:, k, :], ps[slot][:, :]).then_inc(drained[slot], 1)
                if k == 1:
                    dve.wait_ge(vec_filled, 1)
                    dve.tensor_copy(vec[:, :], ps[3][:, 0:V_ALL]).then_inc(drained[3], 1)
                if k >= 1:
                    low_half("start", k - 1)
            low_half("start", KT - 1)
            mean_square("start")
            g = GAIN["rec"]
            for j in range(2):
                split_lo(pieces.use("recA", j), g)
            inverse_root("start")

            def conv_scaled(seg, b, t):
                slot, n = tiles.use(seg, t, b)
                return drained[slot], n

            def conv_in(seg, b, t):
                scaled(tmp[2 * t][:, :], tiles.use(seg, t, b), in_filled, b * 4 + (t + 1))

            def conv(seg, b, t):
                r, acc = tmp[2 * t], tmp[2 * t + 1]
                dve.wait_ge(*conv_scaled(seg, b, t))
                tap = lambda k: vec[:, bass.ds(b * 2 + (V_CONVW + (TAPS - 1 - k) * KT + t), 1)]
                dve.tensor_scalar(acc[:, :], r[:, :], tap(0), vec[:, bass.ds(b * 2 + (V_CONVB + t), 1)],
                                  ALU.mult, ALU.add).then_inc(conv_step, 1)
                for k in range(1, TAPS):
                    dve.wait_ge(conv_step, b * (2 * (TAPS - 1)) + (t * (TAPS - 1) + k))
                    dve.scalar_tensor_tensor(out=acc[:, k:], in0=r[:, :S - k], scalar=tap(k), in1=acc[:, k:],
                                             op0=ALU.mult, op1=ALU.add).then_inc(
                                                 conv_step if k < TAPS - 1 else conv_ready, 1)

            def conv_low(b, t):
                dve.wait_ge(ch_ready, b * 2 + (t + 1))
                dve.tensor_tensor(cl[:, t, :], tmp[2 * t + 1][:, :], ch[:, t, :].bitcast(F32),
                                  ALU.subtract).then_inc(cl_ready, 1)

            def lru_scan(seg, first, b, t):
                def have(k):
                    dve.wait_ge(lru_dve, b * 10 + (5 * t + k))

                dve.tensor_tensor(tmp[3][:, :], ch[:, t, :].bitcast(F32), cl[:, t, :].bitcast(F32),
                                  ALU.add).then_inc(lru_dve, 1)
                i_slot, i_n = tiles.use(seg, first + 2 * t + 1, b)
                dve.wait_ge(drained[i_slot], i_n)
                have(1)
                dve.tensor_tensor(tmp[3][:, :], tmp[3][:, :], tmp[2][:, :], ALU.mult).then_inc(lru_dve, 1)
                dve.wait_ge(lru_act, b * 6 + (3 * t + 3))
                dve.scalar_tensor_tensor(out=tmp[1][:, :], in0=tmp[0][:, :], scalar=1.0, in1=tmp[1][:, :],
                                         op0=ALU.add, op1=ALU.mult).then_inc(lru_dve, 1)
                have(3)
                dve.tensor_tensor(tmp[1][:, :], tmp[1][:, :], tmp[3][:, :], ALU.mult).then_inc(lru_dve, 1)
                have(4)
                dve.tensor_tensor_scan(tmp[2][:, :], tmp[0][:, :], tmp[1][:, :], 0.0,
                                       ALU.mult, ALU.add).then_inc(lru_dve, 1)
                have(5)
                dve.wait_ge(gelu_ready, b * 2 + (t + 1))
                dve.tensor_tensor(tmp[2][:, :], tmp[2][:, :], gelu[:, t, :], ALU.mult).then_inc(y_ready, 1)

            def y_low(b, t):
                dve.wait_ge(yh_ready, b * 2 + (t + 1))
                dve.tensor_tensor(yl[:, t, :], tmp[2][:, :], yh[:, t, :].bitcast(F32),
                                  ALU.subtract).then_inc(yl_ready, 1)

            def gate_scaled(seg, b, t):
                scaled(gelu[:, t, :], tiles.use(seg, gate_tile(seg, t), b), in_filled, b * 4 + (3 + t))

            def rec_lru(seg, first, b, last):
                for j in range(2 if last else 3):
                    if last:
                        split_lo(pieces.use("recE", j))
                    else:
                        split_lo(pieces.use("recL", j, b + 1), g)
                lru_scan(seg, first, b, 0)
                y_low(b, 0)
                if not last:
                    split_lo(pieces.use("recL", 3, b + 1))
                lru_scan(seg, first, b, 1)
                if not last:
                    split_lo(pieces.use("recL", 4, b + 1))
                y_low(b, 1)

            def rec_body(b, last):
                def add(*which):
                    for m in which:
                        add_tile(tiles.use("recL", 3 + m, b), m, b * KT + (m + 1 - KT))

                conv_in("recL", b, 0)
                dve.wait_ge(yl_ready, b * 2)
                conv_in("recL", b, 1)
                gate_scaled("recL", b, 0)
                add(0)
                conv("recL", b, 0)
                add(1, 2)
                conv_low(b, 0)
                conv("recL", b, 1)
                add(3, 4)
                split_lo(pieces.use("recL", 5, b), g)
                add(5)
                conv_low(b, 1)
                add(6)
                split_lo(pieces.use("gates", 0, b))
                add(7)
                gate_scaled("recL", b, 1)
                rec_lru("recL", 12, b, last)

            split_lo(pieces.use("recA", 2), g)
            lp = vec[:, V_LRU:V_LRU + KT]
            dve.scalar_tensor_tensor(out=lru[:, 0, :], in0=lp, scalar=-1.0, in1=lp, op0=ALU.mult,
                                     op1=ALU.min).then_inc(lru_step, 1)
            dve.wait_ge(lru_step, 2)
            steps = [2]

            def lru_next(ins, more=1):
                ins.then_inc(lru_step, 1)
                steps[0] += more
                dve.wait_ge(lru_step, steps[0])

            lru_next(dve.tensor_scalar(lru[:, 2, :], lru[:, 1, :], 1.0, None, ALU.add), 2)
            lru_next(dve.tensor_scalar(lru[:, 4, :], lru[:, 2, :], -1.0, None, ALU.add))
            lru_next(dve.tensor_scalar(lru[:, 5, :], lru[:, 4, :], 0.0, None, ALU.is_equal))
            lru_next(dve.tensor_tensor(lru[:, 4, :], lru[:, 4, :], lru[:, 5, :], ALU.add))
            lru_next(dve.reciprocal(lru[:, 4, :], lru[:, 4, :]))
            lru_next(dve.tensor_tensor(lru[:, 3, :], lru[:, 3, :], lru[:, 1, :], ALU.mult))
            lru_next(dve.tensor_tensor(lru[:, 3, :], lru[:, 3, :], lru[:, 4, :], ALU.mult))
            lru_next(dve.tensor_tensor(lru[:, 5, :], lru[:, 5, :], lru[:, 1, :], ALU.mult))
            lru_next(dve.tensor_tensor(lru[:, 3, :], lru[:, 3, :], lru[:, 5, :], ALU.add))
            lru_next(dve.tensor_scalar(lru[:, 2, :], lp, -1.0, 0.0, ALU.mult, ALU.max))
            lru_next(dve.tensor_tensor(lru[:, 3, :], lru[:, 3, :], lru[:, 2, :], ALU.add))
            lru_next(dve.tensor_scalar(lru[:, 0, :], lru[:, 3, :], LRU_C / 2, None, ALU.mult))
            lru_next(dve.tensor_scalar(lru[:, 1, :], lru[:, 3, :], -LRU_C, None, ALU.mult))
            assert steps[0] == LRU_STEPS, steps

            conv_in("recA", 0, 0)
            conv("recA", 0, 0)
            split_lo(pieces.use("recA", 3), g)
            conv_low(0, 0)
            split_lo(pieces.use("gates", 0, 0))
            conv_in("recA", 0, 1)
            conv("recA", 0, 1)
            conv_low(0, 1)
            for t in range(2):
                gate_scaled("recA", 0, t)
            rec_lru("recA", 4, 0, False)
            with dve.Fori(1, BLOCKS - 1) as b:
                rec_body(b, False)
            rec_body(BLOCKS - 1, True)
            slot, _ = pieces.use("forget", 0)
            dve.memset(raw[slot][:, :], 0.0).then_inc(forget_dve, 1)

            def final_gain(k):
                dve.wait_ge(sq_ready, STAT["ffn1E"] * KT + k + 1)
                dve.tensor_scalar(resid[:, k, :], resid[:, k, :], vec[:, V_FINAL + k:V_FINAL + k + 1], None,
                                  ALU.mult).then_inc(gained, 1)

            def behind(seg, k):
                if seg == "ffn1E":
                    final_gain(k)
                else:
                    low_half(seg, k)

            def epilogue(seg, out_count, nexts):
                nexts[0]()
                for k in range(KT):
                    add_tile(tiles.use(seg, k), k, out_count + k + 1)
                    if k >= 1:
                        behind(seg, k - 1)
                    if k == 5:
                        nexts[1]()
                behind(seg, KT - 1)
                mean_square(seg)
                inverse_root(seg)

            def ffn(f):
                gain = GAIN[f"ffn{f}"]
                seg0, seg = f"ffn{f}A", f"ffn{f}L"

                def gate(sg, tile, grp, t):
                    scaled(tmp[t][:, :], tiles.use(sg, tile, grp), in_filled, grp * 4 + (IN_FFN[f] + 2 * t + 1))

                def hidden(sg, tile, grp, t):
                    use = tiles.use(sg, tile, grp)
                    scaled(tmp[2 + t][:, :], use, in_filled, grp * 4 + (IN_FFN[f] + 2 * t + 2))
                    dve.wait_ge(drained[use[0]], use[1])
                    dve.wait_ge(silu_ready, grp * 2 + (2 * f * GROUPS + t + 1))
                    dve.tensor_tensor(tmp[2 + t][:, :], tmp[2 + t][:, :], tmp[t][:, :], ALU.mult).then_inc(h_ready, 1)

                def h_low(grp, t):
                    dve.wait_ge(hh_ready, grp * 2 + (2 * f * GROUPS + t + 1))
                    dve.tensor_tensor(hl[:, t, :], tmp[2 + t][:, :], hh[:, t, :].bitcast(F32),
                                      ALU.subtract).then_inc(hl_ready, 1)

                split_lo(pieces.use(seg0, 2), gain)
                gate(seg0, 0, 0, 0)
                split_lo(pieces.use(seg0, 3), gain)
                hidden(seg0, 1, 0, 0)
                h_low(0, 0)
                split_lo(pieces.use(seg, 0, 1), gain)
                gate(seg0, 2, 0, 1)
                split_lo(pieces.use(seg, 1, 1))
                hidden(seg0, 3, 0, 1)
                h_low(0, 1)

                def body(grp, last):
                    split_lo(pieces.use(seg, 2, grp))
                    gate(seg, 0, grp, 0)
                    for j in range(2):
                        split_lo(pieces.use(seg, 3 + j, grp), gain)
                        for m in range(4 * j, 4 * j + 4):
                            add_tile(tiles.use(seg, 1 + m, grp), m, grp * KT + (OUT_FFN[f] + m + 1 - KT))
                    split_lo(pieces.use(seg, 5, grp), gain)
                    hidden(seg, 9, grp, 0)
                    h_low(grp, 0)
                    if last:
                        split_lo(pieces.use(f"ffn{f}E", 0))
                    else:
                        split_lo(pieces.use(seg, 0, grp + 1), gain)
                    gate(seg, 10, grp, 1)
                    if last:
                        split_lo(pieces.use(f"ffn{f}E", 1))
                    else:
                        split_lo(pieces.use(seg, 1, grp + 1))
                    hidden(seg, 11, grp, 1)
                    h_low(grp, 1)

                with dve.Fori(1, GROUPS - 1) as grp:
                    body(grp, False)
                body(GROUPS - 1, True)

            epilogue("recE", 8 * (BLOCKS - 1), [lambda: split_lo(pieces.use("ffn0A", 0), GAIN["ffn0"]),
                                                lambda: split_lo(pieces.use("ffn0A", 1), GAIN["ffn0"])])
            ffn(0)
            epilogue("ffn0E", OUT_FFN[0] + 8 * (GROUPS - 1), [lambda: split_lo(pieces.use("forget", 0), V_KV),
                                                              lambda: split_lo(pieces.use("attA", 0), V_KV)])

            z, e = probs[1][0:HEADS].rearrange("p a n -> p (a n)"), o_tmp[0:HEADS, :]
            one_e, over = probs[0][0:HEADS, 0, :], probs[0][0:HEADS, 1, :]
            log, inverse = ps[1][0:HEADS, :], ps[2][0:HEADS, :]
            done = [1]

            def chain(ins):
                ins.then_inc(forget_dve, 1)
                done[0] += 1
                dve.wait_ge(forget_dve, done[0])

            def project_half(j, half, count):
                h = slice(half * BANK, (half + 1) * BANK)
                dve.wait_ge(kq_filled, count)
                if j == 0:
                    dve.tensor_tensor(kv_tmp[:, h], f_ps, rstd[:, h], ALU.mult).then_inc(f_drained, 1)
                else:
                    dve.scalar_tensor_tensor(out=q_tmp[:, h], in0=f_ps, scalar=float(HD) ** -0.5, in1=rstd[:, h],
                                             op0=ALU.mult, op1=ALU.mult).then_inc(f_drained, 1)

            def low_k(i):
                dve.wait_ge(kh_ready, i + 1)
                for j in range(2):
                    mine = slice(j * HD, (j + 1) * HD)
                    dve.tensor_tensor(kl[mine, j, :], kv_tmp[mine, :], kh[mine, j, :].bitcast(F32),
                                      ALU.subtract).then_inc(kl_ready, 1)

            def first_half_tile(j, half):
                project_half(j, half, kq_count(0, j, half))

            split_lo(pieces.use("attA", 1), GAIN["Q"])
            f_slot, f_n = tiles.use("forget", 0)
            dve.memset(c2[:, :].bitcast(F32), 0.0)
            dve.wait_ge(forget_filled, 1)
            dve.tensor_tensor(z, ps[f_slot][0:HEADS, :], rstd[0:HEADS, :], ALU.mult).then_inc(drained[f_slot], 1)
            dve.wait_ge(drained[f_slot], f_n)
            dve.wait_ge(bforget_loaded, 16)
            chain(dve.tensor_scalar(z, z, bforget[:, 0:1], None, ALU.add))
            chain(dve.scalar_tensor_tensor(out=e, in0=z, scalar=-1.0, in1=z, op0=ALU.mult, op1=ALU.min))
            dve.wait_ge(forget_act, 1)
            chain(dve.tensor_scalar(one_e, e, 1.0, None, ALU.add))
            chain(dve.scalar_tensor_tensor(out=over, in0=one_e, scalar=-1.0, in1=e, op0=ALU.add, op1=ALU.subtract))
            first_half_tile(0, 0)
            dve.wait_ge(forget_act, 3)
            chain(dve.tensor_tensor(over, over, inverse, ALU.mult))
            chain(dve.tensor_tensor(over, log, over, ALU.subtract))
            chain(dve.scalar_tensor_tensor(out=z, in0=z, scalar=0.0, in1=over, op0=ALU.min, op1=ALU.subtract))
            chain(dve.memset(one_e, 1.0))
            first_half_tile(0, 1)
            chain(dve.tensor_tensor_scan(e, one_e, z, 0.0, ALU.mult, ALU.add))
            assert done[0] == FORGET_STEPS, done
            first_half_tile(1, 0)
            dve.wait_ge(c_ready, 1)
            dve.tensor_tensor(c2[32:32 + HEADS, :], e, c2[0:HEADS, :].bitcast(F32), ALU.subtract).then_inc(c_ready, 1)
            first_half_tile(1, 1)
            split_lo(pieces.use("attA", 2), V_KV)
            low_k(0)

            def pair(i, uses, with_w=True, with_p=True):
                for j in range(2):
                    mine, other = slice(j * HD, (j + 1) * HD), slice((1 - j) * HD, (2 - j) * HD)
                    dve.wait_ge(qh_ready, i * 2 + (j + 1))
                    dve.tensor_tensor(qs[other, j, :], q_tmp[mine, :], qs[mine, j, :].bitcast(F32),
                                      ALU.subtract).then_inc(ql_ready, 1)
                    dve.tensor_scalar(sel[:, j, :], ones[:, :], negsel[:, bass.ds(i * 2 + j, 1)], None,
                                      ALU.mult).then_inc(sel_ready, 1)
                w = p = 0
                for u, step in pair_steps(with_w, with_p):
                    m = int(step[1]) if len(step) > 1 else 0
                    if step in "AB":
                        half = "AB".index(step)
                        if half == 1 and with_w:
                            split_lo(uses["O"])
                        h = slice(half * BANK, (half + 1) * BANK)
                        dve.wait_ge(kl_ready, i * 2 + 2)
                        dve.wait_ge(v_filled, i * 2 + (half + 1))
                        dve.tensor_tensor(kv_tmp[:, h], f_bank(step), rstd[:, h], ALU.mult).then_inc(f_drained, 1)
                    elif step == "Y":
                        slot, _ = tiles.use("att", 2 * QB, i)
                        dve.wait_ge(vh_ready, i + 1)
                        src = ps[slot][:, :].rearrange("p (b j d) -> p j b d", b=QB, j=2)
                        dve.tensor_tensor(vs[:, 0, :, 1, :], src[:, 0], vs[:, 0, :, 0, :].bitcast(F32), ALU.subtract)
                        dve.tensor_tensor(vs[:, 1, :, 1, :], src[:, 1], vs[:, 1, :, 0, :].bitcast(F32),
                                          ALU.subtract).then_inc(drained[slot], 1)
                    elif step[0] == "S":
                        n, wide = 2 * (u + 1) + m, (2 * range_of(u + 1) + m + 1) * P
                        slot, _ = s_tile(i, u + 1, m)
                        dve.wait_ge(s_filled, i * 2 * QB + (n + 1))
                        dve.tensor_reduce(nmax[:, n:n + 1], ps[slot][:, 0:wide], AX.X, ALU.max,
                                          negate=True).then_inc(nmax_ready, 1)
                    elif step[0] == "N":
                        n, wide = 2 * (u + 1) + m, (2 * range_of(u + 1) + m + 1) * P
                        slot, s_n = s_tile(i, u + 1, m)
                        dve.wait_ge(drained[slot], s_n)
                        dve.reciprocal(rinv[:, n:n + 1], rsum[:, n:n + 1]).then_inc(rinv_ready, 1)
                        dve.wait_ge(rinv_ready, i * 2 * QB + (n + 1))
                        pr = probs[(u + 1) % 2][:, m, 0:wide]
                        dve.tensor_scalar(pr, pr, rinv[:, n:n + 1], None, ALU.mult).then_inc(p_ready, 1)
                    elif step[0] == "T":
                        t = tiles_before(u) + m
                        width = 4 * P if m < range_of(u) else 3 * P
                        dve.wait_ge(pth_ready, i * T_PAIR + (t + 1))
                        dve.tensor_tensor(ptl[t % 2][:, 0:width], t_ps[t % 2][:, 0:width],
                                          pth[t % 2][:, 0:width].bitcast(F32), ALU.subtract).then_inc(ptl_ready, 1)
                    elif step == "O":
                        v = u - 1
                        j, r = v // RANGES, range_of(v)
                        dve.wait_ge(o_low_ready, i * UNITS + u)
                        dve.tensor_tensor(o_tmp[j * HD:(j + 1) * HD, r * 2 * P:(r + 1) * 2 * P], o_ps[0:HD, :],
                                          o_low[v % 2][:, :], ALU.add).then_inc(o_added, 1)
                    elif step in "aw":
                        h = slice(w % 2 * BANK, (w % 2 + 1) * BANK)
                        dve.wait_ge(w_filled, i * 16 + (w + 1 - 16))
                        dve.tensor_tensor(resid[:, w // 2, h], f_bank(step), resid[:, w // 2, h],
                                          ALU.add).then_inc(f_drained, 1)
                        w += 1
                    elif step == "p":
                        p += 1
                        if p % KT == 0:
                            q = p // KT - 1
                            project_half(q // 2, q % 2, kq_count(i + 1, q // 2, q % 2))
                    if with_p and (u, step) in LO_AT:
                        kind, k0, k1 = LO_AT[u, step]
                        split_lo(uses[kind], GAIN[kind[-1]], k0, k1)
                        if kind == "nextV":
                            low_k(i + 1)
                    if not with_p and (u, step) == (UNITS - 1, "T1"):
                        split_lo(uses["lastO"])

            pair(0, att_uses(0), with_w=False)
            with dve.Fori(1, PAIRS - 2, 2) as i:
                for d in range(2):
                    pair(i + d, att_uses(i + d, i, d))
            pair(PAIRS - 1, att_uses(PAIRS - 1, None, 1), with_p=False)
            epilogue("attE", OUT_ATT,
                     [lambda: split_lo(pieces.use("ffn1A", 0), GAIN["ffn1"]), lambda: None])
            split_lo(pieces.use("ffn1A", 1), GAIN["ffn1"])
            ffn(1)
            epilogue("ffn1E", OUT_FFN[1] + 8 * (GROUPS - 1), [lambda: None, lambda: None])

            for b in range(QB):
                dve.wait_ge(rows_filled, b + 1)
                if b >= 4:
                    dve.wait_ge(rows_stored[b % 4], 16)
                dve.tensor_scalar(tmp[b % 4][:, 0:BANK], ps[tiles.use("final", b)[0]][:, 0:BANK],
                                  row_rstd[:, b:b + 1], None, ALU.mult).then_inc(rows_ready[0], 1)


_INS = ["x", "norm_mix", "norm_ffn", "w_ffn_in", "w_ffn_out", "w_rec_in", "conv_w", "conv_b", "w_lru_gates",
        "b_lru_gates", "lru_param", "w_rec_out", "norm_kv", "w_kvf", "b_forget", "w_q", "w_o", "norm_final"]


def kernel(**inputs):
    import numpy as np
    import concourse.bacc as bacc
    from concourse.bass_utils import run_bass_kernel_spmd

    nc = bacc.Bacc("TRN2", target_bir_lowering=False, num_devices=1)
    arrays, args = {}, []
    for name in _INS:
        a = np.ascontiguousarray(inputs[name])
        arrays[f"in_{name}"] = a
        args.append(nc.dram_tensor(f"in_{name}", a.shape, mybir.dt.from_np(a.dtype), kind="ExternalInput").ap())
    out = nc.dram_tensor("out", inputs["x"].shape, F32, kind="ExternalOutput").ap()
    hawk_fox_yoco(nc, *args, out)
    r = run_bass_kernel_spmd(nc, [arrays], core_ids=[0])
    return r.results[0]["out"]
```
